# Optimizing a Trainium2 kernel written in Bass

```python
import math
import jax
import jax.numpy as jnp
from jax import lax
import numpy as np
import jax, jax.numpy as jnp

D_MODEL = 1024
BATCH = 1
SEQ = 256
DEPTH = 1

D_MIX = D_MODEL
HEAD_DIM = 64
D_ATTN = D_MIX // 2
D_CONV = D_MIX - D_ATTN
N_HEADS = D_ATTN // HEAD_DIM
N_KV = 2
HPG = N_HEADS // N_KV
KV_DIM = N_KV * HEAD_DIM
N_MIX_GROUPS = D_MIX // HEAD_DIM
CONV_WIDTH = 3
CMP_LEN = 32
CMP_STRIDE = 16
CMP_HIDDEN = 256
SLC_LEN = 64
N_SELECT = 16
WINDOW = 512
Q_BLOCK = 128
N_BUCKETS = 32
MAX_DISTANCE = 128
N_GROUPS = 8
EXPERTS_PER_GROUP = 8
N_EXPERTS = N_GROUPS * EXPERTS_PER_GROUP
TOP_K = 2
D_EXPERT = D_MODEL // 2
MOE_BLOCK = 128
FORCED_SCORE = 1e4
EPS = 1e-6
N_IN = D_ATTN + 6 * KV_DIM + 3 * N_HEADS + 3 * D_CONV


def rms_norm(x, w):
    xf = x.astype(jnp.float32)
    y = xf * lax.rsqrt(jnp.mean(xf * xf, axis=-1, keepdims=True) + EPS)
    return (y * w.astype(jnp.float32)).astype(x.dtype)

def t5_bucket(dist):
    n = jnp.maximum(dist, 0)
    max_exact = N_BUCKETS // 2
    nf = jnp.maximum(n, 1).astype(jnp.float32)
    large = max_exact + (jnp.log(nf / max_exact) / math.log(MAX_DISTANCE / max_exact)
                         * (N_BUCKETS - max_exact)).astype(jnp.int32)
    large = jnp.minimum(large, N_BUCKETS - 1)
    return jnp.where(n < max_exact, n, large)

def masked_softmax(logits, mask):
    lf = jnp.where(mask, logits.astype(jnp.float32), -jnp.inf)
    m = jnp.max(lf, axis=-1, keepdims=True)
    m = jnp.where(jnp.isfinite(m), m, 0.0)
    e = jnp.where(mask, jnp.exp(lf - m), 0.0)
    return e / jnp.maximum(jnp.sum(e, axis=-1, keepdims=True), 1e-30)

def compress(kv, pos_emb, w1, w2):
    b, s, g, dh = kv.shape
    nc = (s - CMP_LEN) // CMP_STRIDE + 1
    idx = jnp.arange(nc)[:, None] * CMP_STRIDE + jnp.arange(CMP_LEN)[None, :]
    blocks = kv[:, idx] + pos_emb[None, None, :, None, :]
    blocks = jnp.moveaxis(blocks, 3, 2).reshape(b, nc, g, CMP_LEN * dh)
    return jax.nn.silu(blocks @ w1) @ w2

def nsa_attention(q, gates, k_cmp, v_cmp, k_slc, v_slc, k_win, v_win, rel_bias):
    b, s = q.shape[0], q.shape[1]
    nc = k_cmp.shape[1]
    ns = s // SLC_LEN
    n_sel = min(N_SELECT, ns)
    nqb = s // Q_BLOCK
    scale = HEAD_DIM ** -0.5
    bias_gh = rel_bias.T.reshape(N_KV, HPG, N_BUCKETS)

    c_start = jnp.arange(nc) * CMP_STRIDE
    c_end = c_start + CMP_LEN - 1
    s_start = jnp.arange(ns) * SLC_LEN
    overlap = ((c_start[:, None] <= s_start[None, :] + SLC_LEN - 1)
               & (c_end[:, None] >= s_start[None, :])).astype(jnp.float32)

    ks_blocks = k_slc.reshape(b, ns, SLC_LEN, N_KV, HEAD_DIM).transpose(0, 3, 1, 2, 4)
    vs_blocks = v_slc.reshape(b, ns, SLC_LEN, N_KV, HEAD_DIM).transpose(0, 3, 1, 2, 4)
    pad = ((0, 0), (WINDOW, 0), (0, 0), (0, 0))
    kw_pad = jnp.pad(k_win, pad)
    vw_pad = jnp.pad(v_win, pad)

    q_all = q.reshape(b, nqb, Q_BLOCK, N_KV, HPG, HEAD_DIM).swapaxes(0, 1)
    g_all = gates.reshape(b, nqb, Q_BLOCK, N_KV, HPG, 3).swapaxes(0, 1)
    b_ix = jnp.arange(b)[:, None, None, None]
    g_ix = jnp.arange(N_KV)[None, :, None, None]
    g_ix5 = jnp.arange(N_KV)[None, :, None, None, None]
    h_ix5 = jnp.arange(HPG)[None, None, :, None, None]
    blk = jnp.arange(ns)

    def block_fn(args):
        j, qb, gb = args
        s0 = j * Q_BLOCK
        pos = s0 + jnp.arange(Q_BLOCK)

        dist_c = pos[:, None] - c_end[None, :]
        lc = jnp.einsum('bqghd,bngd->bghqn', qb, k_cmp) * scale + bias_gh[:, :, t5_bucket(dist_c)]
        p_cmp = masked_softmax(lc, dist_c >= 0)
        o_cmp = jnp.einsum('bghqn,bngd->bqghd', p_cmp.astype(v_cmp.dtype), v_cmp)

        imp = jnp.einsum('bghqn,ns->bgqs', p_cmp, overlap)
        cur = pos // SLC_LEN
        valid = blk[None, :] <= cur[:, None]
        forced = (blk[None, :] == 0) | (blk[None, :] == cur[:, None]) | (blk[None, :] == cur[:, None] - 1)
        score = jnp.where(forced, FORCED_SCORE, jnp.where(valid, imp, -1.0))
        top_val, top_idx = lax.top_k(score, n_sel)
        sel_ok = top_val >= 0.0
        ks = ks_blocks[b_ix, g_ix, top_idx].reshape(b, N_KV, Q_BLOCK, n_sel * SLC_LEN, HEAD_DIM)
        vs = vs_blocks[b_ix, g_ix, top_idx].reshape(b, N_KV, Q_BLOCK, n_sel * SLC_LEN, HEAD_DIM)
        kpos = (top_idx[..., None] * SLC_LEN + jnp.arange(SLC_LEN)).reshape(b, N_KV, Q_BLOCK, -1)
        dist_s = pos[None, None, :, None] - kpos
        mask_s = jnp.repeat(sel_ok, SLC_LEN, axis=-1) & (dist_s >= 0)
        ls = (jnp.einsum('bqghd,bgqkd->bghqk', qb, ks) * scale
              + bias_gh[g_ix5, h_ix5, t5_bucket(dist_s)[:, :, None]])
        p_s = masked_softmax(ls, mask_s[:, :, None])
        o_slc = jnp.einsum('bghqk,bgqkd->bqghd', p_s.astype(vs.dtype), vs)

        kw = lax.dynamic_slice_in_dim(kw_pad, s0, WINDOW + Q_BLOCK, axis=1)
        vw = lax.dynamic_slice_in_dim(vw_pad, s0, WINDOW + Q_BLOCK, axis=1)
        kpos_w = s0 - WINDOW + jnp.arange(WINDOW + Q_BLOCK)
        dist_w = pos[:, None] - kpos_w[None, :]
        mask_w = (dist_w >= 0) & (dist_w < WINDOW) & (kpos_w[None, :] >= 0)
        lw = jnp.einsum('bqghd,bkgd->bghqk', qb, kw) * scale + bias_gh[:, :, t5_bucket(dist_w)]
        p_w = masked_softmax(lw, mask_w)
        o_win = jnp.einsum('bghqk,bkgd->bqghd', p_w.astype(vw.dtype), vw)

        out = gb[..., 0:1] * o_cmp + gb[..., 1:2] * o_slc + gb[..., 2:3] * o_win
        return out.reshape(b, Q_BLOCK, D_ATTN)

    outs = lax.map(block_fn, (jnp.arange(nqb), q_all, g_all))
    return outs.swapaxes(0, 1).reshape(b, s, D_ATTN)

def short_conv(u, w):
    return lax.conv_general_dilated(u, w[:, None, :], window_strides=(1,),
                                    padding=[(CONV_WIDTH - 1, 0)],
                                    dimension_numbers=('NWC', 'WIO', 'NWC'),
                                    feature_group_count=u.shape[-1])

def hier_moe(h, w_group, b_group, w_expert, b_expert, w1, w3, w2):
    b, s, d = h.shape
    t = b * s
    xt = h.reshape(t, d)
    g_prob = jax.nn.softmax((xt @ w_group + b_group).astype(jnp.float32), axis=-1)
    g_top_p, g_top = lax.top_k(g_prob, 1)
    e_logits = (xt @ w_expert + b_expert).astype(jnp.float32).reshape(t, N_GROUPS, EXPERTS_PER_GROUP)
    e_in = jnp.take_along_axis(e_logits, g_top[:, :, None], axis=1)[:, 0]
    e_top_p, e_top = lax.top_k(jax.nn.softmax(e_in, axis=-1), TOP_K)
    e_top_p = e_top_p / jnp.sum(e_top_p, axis=-1, keepdims=True)
    weights = (g_top_p * e_top_p).reshape(-1)
    expert_ids = (g_top * EXPERTS_PER_GROUP + e_top).reshape(-1)
    token_ids = jnp.repeat(jnp.arange(t), TOP_K)

    a = t * TOP_K
    order = jnp.argsort(expert_ids)
    e_sorted = expert_ids[order]
    tok_sorted = token_ids[order]
    w_sorted = weights[order]
    counts = jax.ops.segment_sum(jnp.ones((a,), jnp.int32), expert_ids, num_segments=N_EXPERTS)
    padded = (counts + MOE_BLOCK - 1) // MOE_BLOCK * MOE_BLOCK
    start = jnp.cumsum(counts) - counts
    pad_end = jnp.cumsum(padded)
    pad_start = pad_end - padded
    dest = pad_start[e_sorted] + (jnp.arange(a) - start[e_sorted])
    n_blocks = (a + N_EXPERTS * (MOE_BLOCK - 1)) // MOE_BLOCK + 1
    rows = n_blocks * MOE_BLOCK
    x_disp = jnp.zeros((rows, d), xt.dtype).at[dest].set(xt[tok_sorted])
    blk_expert = jnp.minimum(jnp.searchsorted(pad_end, jnp.arange(n_blocks) * MOE_BLOCK, side='right'),
                             N_EXPERTS - 1)

    def expert_block(args):
        xb, e = args
        return (jax.nn.silu(xb @ w1[e]) * (xb @ w3[e])) @ w2[e]

    y_disp = lax.map(expert_block, (x_disp.reshape(n_blocks, MOE_BLOCK, d), blk_expert)).reshape(rows, d)
    y = jax.ops.segment_sum(y_disp[dest] * w_sorted[:, None].astype(y_disp.dtype), tok_sorted,
                            num_segments=t)
    return y.reshape(b, s, d)

def first_inputs(seed: int = 0) -> dict:
    key = jax.random.key(seed)
    ks = jax.random.split(key, 26)
    f32 = jnp.float32

    def nrm(k, shape, scale):
        return jax.random.normal(k, shape, f32) * scale

    def gain(k, shape):
        return 1.0 + 0.02 * jax.random.normal(k, shape, f32)

    L = DEPTH
    return {
        'x': nrm(ks[0], (BATCH, SEQ, D_MODEL), 1.0),
        'c': nrm(ks[1], (BATCH, D_MODEL), 1.0),
        'w_ada': nrm(ks[2], (L, D_MODEL, 6 * D_MODEL), 0.5 * D_MODEL ** -0.5),
        'b_ada': nrm(ks[3], (L, 6 * D_MODEL), 0.01),
        'norm1_w': gain(ks[4], (L, D_MODEL)),
        'w_in': nrm(ks[5], (L, D_MODEL, N_IN), D_MODEL ** -0.5),
        'q_norm_w': gain(ks[6], (L, HEAD_DIM)),
        'k_norm_w': gain(ks[7], (L, 3, HEAD_DIM)),
        'cmp_pos_k': nrm(ks[8], (L, CMP_LEN, HEAD_DIM), 0.1),
        'cmp_pos_v': nrm(ks[9], (L, CMP_LEN, HEAD_DIM), 0.1),
        'cmp_k_w1': nrm(ks[10], (L, CMP_LEN * HEAD_DIM, CMP_HIDDEN), (CMP_LEN * HEAD_DIM) ** -0.5),
        'cmp_k_w2': nrm(ks[11], (L, CMP_HIDDEN, HEAD_DIM), CMP_HIDDEN ** -0.5),
        'cmp_v_w1': nrm(ks[12], (L, CMP_LEN * HEAD_DIM, CMP_HIDDEN), (CMP_LEN * HEAD_DIM) ** -0.5),
        'cmp_v_w2': nrm(ks[13], (L, CMP_HIDDEN, HEAD_DIM), CMP_HIDDEN ** -0.5),
        'conv_w': nrm(ks[14], (L, CONV_WIDTH, D_CONV), CONV_WIDTH ** -0.5),
        'out_norm_w': gain(ks[15], (L, D_MIX)),
        'w_out': nrm(ks[16], (L, D_MIX, D_MODEL), D_MIX ** -0.5),
        'rel_bias': nrm(ks[17], (N_BUCKETS, N_HEADS), 0.5),
        'norm2_w': gain(ks[18], (L, D_MODEL)),
        'w_group': nrm(ks[19], (L, D_MODEL, N_GROUPS), D_MODEL ** -0.5),
        'b_group': nrm(ks[20], (L, N_GROUPS), 0.01),
        'w_expert': nrm(ks[21], (L, D_MODEL, N_EXPERTS), D_MODEL ** -0.5),
        'b_expert': nrm(ks[22], (L, N_EXPERTS), 0.01),
        'w1': nrm(ks[23], (L, N_EXPERTS, D_MODEL, D_EXPERT), D_MODEL ** -0.5),
        'w3': nrm(ks[24], (L, N_EXPERTS, D_MODEL, D_EXPERT), D_MODEL ** -0.5),
        'w2': nrm(ks[25], (L, N_EXPERTS, D_EXPERT, D_MODEL), D_EXPERT ** -0.5),
    }

def first_block(x, c, w_ada, b_ada, norm1_w, w_in, q_norm_w, k_norm_w, cmp_pos_k, cmp_pos_v,
              cmp_k_w1, cmp_k_w2, cmp_v_w1, cmp_v_w2, conv_w, out_norm_w, w_out, rel_bias,
              norm2_w, w_group, b_group, w_expert, b_expert, w1, w3, w2):
    b, s, _ = x.shape
    cond = jax.nn.silu(c)
    splits = [D_ATTN, D_ATTN + 6 * KV_DIM, D_ATTN + 6 * KV_DIM + 3 * N_HEADS,
              D_ATTN + 6 * KV_DIM + 3 * N_HEADS + D_CONV,
              D_ATTN + 6 * KV_DIM + 3 * N_HEADS + 2 * D_CONV]
    for l in range(DEPTH):
        mod = cond @ w_ada[l] + b_ada[l]
        sh1, sc1, g1, sh2, sc2, g2 = jnp.split(mod[:, None, :], 6, axis=-1)

        h = rms_norm(x, norm1_w[l]) * (1 + sc1) + sh1
        proj = h @ w_in[l]
        q, kvs, gate_logits, b_gate, c_gate, u = jnp.split(proj, splits, axis=-1)
        q = rms_norm(q.reshape(b, s, N_HEADS, HEAD_DIM), q_norm_w[l])
        kv = kvs.reshape(b, s, 6, N_KV, HEAD_DIM)
        k_c = rms_norm(compress(kv[:, :, 0], cmp_pos_k[l], cmp_k_w1[l], cmp_k_w2[l]), k_norm_w[l, 0])
        v_c = compress(kv[:, :, 1], cmp_pos_v[l], cmp_v_w1[l], cmp_v_w2[l])
        k_s = rms_norm(kv[:, :, 2], k_norm_w[l, 1])
        k_w = rms_norm(kv[:, :, 4], k_norm_w[l, 2])
        gates = jax.nn.sigmoid(gate_logits.reshape(b, s, N_HEADS, 3))
        o_attn = nsa_attention(q, gates, k_c, v_c, k_s, kv[:, :, 3], k_w, kv[:, :, 5], rel_bias)
        y_conv = b_gate * short_conv(c_gate * u, conv_w[l])
        mix = jnp.concatenate([o_attn, y_conv], axis=-1).reshape(b, s, N_MIX_GROUPS, HEAD_DIM)
        mix = rms_norm(mix, out_norm_w[l].reshape(N_MIX_GROUPS, HEAD_DIM)).reshape(b, s, D_MIX)
        x = x + g1 * (mix @ w_out[l])

        h2 = rms_norm(x, norm2_w[l]) * (1 + sc2) + sh2
        x = x + g2 * hier_moe(h2, w_group[l], b_group[l], w_expert[l], b_expert[l], w1[l], w3[l], w2[l])
    return x


DEPTH_2 = 2

GRID_W = 64
CTX_LEN = 256

FOURIER_HEADS = 4
FOURIER_HEAD_DIM = D_MODEL // 8
FOURIER_WIDTH = FOURIER_HEADS * FOURIER_HEAD_DIM
N_Q_HEADS = (D_MODEL // 2) // HEAD_DIM
N_KV_HEADS = 2
GQA_GROUP = N_Q_HEADS // N_KV_HEADS
ATTN_WIDTH = N_Q_HEADS * HEAD_DIM
KV_WIDTH = N_KV_HEADS * HEAD_DIM
Q_END = FOURIER_WIDTH + ATTN_WIDTH
IN_WIDTH = Q_END + 2 * KV_WIDTH
MIX_WIDTH = FOURIER_WIDTH + ATTN_WIDTH
WINDOW_2 = 128
BLOCK = 128
ROPE_THETA = 10000.0
POOL_WINDOWS = (2, 4, 8, 16)
POOL_GROUP = D_MODEL // len(POOL_WINDOWS)
FFN_HIDDEN = ((-(-8 * D_MODEL // 3)) + 255) // 256 * 256
N_EVEN = (DEPTH_2 + 1) // 2
N_ODD = DEPTH_2 // 2


def rms_norm_2(x, g):
    xf = x.astype(jnp.float32)
    y = xf * lax.rsqrt(jnp.mean(xf * xf, axis=-1, keepdims=True) + EPS)
    return (y * g.astype(jnp.float32)).astype(x.dtype)

def ada_mod(cond, w, b):
    m = jax.nn.silu(cond) @ w + b
    return jnp.split(m[..., None, :], 6, axis=-1)

def modulate(h, shift, scale):
    return h * (1 + scale) + shift

def axial_rope_tables(n_tokens):
    rows = n_tokens // GRID_W
    row = jnp.repeat(jnp.arange(rows, dtype=jnp.float32), GRID_W)
    col = jnp.tile(jnp.arange(GRID_W, dtype=jnp.float32), rows)
    n_freq = HEAD_DIM // 4
    inv = ROPE_THETA ** (-jnp.arange(n_freq, dtype=jnp.float32) / n_freq)
    ang = jnp.concatenate([row[:, None] * inv[None], col[:, None] * inv[None]], axis=-1)
    return jnp.cos(ang), jnp.sin(ang)

def apply_rope(x, cos, sin):
    xf = x.astype(jnp.float32).reshape(*x.shape[:-1], HEAD_DIM // 2, 2)
    x1, x2 = xf[..., 0], xf[..., 1]
    c, s = cos[:, None, :], sin[:, None, :]
    out = jnp.stack([x1 * c - x2 * s, x1 * s + x2 * c], axis=-1).reshape(x.shape)
    return out.astype(x.dtype)

def fourier_mix(u):
    B, N, _ = u.shape
    uh = u.astype(jnp.float32).reshape(B, N, FOURIER_HEADS, FOURIER_HEAD_DIM)
    y = jnp.fft.fftn(uh, axes=(1, 3), norm='ortho').real
    return y.reshape(B, N, FOURIER_WIDTH).astype(u.dtype)

def sink_logits(sink, lead_shape):
    s = sink.astype(jnp.float32).reshape(1, N_KV_HEADS, GQA_GROUP, 1, 1)
    return jnp.broadcast_to(s, lead_shape + (1,))

def window_attention(q, k, v, k_ctx, v_ctx, sink):
    B, S = q.shape[:2]
    L = k_ctx.shape[1]
    nb = S // BLOCK
    scale = HEAD_DIM ** -0.5
    pad = ((0, 0), (BLOCK, BLOCK), (0, 0), (0, 0))
    kp, vp = jnp.pad(k, pad), jnp.pad(v, pad)
    qb = q.reshape(B, nb, BLOCK, N_KV_HEADS, GQA_GROUP, HEAD_DIM).transpose(1, 0, 2, 3, 4, 5)

    def one_block(args):
        i, q_i = args
        start = i * BLOCK
        k_i = lax.dynamic_slice_in_dim(kp, start, 3 * BLOCK, axis=1)
        v_i = lax.dynamic_slice_in_dim(vp, start, 3 * BLOCK, axis=1)
        qpos = start + jnp.arange(BLOCK)
        kpos = start - BLOCK + jnp.arange(3 * BLOCK)
        valid = (jnp.abs(kpos[None, :] - qpos[:, None]) <= WINDOW_2) & (kpos[None, :] >= 0) & (kpos[None, :] < S)
        s_win = jnp.einsum('bqkgd,bjkd->bkgqj', q_i, k_i).astype(jnp.float32) * scale
        s_win = jnp.where(valid[None, None, None], s_win, -jnp.inf)
        s_ctx = jnp.einsum('bqkgd,bckd->bkgqc', q_i, k_ctx).astype(jnp.float32) * scale
        logits = jnp.concatenate([s_win, s_ctx, sink_logits(sink, s_win.shape[:-1])], axis=-1)
        p = jax.nn.softmax(logits, axis=-1)
        p_win = p[..., :3 * BLOCK].astype(v.dtype)
        p_ctx = p[..., 3 * BLOCK:3 * BLOCK + L].astype(v.dtype)
        return (jnp.einsum('bkgqj,bjkd->bqkgd', p_win, v_i)
                + jnp.einsum('bkgqc,bckd->bqkgd', p_ctx, v_ctx))

    o = lax.map(one_block, (jnp.arange(nb), qb))
    return o.transpose(1, 0, 2, 3, 4, 5).reshape(B, S, ATTN_WIDTH)

def context_attention(q_c, k_c, v_c, sink):
    B, L = q_c.shape[:2]
    qg = q_c.reshape(B, L, N_KV_HEADS, GQA_GROUP, HEAD_DIM)
    s = jnp.einsum('bqkgd,bckd->bkgqc', qg, k_c).astype(jnp.float32) * HEAD_DIM ** -0.5
    p = jax.nn.softmax(jnp.concatenate([s, sink_logits(sink, s.shape[:-1])], axis=-1), axis=-1)
    p = p[..., :L].astype(v_c.dtype)
    return jnp.einsum('bkgqc,bckd->bqkgd', p, v_c).reshape(B, L, ATTN_WIDTH)

def even_mixer(xn, xcn, w_in, w_out, sink, cos, sin, with_ctx_out):
    B, S, _ = xn.shape
    L = xcn.shape[1]
    proj = xn @ w_in
    f_in = proj[..., :FOURIER_WIDTH]
    q = proj[..., FOURIER_WIDTH:Q_END].reshape(B, S, N_Q_HEADS, HEAD_DIM)
    k = proj[..., Q_END:Q_END + KV_WIDTH].reshape(B, S, N_KV_HEADS, HEAD_DIM)
    v = proj[..., Q_END + KV_WIDTH:].reshape(B, S, N_KV_HEADS, HEAD_DIM)
    q = apply_rope(q, cos, sin)
    k = apply_rope(k, cos, sin)
    kv_c = xcn @ w_in[:, Q_END:]
    k_c = kv_c[..., :KV_WIDTH].reshape(B, L, N_KV_HEADS, HEAD_DIM)
    v_c = kv_c[..., KV_WIDTH:].reshape(B, L, N_KV_HEADS, HEAD_DIM)
    attn = window_attention(q, k, v, k_c, v_c, sink)
    y = jnp.concatenate([fourier_mix(f_in), attn], axis=-1) @ w_out
    if not with_ctx_out:
        return y, None
    fq_c = xcn @ w_in[:, :Q_END]
    f_c = fq_c[..., :FOURIER_WIDTH]
    q_c = fq_c[..., FOURIER_WIDTH:].reshape(B, L, N_Q_HEADS, HEAD_DIM)
    attn_c = context_attention(q_c, k_c, v_c, sink)
    y_c = jnp.concatenate([fourier_mix(f_c), attn_c], axis=-1) @ w_out
    return y, y_c

def pool_mix(h, w_pool, scale):
    B, N, _ = h.shape
    hf = h.astype(jnp.float32)
    csum = jnp.pad(jnp.cumsum(hf, axis=1), ((0, 0), (1, 0), (0, 0)))
    t = np.arange(N)
    outs = []
    for g, w in enumerate(POOL_WINDOWS):
        lo = np.clip(t - w // 2, 0, N)
        hi = np.clip(t + w // 2, 0, N)
        sl = slice(g * POOL_GROUP, (g + 1) * POOL_GROUP)
        cg = csum[..., sl]
        count = jnp.asarray(hi - lo, dtype=jnp.float32)[None, :, None]
        outs.append((cg[:, hi] - cg[:, lo]) / count - hf[..., sl])
    y = jnp.stack(outs, axis=2).astype(h.dtype)
    y = jnp.einsum('bngc,gcd->bngd', y, w_pool).reshape(B, N, D_MODEL)
    return y * scale

def swiglu(h, w1, w3, w2):
    return (jax.nn.silu(h @ w1) * (h @ w3)) @ w2

def second_inputs(seed: int = 0) -> dict:
    key = jax.random.key(seed)
    ks = jax.random.split(key, 18)
    f32 = jnp.float32

    def nrm(k, shape, s=1.0):
        return s * jax.random.normal(k, shape, f32)

    return {
        'x': nrm(ks[0], (BATCH, SEQ, D_MODEL)),
        'c': nrm(ks[1], (BATCH, D_MODEL)),
        'ctx': nrm(ks[2], (BATCH, CTX_LEN, D_MODEL)),
        'c_ctx': nrm(ks[3], (D_MODEL,)),
        'ada_w': nrm(ks[4], (DEPTH_2, D_MODEL, 6 * D_MODEL), 0.5 * D_MODEL ** -0.5),
        'ada_b': nrm(ks[5], (DEPTH_2, 6 * D_MODEL), 0.02),
        'norm_mix_g': 1.0 + nrm(ks[6], (DEPTH_2, D_MODEL), 0.05),
        'norm_ffn_g': 1.0 + nrm(ks[7], (DEPTH_2, D_MODEL), 0.05),
        'mix_in_w': nrm(ks[8], (N_EVEN, D_MODEL, IN_WIDTH), D_MODEL ** -0.5),
        'mix_out_w': nrm(ks[9], (N_EVEN, MIX_WIDTH, D_MODEL), MIX_WIDTH ** -0.5),
        'attn_sink': nrm(ks[10], (N_EVEN, N_Q_HEADS), 0.5),
        'pool_w': nrm(ks[11], (N_ODD, len(POOL_WINDOWS), POOL_GROUP, POOL_GROUP), POOL_GROUP ** -0.5),
        'pool_scale': 1.0 + nrm(ks[12], (N_ODD, D_MODEL), 0.1),
        'ffn_w1': nrm(ks[13], (DEPTH_2, D_MODEL, FFN_HIDDEN), D_MODEL ** -0.5),
        'ffn_w3': nrm(ks[14], (DEPTH_2, D_MODEL, FFN_HIDDEN), D_MODEL ** -0.5),
        'ffn_w2': nrm(ks[15], (DEPTH_2, FFN_HIDDEN, D_MODEL), FFN_HIDDEN ** -0.5),
        'final_g': 1.0 + nrm(ks[16], (D_MODEL,), 0.05),
    }

def second_block(x, c, ctx, c_ctx, ada_w, ada_b, norm_mix_g, norm_ffn_g, mix_in_w, mix_out_w,
              attn_sink, pool_w, pool_scale, ffn_w1, ffn_w3, ffn_w2, final_g):
    n_tokens = x.shape[1]
    cos, sin = axial_rope_tables(n_tokens)
    last_ctx_reader = max(range(0, DEPTH_2, 2))
    h, hc = x, ctx
    for layer in range(DEPTH_2):
        sh1, sc1, g1, sh2, sc2, g2 = ada_mod(c, ada_w[layer], ada_b[layer])
        update_ctx = layer < last_ctx_reader
        need_ctx_in = update_ctx or (layer % 2 == 0 and layer <= last_ctx_reader)
        if need_ctx_in:
            csh1, csc1, cg1, csh2, csc2, cg2 = ada_mod(c_ctx, ada_w[layer], ada_b[layer])
            xcn = modulate(rms_norm_2(hc, norm_mix_g[layer]), csh1, csc1)
        xn = modulate(rms_norm_2(h, norm_mix_g[layer]), sh1, sc1)
        j = layer // 2
        if layer % 2 == 0:
            y, y_c = even_mixer(xn, xcn, mix_in_w[j], mix_out_w[j], attn_sink[j], cos, sin, update_ctx)
        else:
            y = pool_mix(xn, pool_w[j], pool_scale[j])
            y_c = pool_mix(xcn, pool_w[j], pool_scale[j]) if update_ctx else None
        h = h + g1 * y
        hn = modulate(rms_norm_2(h, norm_ffn_g[layer]), sh2, sc2)
        h = h + g2 * swiglu(hn, ffn_w1[layer], ffn_w3[layer], ffn_w2[layer])
        if update_ctx:
            hc = hc + cg1 * y_c
            hcn = modulate(rms_norm_2(hc, norm_ffn_g[layer]), csh2, csc2)
            hc = hc + cg2 * swiglu(hcn, ffn_w1[layer], ffn_w3[layer], ffn_w2[layer])
    return rms_norm_2(h, final_g)


def setup_inputs(seed=0):
    out = dict(first_inputs(seed))
    for name, value in second_inputs(seed + 1).items():
        if name != "x":
            out[name + "_2"] = value
    return out


def reference(
    x, c, w_ada, b_ada, norm1_w, w_in, q_norm_w, k_norm_w, cmp_pos_k, cmp_pos_v, cmp_k_w1,
    cmp_k_w2, cmp_v_w1, cmp_v_w2, conv_w, out_norm_w, w_out, rel_bias, norm2_w, w_group,
    b_group, w_expert, b_expert, w1, w3, w2, c_2, ctx_2, c_ctx_2, ada_w_2, ada_b_2,
    norm_mix_g_2, norm_ffn_g_2, mix_in_w_2, mix_out_w_2, attn_sink_2, pool_w_2, pool_scale_2,
    ffn_w1_2, ffn_w3_2, ffn_w2_2, final_g_2,
):
    x = first_block(
        x, c, w_ada, b_ada, norm1_w, w_in, q_norm_w, k_norm_w, cmp_pos_k, cmp_pos_v, cmp_k_w1,
        cmp_k_w2, cmp_v_w1, cmp_v_w2, conv_w, out_norm_w, w_out, rel_bias, norm2_w, w_group,
        b_group, w_expert, b_expert, w1, w3, w2,
    )
    return second_block(
        x, c_2, ctx_2, c_ctx_2, ada_w_2, ada_b_2, norm_mix_g_2, norm_ffn_g_2, mix_in_w_2,
        mix_out_w_2, attn_sink_2, pool_w_2, pool_scale_2, ffn_w1_2, ffn_w3_2, ffn_w2_2,
        final_g_2,
    )


_drawn_inputs = setup_inputs


def setup_inputs(seed=0):
    import zlib

    import numpy as np

    out = dict(_drawn_inputs(seed))
    spreads = {}
    factors = {'b_ada': 3.81,
     'norm1_w': 5.698,
     'q_norm_w': 8.0,
     'k_norm_w': 8.0,
     'cmp_pos_k': 8.0,
     'cmp_pos_v': 3.447,
     'out_norm_w': 7.807,
     'norm2_w': 8.0,
     'b_group': 8.0,
     'b_expert': 8.0,
     'ctx_2': 3.863,
     'norm_mix_g_2': 10.471,
     'norm_ffn_g_2': 9.528,
     'attn_sink_2': 8.0,
     'ada_b_2': 2.675,
     'pool_scale_2': 5.573}
    for name, (base, spread) in spreads.items():
        noise = np.random.default_rng([zlib.crc32(name.encode()), seed]).standard_normal(out[name].shape)
        drawn = base * np.exp(spread * noise) if base else spread * noise
        out[name] = jnp.asarray(drawn.astype(out[name].dtype))
    for name, factor in factors.items():
        out[name] = (out[name] * factor).astype(out[name].dtype)
    return out
```

```python
import math
from contextlib import ExitStack

import numpy as np
import concourse.bass as bass
from concourse import mybir

F32 = mybir.dt.float32
I32 = mybir.dt.int32
ACT = mybir.ActivationFunctionType
ALU = mybir.AluOpType
AX = mybir.AxisListType

P = 128
T = 256
NT = T // P
D = 1024
KD = D // P
HD = 64
NH = 8
NKV = 2
PAIRS = NH // NKV
EPS = 1e-6
NEG = -1.0e30
SCALE = HD ** -0.5
CMP_STRIDE, CMP_LEN = 16, 32
NC = (T - CMP_LEN) // CMP_STRIDE + 1
LPAIRS = CMP_LEN // 2
CMP_HID = 256
NB = 32
TABW = 448
C1, C0 = 384, 416
E = 64
FE = 512
SLOTS = 64
NOV = 7
OVR = NOV + 1
ECOL = E + OVR + 2
FFN = 2816
FCH = 256
NS = 6
CHUNK = 4096

VEC = {}
_at = 0
for _n, _w in [("norm1", 8), ("norm2", 8), ("outn", 8), ("nmix0", 8), ("nmix1", 8), ("nffn0", 8), ("nffn1", 8),
               ("pscale", 8), ("c", 8), ("c2", 8), ("cctx", 8), ("qn", 1), ("kn", 3), ("posk", 16), ("posv", 16),
               ("conv", 12)]:
    VEC[_n] = (_at, _at + _w)
    _at += _w
NVEC = _at

CON, CONB = {}, {}
_at = 0
for _n, _w in [("ident", 128), ("tri", 128), ("ones", 128), ("bd", 128), ("sel", 512), ("iota", 64), ("rev", 8),
               ("eidx", 64), ("cmask", 256)]:
    CON[_n] = (_at, _at + _w)
    _at += _w
NCON = _at
_at = 0
for _n, _w in [("cosn", 512), ("sinn", 512), ("cosd", 128), ("nsind", 128), ("pool", 2048), ("rcos", 64),
               ("rsin", 64), ("wmask", 512)]:
    CONB[_n] = (_at, _at + _w)
    _at += _w
NCONB = _at

RA, RW, RC, RL, RO = 0, 12, 18, 20, 44
RE = 46
RM = RE + 3 * E
RF0 = RM + 5
NF = FFN // FCH
RP = RF0 + 2 * NF
RF1 = RP + 1
PEEL = 2


class Chain:

    def __init__(self, eng, sem):
        self.eng, self.sem, self.n, self.i = eng, sem, 0, None

    def __call__(self, ins):
        ins.then_inc(self.sem, 1)
        self.n += 1
        at = self.n if self.i is None else self.i * self.per + (self.before + self.n)
        self.eng.wait_ge(self.sem, at)

    def enter(self, i, per):
        self.before, self.n, self.i, self.per = self.n, 0, i, per

    def leave(self, times):
        assert self.n == self.per, (self.n, self.per)
        self.n, self.i = self.before + times * self.per, None


def build(nc, A, out):
    with ExitStack() as ctx:
        sb = lambda n, s, d=F32: ctx.enter_context(nc.sbuf_tensor(n, s, d))
        sem = lambda n: ctx.enter_context(nc.semaphore(n))

        ring = sb("ring", [P, NS, CHUNK])
        con = sb("con", [P, NCON])
        vec = sb("vec", [P, NVEC])
        x = sb("x", [P, NT, D])
        xn = sb("xn", [P, NT, D])
        hT = sb("hT", [P, KD, T])
        mixT = sb("mixT", [P, KD, T])
        modrow = sb("modrow", [P, 3 * 1536])
        modcol = sb("modcol", [P, 3, 32])
        ctxcol = sb("ctxcol", [P, 16])
        cond = sb("cond", [P, 2, KD, 32])
        gB = sb("gB", [P, D])
        small = sb("small", [P, 256])
        wr = sb("wr", [P, KD, 72])
        brB = sb("brB", [P, 72])
        oh, relb = gB[0:NB, 0:384], gB[0:NB, 384:384 + NH]
        cw2 = sb("cw2", [P, 2, 2, HD])
        arena = sb("arena", [P, 11400])
        ps = ctx.enter_context(nc.psum_tensor("ps", [P, 8, 512], F32))

        epsc = small[:, 0:1]
        ss = small[:, 2:4]
        rstd = small[:, 4:6]
        Acol = small[:, 8:16]
        Bcol = small[:, 16:24]
        SS = small[:, 24:48]
        RS = small[:, 48:72]
        nM = small[:, 72:84].rearrange("p (h b i) -> p h b i", h=2, b=3)
        SM = small[:, 84:96].rearrange("p (h b i) -> p h b i", h=2, b=3)
        CO = small[:, 96:108].rearrange("p (h b i) -> p h b i", h=2, b=3)
        sd24 = small[:, 112:136]
        G3 = small[:, 136:184].rearrange("p (h b i) -> p h b i", h=8, b=3)
        sd2 = small[:, 184:186]

        def C(n):
            return con[:, CON[n][0]:CON[n][1]]

        def V(n):
            return vec[:, VEC[n][0]:VEC[n][1]]

        ident, ones, tri = C("ident"), C("ones"), C("tri")
        sel = C("sel").rearrange("p (j m) -> p j m", j=4)

        at = [0]

        def take(n):
            at[0] += n
            assert at[0] <= 11400, at[0]
            return arena[:, at[0] - n:at[0]]

        q = take(1024).rearrange("p (t n) -> p t n", t=NT)
        ksv = take(512).rearrange("p (t n) -> p t n", t=NT)
        kwg = take(560).rearrange("p (t n) -> p t n", t=NT)
        kTs, kTw = take(256), take(256)
        zone = take(3104)
        bT = zone[:, 0:1024].rearrange("p (f t) -> p f t", f=4)
        cT = zone[:, 1024:2048].rearrange("p (f t) -> p f t", f=4)
        vT = zone[:, 2048:2048 + 4 * 258].rearrange("p (f t) -> p f t", f=4)
        L = zone[:, 0:4 * TABW].rearrange("p (a n) -> p a n", a=4)
        PTs = zone[:, 1792:2816].rearrange("p (h n) -> p h n", h=2)
        hTf = hT[:, :, :].rearrange("p k t -> p (k t)")
        PTw = hTf[:, 0:768].rearrange("p (h n) -> p h n", h=2)
        qT = hTf[:, 768:1024]
        qn = hTf[:, 1024:1280].rearrange("p (t h d) -> p t h d", t=2, h=2)
        xnf = xn[:, :, :].rearrange("p t d -> p (t d)")
        sq = xnf[:, 0:1024]
        attn = xnf[:, 0:1024].rearrange("p (i h d) -> p i h d", i=2, h=NH)
        Ot = xnf[:, 1024:1792].rearrange("p (h b i d) -> p h b i d", h=2, b=3, i=2)
        kvT2 = xnf[:, 1024:2048].rearrange("p (v g t) -> p v g t", v=2, g=2)
        blk = take(2 * LPAIRS * 2 * NC).rearrange("p (v m g n) -> p v m g n", v=2, m=LPAIRS, g=2)
        hidS = xnf[:, 1024:1536]
        hidT = xnf[:, 1536:1664].rearrange("p (v n) -> p v n", v=4)
        kcn = xnf[:, 1664:1792]
        vc = take(256).rearrange("p (i g d) -> p i g d", i=2, g=2)
        kcT = take(16)
        tab = take(NH * TABW).rearrange("p (h n) -> p h n", h=NH)
        tabrow = tab.rearrange("p h n -> p (h n)")[:, 0:NH * 384].rearrange("p (h n) -> p h n", h=NH)
        btab = nc.dram_tensor("btab", (NH, P * 384), F32, kind="Internal").ap()

        at[0] = 0
        gat = take(2 * ECOL).rearrange("p (t e) -> p t e", t=NT)
        rnk = take(2 * ECOL).rearrange("p (t e) -> p t e", t=NT)
        msk = take(2 * E).rearrange("p (t e) -> p t e", t=NT)
        lg = take(144).rearrange("p (t e) -> p t e", t=NT)
        prod = take(2 * NOV * E)
        selo = take(NOV * E).rearrange("p (b e) -> p b e", b=NOV)
        cnt, nx, ce, cex = take(E), take(E), take(E), take(E)
        r8 = [take(16).rearrange("p (t e) -> p t e", t=NT) for _ in range(8)]
        r1 = [take(2) for _ in range(8)]
        ovf = take(10)
        ovi = take(10).bitcast(I32)
        Ssel, SG = (take(NT * P).rearrange("p (t s) -> p t s", t=NT) for _ in range(2))
        XeT = mixT[:, :, 0:P]
        gsil = take(FE)
        hexp = gsil
        SGT = take(T)
        heT = take(FE).rearrange("p (f s) -> p f s", f=FE // P)
        Ye = take(D)
        at[0] = max(at[0], 5120)
        conb = take(NCONB)
        ctx_in = take(NT * D).rearrange("p (t d) -> p t d", t=NT)
        at[0] = 0
        u2 = take(1024).rearrange("p (t n) -> p t n", t=NT)
        attn2 = u2.rearrange("p t (h d) -> p t h d", d=HD)
        T1 = take(2048).rearrange("p (h c n) -> p h c n", h=4, c=2)
        q2 = take(1024).rearrange("p (t n) -> p t n", t=NT)
        kv2 = take(512).rearrange("p (t n) -> p t n", t=NT)
        kvc = take(512).rearrange("p (t n) -> p t n", t=NT)
        assert at[0] <= 5200
        f1f = T1.rearrange("p h c n -> p (h c n)")
        kT2, kcT2, qT2 = f1f[:, 0:256], f1f[:, 256:512], f1f[:, 512:768]
        qn2 = f1f[:, 768:1024].rearrange("p (t h d) -> p t h d", t=2, h=2)
        L2 = ctx_in.rearrange("p t d -> p (t d)").rearrange("p (a n) -> p a n", a=4)
        PT2 = xnf.rearrange("p (a n) -> p a n", a=4)
        ctxT = mixT
        sinkB = small[:, 186:194]
        nM2, mc2, s1, s2, se = (small[:, 196 + 4 * n:200 + 4 * n] for n in range(5))
        cexc, cssc = small[:, 216:218], small[:, 218:220]
        gs = arena[:, 0:768].rearrange("p (b n) -> p b n", b=3)
        gT = arena[:, 1024:1024 + 6 * 256].rearrange("p (b n) -> p b n", b=6)
        rowB = arena[:, 2560:2560 + D]

        def CB(n):
            return conb[:, CONB[n][0]:CONB[n][1]]

        loaded = [sem(f"ring_loaded{s}") for s in range(NS)]
        ring_used = sem("ring_used")
        con_in, x_in, bias_in, tab_in, misc_in, btab_out, out_done = map(
            sem, ["con_in", "x_in", "bias_in", "tab_in", "misc_in", "btab_out", "out_done"])
        zeroed, cond_ready = sem("zeroed"), sem("cond_ready")
        chainD, chainD2, chainA = sem("chain_dve"), sem("chain_dve2"), sem("chain_act")
        ada_ev, col_tr, col_ev = map(sem, ["ada_ev", "col_tr", "col_ev"])
        nrm_sq, nrm_rs, nrm_xn, nrm_tr, nrm_hT = map(sem, ["nrm_sq", "nrm_rs", "nrm_xn", "nrm_tr", "nrm_hT"])
        x_new = sem("x_new")
        win_act, win_dve = map(sem, ["win_act", "win_dve"])
        cv_sq, cv_sum, cv_sd, cv_y, cv_mix = map(sem, ["cv_sq", "cv_sum", "cv_sd", "cv_y", "cv_mix"])
        blk_ready, hid_act, hidT_tr, hidT_ev, kc_mm, kc_ss, kc_sd, kc_n, kc_tr, kc_ready = map(
            sem, ["blk_ready", "hid_act", "hidT_tr", "hidT_ev", "kc_mm", "kc_ss", "kc_sd", "kc_n", "kc_tr",
                  "kc_ready"])
        tabr_mm, tabr_ev, tab_ready = sem("tabr_mm"), sem("tabr_ev"), sem("tab_ready")
        qk_ss, qk_sd, k_n, k_tr, k_ready = map(sem, ["qk_ss", "qk_sd", "k_n", "k_tr", "k_ready"])
        gate_ready = sem("gate_ready")
        a_qn, a_qtr, a_qT, a_s, a_w, a_L, a_Lw, a_M, a_E, a_T, a_P, a_O, a_done = map(
            sem, ["a_qn", "a_qtr", "a_qT", "a_s", "a_w", "a_L", "a_Lw", "a_M", "a_E", "a_T", "a_P", "a_O", "a_done"])
        at_ss, at_sd, at_n, at_tr, at_mix = map(sem, ["at_ss", "at_sd", "at_n", "at_tr", "at_mix"])
        g_mm, g_ev = sem("g_mm"), sem("g_ev")

        lg_mm, lg_gx, lg_ex, lg_mask, lg_rank, h2_tr, h2_ev, ov_ready, acc_zero = map(
            sem, ["lg_mm", "lg_gx", "lg_ex", "lg_mask", "lg_rank", "h2_tr", "h2_ev", "ov_ready", "acc_zero"])

        block2_in, row_in, row_free = sem("block2_in"), sem("row_in"), sem("row_free")
        cx_sd, cx_n, cx_tr, cx_T = map(sem, ["cx_sd", "cx_n", "cx_tr", "cx_T"])
        m_ev, rope_q, rope_k, kt2_tr, kt2_ev, f_T1, f_T1ev, f_y, f_yev = map(
            sem, ["m_ev", "rope_q", "rope_k", "kt2_tr", "kt2_ev", "f_T1", "f_T1ev", "f_y", "f_yev"])
        b_qn, b_qtr, b_qT, b_s, b_M, b_E, b_T, b_P, b_O, b_done, at2_tr, at2_mix = map(
            sem, ["b_qn", "b_qtr", "b_qT", "b_s", "b_M", "b_E", "b_T", "b_P", "b_O", "b_done", "at2_tr", "at2_mix"])
        f_h, f_s, f_g = sem("f_h"), sem("f_s"), sem("f_g")
        p_tr, p_T, p_y = sem("p_tr"), sem("p_T"), sem("p_y")

        class Signals:

            def __init__(self, name):
                (self.sel, self.tok, self.tokT, self.h1, self.h3, self.silu, self.hid, self.tr, self.trT, self.y, self.yc,
                 self.out) = (sem(f"{name}_{n}") for n in ("sel", "tok", "tokT", "h1", "h3", "silu", "hid", "tr", "trT",
                                                           "y", "yc", "out"))

        first, later = Signals("first"), Signals("later")
        ov_loaded = [sem(f"ov_loaded{s}") for s in range(NS)]
        ov_used = sem("ov_used")
        first.loaded, first.used = loaded, ring_used
        later.loaded, later.used = ov_loaded, ov_used

        def chunk_slot(n):
            return ring[:, n % NS, :]

        def done(eng, n, i=None):
            eng.wait_ge(ring_used, NS + n + 1 if i is None else i * NS + (NS + n + 1))

        def ring_view(n, k):
            return chunk_slot(n).rearrange("p (k n) -> p k n", k=k)

        block = ctx.enter_context(nc.Block())

        @block.sync
        def _(sp):
            def load(n, src, k, w, i=None, per=NS):
                sp.wait_ge(ring_used, n + 1 if i is None else i * per + (n + 1))
                dst = chunk_slot(n)[:, 0:k * w].rearrange("p (k n) -> p k n", k=k)
                sp.dma_start(dst, src).then_inc(loaded[n % NS], 16)

            rows = lambda w: w.rearrange("(k p) n -> p k n", p=P)
            sp.dma_start(con[:, :], A["con"]).then_inc(con_in, 16)
            sp.dma_start(vec[:, :], A["vec"]).then_inc(con_in, 16)
            sp.dma_start(x[:, :, :], A["x"].rearrange("(t p) d -> p t d", p=P)).then_inc(x_in, 16)
            wa = rows(A["w_ada"])
            with sp.Fori(0, 2) as i:
                for s in range(NS):
                    load(RA + s, wa[:, :, bass.ds(i * (NS * 512) + s * 512, 512)], KD, 512, i)
            wi = rows(A["w_in"])
            for c, (a, b) in enumerate([(0, 512), (512, 1024), (1024, 1304), (1304, 1816), (1816, 2328), (2328, 2840)]):
                load(RW + c, wi[:, :, a:b], KD, b - a)
            load(RC, rows(A["cmp_k_w1"]), LPAIRS, CMP_HID)
            load(RC + 1, rows(A["cmp_v_w1"]), LPAIRS, CMP_HID)
            wa2 = rows(A["ada_w_2"])
            with sp.Fori(0, PAIRS) as i:
                for s in range(NS):
                    load(RL + s, wa2[:, :, bass.ds(i * (NS * 512) + s * 512, 512)], KD, 512, i)
            wo = rows(A["w_out"])
            for c in range(2):
                load(RO + c, wo[:, :, c * 512:(c + 1) * 512], KD, 512)
            def expert_loads(S, pair, i):
                for j, (w, k) in enumerate((("w1", KD), ("w3", KD), ("w2", FE // P))):
                    for u in range(2):
                        n = 2 * j + u
                        sp.wait_ge(S.used, i * NS + (n + 1 + (RE if S is first else 0)))
                        src = A[w][bass.ds(pair[u], 1)].rearrange("e (k p) n -> p (e k) n", p=P)
                        dst = chunk_slot(RE + n).rearrange("p (k n) -> p k n", k=k)
                        sp.dma_start(dst, src).then_inc(S.loaded[(RE + n) % NS], 16)

            with sp.Fori(0, E // 2) as i:
                expert_loads(first, (i * 2, i * 2 + 1), i)
            sp.wait_ge(ov_ready, 1)
            nov = sp.value_load(ovi[0:1, OVR:OVR + 1], min_val=0, max_val=NOV)
            with sp.If(nov > 0):
                sp.wait_ge(ring_used, NS + RE + 3 * E)
                with sp.Fori(0, OVR // 2) as i:
                    pair = [sp.value_load(ovi[0:1, bass.ds(i * 2 + u, 1)], min_val=0, max_val=E - 1) for u in range(2)]
                    expert_loads(later, pair, i)
                sp.wait_ge(ov_used, NS + 3 * OVR)
            sp.end_ifs()
            mi = rows(A["mix_in"])
            for c in range(3):
                w = min(512, 1280 - c * 512)
                load(RM + c, mi[:, :, c * 512:c * 512 + w], KD, w)
            mo = rows(A["mix_out"])
            for c in range(2):
                load(RM + 3 + c, mo[:, :, c * 512:(c + 1) * 512], KD, 512)

            def ffn_step(l, n, c, i=None):
                f13 = rows(A["f13"][l])
                f2 = A["f2"][l].rearrange("(k p) n -> p k n", p=P)
                at = c if i is None else i * 3 + c
                load(n, f13[:, :, c * 512:(c + 1) * 512] if i is None else
                     f13[:, :, bass.ds(i * 1536 + c * 512, 512)], KD, 512, i)
                load(n + 1, f2[:, 2 * c:2 * c + 2, :] if i is None else
                     f2[:, bass.ds(i * 6 + 2 * c, 2), :], 2, D, i)

            def ffn(l, n0):
                for c in range(PEEL):
                    ffn_step(l, n0 + 2 * c, c)
                with sp.Fori(0, (NF - PEEL) // 3) as i:
                    for u in range(3):
                        ffn_step(l, n0 + 2 * (PEEL + u), PEEL + u, i)

            ffn(0, RF0)
            load(RP, rows(A["pool_w"]), KD, 256)
            ffn(1, RF1)
            for t in range(NT):
                sp.wait_ge(x_new, 6 * NT + t + 1)
                sp.dma_start(out[0, t * P:(t + 1) * P, :], xn[:, t, :]).then_inc(out_done, 16)
            sp.wait_ge(out_done, 16 * NT)
        @block.gpsimd
        def _(pool):
            nc.gpsimd.memset(modrow[:, :], 0.0).then_inc(zeroed, 1)
            nc.gpsimd.memset(cond[:, :, :, :], 0.0).then_inc(zeroed, 1)
            nc.gpsimd.memset(vT[:, :, 0:2], 0.0).then_inc(zeroed, 1)
            nc.gpsimd.memset(epsc, EPS).then_inc(zeroed, 1)
            nc.gpsimd.memset(vc, 0.0).then_inc(zeroed, 1)

        @block.scalar
        def _(act):
            link = Chain(act, chainA)
            act.dma_start(relb[:, :], A["rel_bias"]).then_inc(tab_in, 16)
            act.dma_start(oh[:, :], A["oh"]).then_inc(tab_in, 16)
            act.dma_start(cw2[:, 0, :, :], A["cmp_k_w2"].rearrange("(j p) n -> p j n", p=P)).then_inc(misc_in, 16)
            act.dma_start(cw2[:, 1, :, :], A["cmp_v_w2"].rearrange("(j p) n -> p j n", p=P)).then_inc(misc_in, 16)
            act.dma_start(wr[:, :, :], A["wr"].rearrange("(k p) n -> p k n", p=P)).then_inc(misc_in, 16)
            act.dma_start(brB[:, :], A["br"].partition_broadcast(P)).then_inc(misc_in, 16)
            act.wait_ge(zeroed, 1)
            for l in range(3):
                act.dma_start(modrow[0:P:32, l * 1536:(l + 1) * 1536], A["adab"][l]).then_inc(bias_in, 16)
            act.dma_start(modrow[1:P:32, 1536:3072], A["adab"][1]).then_inc(bias_in, 16)
            act.wait_ge(con_in, 32)
            act.wait_ge(zeroed, 2)
            nc.scalar.activation(cond[:, 0, :, 0], V("c"), ACT.Silu)
            nc.scalar.activation(cond[:, 1, :, 0], V("c2"), ACT.Silu)
            nc.scalar.activation(cond[:, 1, :, 1], V("cctx"), ACT.Silu).then_inc(cond_ready, 1)

            def norm(u, ready):
                act.wait_ge(*ready)
                for t in range(NT):
                    last = nc.scalar.activation(xn[:, t, :], x[:, t, :], ACT.Square, accum_out=ss[:, t:t + 1])
                link(last)
                if u == 0:
                    act.wait_ge(zeroed, 4)
                nc.scalar.activation(sd2, ss, ACT.Sqrt, scale=1.0 / D, bias=epsc).then_inc(nrm_sq, 1)

            norm(0, (x_in, 16))
            for h in range(NH):
                act.wait_ge(tabr_mm, h + 1)
                nc.scalar.activation(tabrow[:, h, :], ps[:, h, 0:384], ACT.Copy).then_inc(tabr_ev, 1)
            act.wait_ge(tabr_ev, NH)
            act.dma_start(btab.rearrange("h (p n) -> p h n", p=P), tabrow).then_inc(btab_out, 16)
            act.wait_ge(btab_out, 16)
            for h in range(NH):
                src = btab[h, 127:127 + P * 383].rearrange("(p w) -> p w", w=383)[:, 0:256]
                act.dma_start(tab[:, h, 0:256], src).then_inc(tab_in, 16)

            done(act, RW + 0)
            for t in range(NT):
                last = nc.scalar.activation(q[:, t, :], ps[:, t, :], ACT.Copy)
            last.then_inc(win_act, 1)
            done(act, RW + 1)
            nc.scalar.activation(ksv, ps[:, 3, :].rearrange("p (t n) -> p t n", t=NT), ACT.Copy).then_inc(win_act, 1)
            done(act, RW + 2)
            for t in range(NT):
                last = nc.scalar.activation(kwg[:, t, :], ps[:, 4 + t, 0:280], ACT.Copy)
            link(last)
            for t in range(NT):
                last = nc.scalar.activation(
                    G3[:, :, :, 1 - t], kwg[:, t, 256:280].rearrange("p (h b) -> p h b", b=3), ACT.Sigmoid)
            last.then_inc(win_act, 1)
            done(act, RW + 3)
            nc.scalar.activation(bT, ps[:, 6:8, :].rearrange("p b (f t) -> p (b f) t", f=2), ACT.Copy).then_inc(win_act, 1)
            done(act, RW + 4)
            nc.scalar.activation(cT, ps[:, 0:2, :].rearrange("p b (f t) -> p (b f) t", f=2), ACT.Copy).then_inc(win_act, 1)
            act.wait_ge(qk_ss, 1)
            nc.scalar.activation(sd24, SS, ACT.Sqrt, scale=1.0 / HD, bias=epsc).then_inc(qk_sd, 1)
            act.wait_ge(cv_y, 1)
            nc.scalar.activation(sq.rearrange("p (f t) -> p f t", f=4), cT, ACT.Square).then_inc(cv_sq, 1)
            act.wait_ge(cv_sum, 1)
            nc.scalar.activation(sq, ps[:, 0:2, :].rearrange("p b n -> p (b n)"), ACT.Sqrt, scale=1.0 / HD,
                                 bias=epsc).then_inc(cv_sd, 1)
            done(act, RC + 1)
            nc.scalar.activation(hidS[0:30, :], ps[0:30, 4, :], ACT.Silu).then_inc(hid_act, 1)
            act.wait_ge(kc_ss, 1)
            nc.scalar.activation(sd24[0:NC, 0:2], SS[0:NC, 0:2], ACT.Sqrt, scale=1.0 / HD,
                                 bias=epsc[0:NC]).then_inc(kc_sd, 1)

            with act.Fori(0, PAIRS) as i:
                act.wait_ge(a_M, i + 1)
                for a in range(4):
                    h, b = a % 2, 1 + a // 2
                    for ii, (lo, hi) in enumerate([(0, 256), (256, 384)]):
                        last = nc.scalar.activation(L[:, a, lo:hi], L[:, a, lo:hi], ACT.Exp, bias=nM[:, h, b, ii:ii + 1],
                                                    accum_out=SM[:, h, b, ii:ii + 1])
                for h in range(2):
                    for ii, lo in enumerate([C1, C0]):
                        last = nc.scalar.activation(L[:, h, lo:lo + NC], L[:, h, lo:lo + NC], ACT.Exp,
                                                    bias=nM[:, h, 0, ii:ii + 1], accum_out=SM[:, h, 0, ii:ii + 1])
                last.then_inc(a_E, 1)
                act.wait_ge(a_T, i * 2 + 2)
                nc.scalar.activation(PTw, ps[:, 4:6, 0:384], ACT.Copy).then_inc(a_P, 1)
            act.wait_ge(at_ss, 1)
            nc.scalar.activation(sd24[:, 0:16], SS[:, 0:16], ACT.Sqrt, scale=1.0 / HD, bias=epsc).then_inc(at_sd, 1)
            act.wait_ge(g_mm, 1)
            nc.scalar.activation(gB[:, :], ps[:, 0:2, :].rearrange("p b n -> p (b n)"), ACT.Copy).then_inc(g_ev, 1)

            act.wait_ge(x_new, NT)
            act.dma_start(conb, A["conb"]).then_inc(block2_in, 16)
            act.dma_start(ctx_in, A["ctx"].rearrange("(t p) d -> p t d", p=P)).then_inc(block2_in, 16)
            act.dma_start(sinkB, A["sink"].partition_broadcast(P)).then_inc(block2_in, 16)
            norm(1, (x_new, NT))
            act.wait_ge(lg_gx, 1)
            nc.scalar.activation(r8[1], r8[0], ACT.Exp).then_inc(lg_ex, 1)
            act.wait_ge(h2_tr, 1)
            for t in range(NT):
                last = nc.scalar.activation(xn[:, t, :], ps[:, 4 + 2 * t:6 + 2 * t, :].rearrange("p b n -> p (b n)"),
                                            ACT.Copy)
            last.then_inc(h2_ev, 1)
            act.wait_ge(lg_gx, 2)
            nc.scalar.activation(r1[4], r1[3], ACT.Exp).then_inc(lg_ex, 1)

            def expert_pair(S, i):
                act.wait_ge(S.h1, i + 1)
                nc.scalar.activation(gsil, ps[:, 0, :], ACT.Silu).then_inc(S.silu, 1)
                act.wait_ge(S.y, i + 1)
                nc.scalar.activation(Ye, ps[:, 0:2, :].rearrange("p b n -> p (b n)"), ACT.Copy).then_inc(S.yc, 1)

            with act.Fori(0, E // 2) as i:
                expert_pair(first, i)
            act.wait_ge(ov_ready, 1)
            nov = act.value_load(ovi[0:1, OVR:OVR + 1], min_val=0, max_val=NOV)
            with act.If(nov > 0):
                with act.Fori(0, OVR // 2) as i:
                    expert_pair(later, i)
            act.end_ifs()
            act.wait_ge(g_mm, 2)
            nc.scalar.activation(gB[:, :], ps[:, 0:2, :].rearrange("p b n -> p (b n)"), ACT.Copy).then_inc(g_ev, 1)

            flat = lambda a, b: ps[:, a:b, :].rearrange("p b n -> p (b n)")
            norm(2, (x_new, 2 * NT))
            act.wait_ge(block2_in, 48)
            act.wait_ge(nrm_xn, 3)
            for t in range(NT):
                link(nc.scalar.activation(gB[:, :], ctx_in[:, t, :], ACT.Square, accum_out=cssc[:, t:t + 1]))
            nc.scalar.activation(cexc, cssc, ACT.Sqrt, scale=1.0 / D, bias=epsc).then_inc(cx_sd, 1)
            done(act, RM)
            nc.scalar.activation(u2.rearrange("p t n -> p (t n)"), flat(4, 6), ACT.Copy).then_inc(m_ev, 1)
            done(act, RM + 1)
            nc.scalar.activation(q2.rearrange("p t n -> p (t n)"), flat(6, 8), ACT.Copy).then_inc(m_ev, 1)
            done(act, RM + 2)
            nc.scalar.activation(kv2.rearrange("p t n -> p (t n)"), ps[:, 0, :], ACT.Copy)
            nc.scalar.activation(kvc.rearrange("p t n -> p (t n)"), ps[:, 1, :], ACT.Copy).then_inc(m_ev, 1)
            act.wait_ge(f_T1, 1)
            nc.scalar.activation(f1f, flat(4, 8), ACT.Copy).then_inc(f_T1ev, 1)
            act.wait_ge(f_y, 1)
            nc.scalar.activation(mixT[:, 0:4, :].rearrange("p k t -> p (k t)"), flat(0, 2), ACT.Copy).then_inc(f_yev, 1)
            with act.Fori(0, PAIRS) as i:
                act.wait_ge(b_M, i + 1)
                nc.scalar.activation(se, se, ACT.Exp)
                for a in range(4):
                    nc.scalar.activation(L2[:, a, 0:256], L2[:, a, 0:256], ACT.Exp, bias=nM2[:, a:a + 1],
                                         accum_out=s1[:, a:a + 1])
                    last = nc.scalar.activation(L2[:, a, 256:512], ps[:, a, 256:512], ACT.Exp, bias=nM2[:, a:a + 1],
                                                accum_out=s2[:, a:a + 1])
                last.then_inc(b_E, 1)
                act.wait_ge(b_T, i + 1)
                nc.scalar.activation(PT2[:, 0:2, :], ps[:, 0:2, :], ACT.Copy).then_inc(b_P, 1)

            def gate(n, b0):
                act.wait_ge(g_mm, n)
                nc.scalar.activation(gB[:, :], flat(b0, b0 + 2), ACT.Copy).then_inc(g_ev, 1)

            def ffn_step(l, u, c, i=None):
                for f in range(2):
                    n = 2 * NF * l + 2 * c + f + 1
                    b = (2 * u + f) % 3
                    act.wait_ge(f_h, n if i is None else i * 6 + n)
                    nc.scalar.activation(gs[:, b, :], ps[:, b, 0:256], ACT.Silu).then_inc(f_s, 1)

            def ffn(l):
                for c in range(PEEL):
                    ffn_step(l, c + 1, c)
                with act.Fori(0, (NF - PEEL) // 3) as i:
                    for u in range(3):
                        ffn_step(l, u, PEEL + u, i)

            gate(3, 2)
            norm(3, (x_new, 3 * NT))
            ffn(0)
            gate(4, 0)
            act.wait_ge(x_new, 4 * NT)
            act.dma_start(rowB, A["pscale"].partition_broadcast(P)).then_inc(row_in, 16)
            norm(4, (x_new, 4 * NT))
            gate(5, 4)
            act.wait_ge(x_new, 5 * NT)
            act.dma_start(rowB, A["final_g"].partition_broadcast(P)).then_inc(row_in, 16)
            norm(5, (x_new, 5 * NT))
            ffn(1)
            gate(6, 0)
            norm(6, (x_new, 6 * NT))

        @block.vector
        def _(dve):
            link = Chain(dve, chainD)
            tt, ts, stt = nc.vector.tensor_tensor, nc.vector.tensor_scalar, nc.vector.scalar_tensor_tensor

            def modulation(src, w):
                stt(Acol, src[:, 8:16], 1.0, w, ALU.add, ALU.mult)
                link(nc.vector.tensor_copy(Bcol, src[:, 0:8]))

            def norm(u, banks=4):
                dve.wait_ge(nrm_sq, u + 1)
                link(nc.vector.reciprocal(rstd, sd2))
                for t in range(NT):
                    last = ts(xn[:, t, :], x[:, t, :], rstd[:, t:t + 1], None, ALU.mult)
                last.then_inc(nrm_xn, 1)

            def norm_out(u, b0):
                dve.wait_ge(nrm_tr, u + 1)
                for k in range(KD):
                    last = ts(hT[:, k, :], ps[:, b0 + k // 2, (k % 2) * T:(k % 2 + 1) * T], Acol[:, k:k + 1],
                              Bcol[:, k:k + 1], ALU.mult, ALU.add)
                last.then_inc(nrm_hT, 1)

            def columns(l):
                dve.wait_ge(col_tr, l + 1)
                v = ps[:, 2:4, :].rearrange("p b (c n) -> p (b c) n", n=P)
                last = nc.vector.tensor_copy(modcol[:, l, :].rearrange("p (c j) -> p c j", j=4), v[:, :, 0:P:32])
                if l == 1:
                    last = nc.vector.tensor_copy(ctxcol[:, :].rearrange("p (c j) -> p c j", j=4), v[:, 0:4, 1:P:32])
                last.then_inc(col_ev, 1)

            dve.sem_inc(ada_ev, 1)
            norm(0)
            psf = ps[:, 0:2, :].rearrange("p b n -> p (b n)")[:, 0:768]
            dve.wait_ge(bias_in, 64)
            with dve.Fori(0, 2) as i:
                done(dve, RA + NS - 1, i)
                m = modrow[:, bass.ds(i * 768, 768)]
                tt(m, psf, m, ALU.add).then_inc(ada_ev, 1)
            columns(0)
            dve.wait_ge(col_ev, 1)
            modulation(modcol[:, 0, :], V("norm1"))
            norm_out(0, 4)

            done(dve, RW + 1)
            for v in range(2):
                for g in range(2):
                    src = ps[64 * g:64 * g + 64, 2, v * T:(v + 1) * T]
                    nc.vector.tensor_copy(kvT2[0:64, v, g, :], src)
                    last = nc.vector.tensor_copy(kvT2[64:128, v, g, 0:T - 1], src[:, 1:T])
            last.then_inc(win_dve, 1)
            dve.wait_ge(win_dve, 1)
            for v in range(2):
                pos = V("posk" if v == 0 else "posv")
                for g in range(2):
                    for half in range(2):
                        src = kvT2[:, v, g, 16 * half:16 * half + 240].rearrange("p (n m) -> p m n", m=16)[:, 0:16:2, :]
                        last = tt(blk[:, v, 8 * half:8 * half + 8, g, :], src,
                                  pos[:, 8 * half:8 * half + 8].unsqueeze(2).to_broadcast([P, 8, NC]), ALU.add)
            last.then_inc(blk_ready, 1)

            dve.wait_ge(win_act, 3)
            qh = q.rearrange("p t (h d) -> p (t h) d", d=HD)
            sq3 = sq.rearrange("p (h d) -> p h d", d=HD)
            link(tt(sq3, qh, qh, ALU.mult))
            link(nc.vector.tensor_reduce(SS[:, 0:16], sq3, AX.X, ALU.add))
            for n, kk in enumerate((ksv, kwg)):
                k4 = kk[:, :, 0:P]
                s4 = sq[:, 0:256].rearrange("p (t n) -> p t n", t=2)
                link(tt(s4, k4, k4, ALU.mult))
                link(nc.vector.tensor_reduce(SS[:, 16 + 4 * n:20 + 4 * n], sq3[:, 0:4, :], AX.X, ALU.add))
            dve.sem_inc(qk_ss, 1)
            dve.wait_ge(qk_sd, 1)
            link(nc.vector.reciprocal(RS, sd24))
            for n, kk in enumerate((ksv, kwg)):
                for t in range(NT):
                    k3 = kk[:, t, 0:P].rearrange("p (g d) -> p g d", g=2)
                    r = RS[:, 16 + 4 * n + 2 * t:18 + 4 * n + 2 * t].unsqueeze(2).to_broadcast([P, 2, HD])
                    last = tt(k3, k3, r, ALU.mult)
            last.then_inc(k_n, 1)

            done(dve, RW + 5)
            dve.wait_ge(win_act, 5)
            dve.wait_ge(zeroed, 3)
            link(tt(vT[:, :, 2:258], ps[:, 2:4, :].rearrange("p b (f t) -> p (b f) t", f=2), cT, ALU.mult))
            cw = V("conv").rearrange("p (j f) -> p j f", j=3)
            for f in range(4):
                last = ts(cT[:, f, :], vT[:, f, 2:258], cw[:, 2, f:f + 1], None, ALU.mult)
            link(last)
            for j in (1, 0):
                for f in range(4):
                    last = stt(cT[:, f, :], vT[:, f, j:j + T], cw[:, j, f:f + 1], cT[:, f, :], ALU.mult, ALU.add)
                link(last)
            tt(cT, cT, bT, ALU.mult).then_inc(cv_y, 1)
            dve.wait_ge(k_tr, 1)
            kn = V("kn")
            ts(kTs, ps[:, 7, 0:256], kn[:, 1:2], None, ALU.mult)
            ts(kTw, ps[:, 7, 256:512], kn[:, 2:3], None, ALU.mult).then_inc(k_ready, 1)
            dve.wait_ge(cv_sd, 1)
            link(nc.vector.reciprocal(sq, sq))
            for f in range(4):
                last = stt(mixT[:, 4 + f, :], cT[:, f, :], V("outn")[:, 4 + f:5 + f], sq[:, f * T:(f + 1) * T], ALU.mult,
                           ALU.mult)
            last.then_inc(cv_mix, 1)
            dve.wait_ge(hidT_tr, 1)
            nc.vector.tensor_copy(hidT[:, :, 0:30], ps[:, 5, 0:128].rearrange("p (v n) -> p v n", v=4)[:, :, 0:30]
                                  ).then_inc(hidT_ev, 1)
            dve.wait_ge(kc_mm, 1)
            kc = ps[0:NC, 6, 0:128]
            dve.wait_ge(zeroed, 5)
            nc.vector.tensor_copy(vc[0:NC, 0, :, :], ps[0:NC, 6, 128:256].rearrange("p (g d) -> p g d", g=2))
            nc.vector.tensor_copy(vc[32:32 + NC, 1, :, :], ps[32:32 + NC, 6, 128:256].rearrange("p (g d) -> p g d", g=2))
            link(nc.vector.tensor_copy(kcn[0:NC, :], kc))
            link(tt(hidS[0:NC, 0:128], kcn[0:NC, :], kcn[0:NC, :], ALU.mult))
            nc.vector.tensor_reduce(SS[0:NC, 0:2], hidS[0:NC, 0:128].rearrange("p (g d) -> p g d", g=2), AX.X,
                                    ALU.add).then_inc(kc_ss, 1)
            dve.wait_ge(kc_sd, 1)
            link(nc.vector.reciprocal(sd24[0:NC, 2:4], sd24[0:NC, 0:2]))
            tt(kcn[0:NC, :].rearrange("p (g d) -> p g d", g=2), kcn[0:NC, :].rearrange("p (g d) -> p g d", g=2),
               sd24[0:NC, 2:4].unsqueeze(2).to_broadcast([NC, 2, HD]), ALU.mult).then_inc(kc_n, 1)
            dve.wait_ge(kc_tr, 1)
            ts(kcT[:, 0:NC], ps[:, 6, 256:256 + NC], kn[:, 0:1], None, ALU.mult).then_inc(kc_ready, 1)
            dve.wait_ge(tab_in, 32 + 16 * NH)
            link(tt(tab[:, :, 0:256], tab[:, :, 0:256], C("cmask").unsqueeze(1).to_broadcast([P, NH, 256]), ALU.add))
            nc.vector.tensor_copy(tab[:, :, 256:384], tab[:, :, 128:256])
            nc.vector.memset(tab[:, :, C0 + 7:C0 + NC], NEG)
            nc.vector.tensor_copy(tab[:, :, C0:C0 + 7], tab[:, :, 159:256:16])
            nc.vector.memset(L[:, 0:2, C1 + NC:C0], 0.0)
            link(nc.vector.tensor_copy(tab[:, :, C1:C1 + NC], tab[:, :, 31:256:16]))

            q5 = q.rearrange("p t (h i d) -> p t h i d", h=2, d=HD)
            r5 = RS[:, 0:16].rearrange("p (t h i) -> p t h i", t=2, h=2)
            tab4 = tab.rearrange("p (h i) n -> p h i n", h=2)
            G4 = G3.rearrange("p (h i) b j -> p h i (b j)", h=2)
            attn5 = attn.rearrange("p j (h i) d -> p h j i d", h=2)
            with dve.Fori(0, PAIRS) as i:
                link.enter(i, 7)
                one = bass.ds(i, 1)
                tt(qn, q5[:, :, :, one, :].rearrange("p t h i d -> p t h (i d)"),
                   r5[:, :, :, one].to_broadcast([P, 2, 2, HD]), ALU.mult).then_inc(a_qn, 1)
                dve.wait_ge(a_qtr, i + 1)
                ts(qT, ps[:, 7, 0:T], V("qn"), SCALE, ALU.mult, ALU.mult).then_inc(a_qT, 1)
                tb = tab4[:, :, one, :].rearrange("p h i n -> p h (i n)")
                dve.wait_ge(a_s, i + 1)
                tt(L[:, 0:2, 0:384], ps[:, 2:4, 0:384], tb[:, :, 0:384], ALU.add)
                split = lambda ap: ap.rearrange("p h (j n) -> p h j n", j=2)[:, :, :, 0:NC]
                tt(split(L[:, 0:2, C1:TABW]), split(ps[:, 2:4, C1:TABW]), split(tb[:, :, C1:TABW]), ALU.add)
                dve.wait_ge(a_w, i + 1)
                link(tt(L[:, 2:4, 0:384], ps[:, 4:6, 0:384], tb[:, :, 0:384], ALU.add))
                Lb = L.rearrange("p (b h) n -> p h b n", b=2)
                nc.vector.tensor_reduce(nM[:, :, 1:3, 0], Lb[:, :, :, 0:256], AX.X, ALU.max, negate=True)
                nc.vector.tensor_reduce(nM[:, :, 1:3, 1], Lb[:, :, :, 256:384], AX.X, ALU.max, negate=True)
                link(nc.vector.tensor_reduce(nM[:, :, 0, :], split(L[:, 0:2, C1:TABW]), AX.X, ALU.max, negate=True))
                ts(nM[:, :, 0, :], nM[:, :, 0, :], -0.01 * NEG, None, ALU.min).then_inc(a_M, 1)
                dve.wait_ge(a_E, i + 1)
                link(ts(CO, SM, 1e-30, None, ALU.max))
                link(nc.vector.reciprocal(CO, CO))
                g = G4[:, :, one, :].rearrange("p h i n -> p h (i n)")
                COf = CO.rearrange("p h b j -> p h (b j)")
                link(tt(COf, COf, g, ALU.mult))
                dve.wait_ge(a_T, i * 2 + 1)
                nc.vector.tensor_copy(PTs[:, :, 0:384], ps[:, 2:4, 0:384])
                nc.vector.tensor_copy(PTs[0:47, :, 384:512], ps[0:47, 2:4, 384:512]).then_inc(a_P, 1)
                dve.wait_ge(a_O, i + 1)
                link(tt(Ot.rearrange("p h b j d -> p h (b j) d"), ps[:, 6:8, 0:384].rearrange("p h (c d) -> p h c d", d=HD),
                        COf.unsqueeze(3).to_broadcast([P, 2, 6, HD]), ALU.mult))
                link(tt(Ot[:, :, 0], Ot[:, :, 0], Ot[:, :, 1], ALU.add))
                tt(attn5[:, :, :, one, :].rearrange("p h j i d -> p h j (i d)"), Ot[:, :, 0], Ot[:, :, 2], ALU.add
                   ).then_inc(a_done, 1)
                done(dve, RL + NS - 1, i)
                m = modrow[:, bass.ds(i * 768 + 1536, 768)]
                tt(m, psf, m, ALU.add).then_inc(ada_ev, 1)
            link.leave(PAIRS)
            dve.wait_ge(a_done, PAIRS)
            at3 = attn.rearrange("p j h d -> p (j h) d")
            sqa = zone[:, 0:1024].rearrange("p (h d) -> p h d", d=HD)
            link(tt(sqa, at3, at3, ALU.mult))
            nc.vector.tensor_reduce(SS[:, 0:16], sqa, AX.X, ALU.add).then_inc(at_ss, 1)
            dve.wait_ge(at_sd, 1)
            link(nc.vector.reciprocal(RS[:, 0:16], sd24[:, 0:16]))
            tt(at3, at3, RS[:, 0:16].unsqueeze(2).to_broadcast([P, 16, HD]), ALU.mult).then_inc(at_n, 1)
            dve.wait_ge(at_tr, 1)
            for j in range(4):
                last = ts(mixT[:, j, :], ps[:, 2 + j // 2, (j % 2) * T:(j % 2 + 1) * T], V("outn")[:, j:j + 1], None, ALU.mult)
            last.then_inc(at_mix, 1)
            dve.wait_ge(g_ev, 1)
            done(dve, RO + 1)
            y = ps[:, 4:8, :].rearrange("p (t c) n -> p t (c n)", t=NT)
            for t in range(NT):
                link(tt(xn[:, t, :], y[:, t, :], gB[:, :], ALU.mult))
                tt(x[:, t, :], x[:, t, :], xn[:, t, :], ALU.add).then_inc(x_new, 1)

            columns(1)
            columns(2)
            modulation(modcol[:, 0, 16:32], V("norm2"))
            norm(1)
            norm_out(1, 4)
            dve.wait_ge(misc_in, 64)
            dve.wait_ge(lg_mm, 1)
            b2 = lambda ap: ap.unsqueeze(2).to_broadcast([P, NT, 8])
            lgg = lg[:, :, 0:8]
            link(tt(lg, ps[:, 0, 0:144].rearrange("p (t e) -> p t e", t=NT),
                    brB[:, :].unsqueeze(1).to_broadcast([P, NT, 72]), ALU.add))
            gmax, gsum, gp, d21, rr, w1c, w2c, mx = r1
            gx, gex, onehot_g, ein, o1, o2, e2, tmp8 = r8
            rev = C("rev").unsqueeze(1).to_broadcast([P, NT, 8])

            def first_max(onehot, v, m):
                link(nc.vector.tensor_reduce(m, v, AX.X, ALU.max))
                link(tt(tmp8, v, b2(m), ALU.is_equal))
                link(tt(tmp8, tmp8, rev, ALU.mult))
                link(nc.vector.tensor_reduce(mx, tmp8, AX.X, ALU.max))
                link(tt(onehot, tmp8, b2(mx), ALU.is_equal))

            link(nc.vector.tensor_reduce(gmax, lgg, AX.X, ALU.max))
            tt(gx, lgg, b2(gmax), ALU.subtract).then_inc(lg_gx, 1)
            first_max(onehot_g, lgg, w2c)
            pv = prod[:, 0:128].rearrange("p (t e g) -> p t e g", t=NT, e=8)
            link(tt(pv, lg[:, :, 8:72].rearrange("p t (g e) -> p t e g", g=8),
                    onehot_g.unsqueeze(2).to_broadcast([P, NT, 8, 8]), ALU.mult))
            link(nc.vector.tensor_reduce(ein, pv, AX.X, ALU.add))
            first_max(o1, ein, w1c)
            link(stt(e2, o1, 2 * NEG, ein, ALU.mult, ALU.add))
            first_max(o2, e2, w2c)
            tt(d21, w2c, w1c, ALU.subtract).then_inc(lg_gx, 1)
            link(tt(tmp8, o1, o2, ALU.add))
            mt = msk.rearrange("p t (g e) -> p t g e", g=8)
            tt(mt, onehot_g.unsqueeze(3).to_broadcast([P, NT, 8, 8]), tmp8.unsqueeze(2).to_broadcast([P, NT, 8, 8]),
               ALU.mult).then_inc(lg_mask, 1)
            dve.wait_ge(lg_ex, 1)
            link(nc.vector.tensor_reduce(gsum, gex, AX.X, ALU.add))
            link(nc.vector.reciprocal(gp, gsum))
            dve.wait_ge(lg_ex, 2)
            link(ts(w1c, rr, 1.0, None, ALU.add))
            link(nc.vector.reciprocal(w1c, w1c))
            link(tt(w1c, w1c, gp, ALU.mult))
            link(tt(w2c, w1c, rr, ALU.mult))
            link(tt(o1, o1, b2(w1c), ALU.mult))
            link(tt(o2, o2, b2(w2c), ALU.mult))
            link(tt(o1, o1, o2, ALU.add))
            nc.vector.memset(gat[:, :, E:ECOL], 0.0)
            nc.vector.memset(rnk[:, :, E:ECOL], 0.0)
            nc.vector.memset(Ye, 0.0).then_inc(acc_zero, 1)
            link(tt(gat[:, :, 0:E].rearrange("p t (g e) -> p t g e", g=8),
                    onehot_g.unsqueeze(3).to_broadcast([P, NT, 8, 8]), o1.unsqueeze(2).to_broadcast([P, NT, 8, 8]),
                    ALU.mult))
            dve.wait_ge(lg_rank, 1)
            rk = ps[:, 1, 0:128].rearrange("p (t e) -> p t e", t=NT)
            link(tt(rnk[:, :, 0:E], rk, msk, ALU.mult))

            def select(S, cols):
                four = lambda ap: ap.rearrange("p t (e s) -> p t e s", e=2)
                iota = C("iota").unsqueeze(1).to_broadcast([P, 2, SLOTS])
                bc = lambda ap: ap[:, :, cols].unsqueeze(3).to_broadcast([P, NT, 2, SLOTS])
                for t in range(NT):
                    last = tt(four(Ssel)[:, t], bc(rnk)[:, t], iota, ALU.is_equal)
                link(last)
                for t in range(NT):
                    last = tt(four(SG)[:, t], four(Ssel)[:, t], bc(gat)[:, t], ALU.mult)
                last.then_inc(S.sel, 1)

            def gathered(S, v):
                dve.wait_ge(S.tok, v)
                nc.vector.tensor_copy(XeT, ps[:, 2:4, :].rearrange("p b (k s) -> p (b k) s", s=P)).then_inc(S.tokT, 1)

            def expert_pair(S, i, cols):
                dve.wait_ge(S.silu, i + 1)
                dve.wait_ge(S.h3, i + 1)
                tt(hexp, gsil, ps[:, 1, :], ALU.mult).then_inc(S.hid, 1)
                dve.wait_ge(S.tr, i + 1)
                nc.vector.tensor_copy(SGT, ps[:, 2, 0:T])
                nc.vector.tensor_copy(heT.rearrange("p f s -> p (f s)"), ps[:, 3, :]).then_inc(S.trT, 1)
                select(S, cols)
                gathered(S, i + (1 + (S is first)))

            link(nc.vector.tensor_copy(cnt, ps[:, 1, 128:192]))
            select(first, slice(0, 2))
            link(ts(nx, cnt, float(SLOTS), None, ALU.is_gt))
            link(stt(nx, cnt, 2.0 * SLOTS, nx, ALU.is_gt, ALU.add))
            link(stt(nx, cnt, 3.0 * SLOTS, nx, ALU.is_gt, ALU.add))
            gathered(first, 1)
            link(nc.vector.tensor_tensor_scan(ce, C("ones")[:, 0:E], nx, 0.0, ALU.mult, ALU.add))
            link(tt(cex, ce, nx, ALU.subtract))
            for b in range(NOV):
                last = ts(selo[:, b, :], ce, float(b), None, ALU.is_gt)
            link(last)
            for b in range(NOV):
                last = stt(selo[:, b, :], cex, float(b), selo[:, b, :], ALU.is_le, ALU.mult)
            link(last)
            pe3 = prod[:, 0:NOV * E].rearrange("p (b e) -> p b e", b=NOV)
            rb = lambda ap: ap.unsqueeze(1).to_broadcast([P, NOV, E])
            link(tt(pe3, selo, rb(cex), ALU.mult))
            off = r8[6].rearrange("p t e -> p (t e)")[:, 0:NOV]
            link(nc.vector.tensor_reduce(off, pe3, AX.X, ALU.add))
            link(tt(off, off, C("iota")[:, 0:NOV], ALU.subtract))
            link(ts(off, off, float(SLOTS), None, ALU.mult))
            for t in range(NT):
                link(tt(pe3, selo, rb(rnk[:, t, 0:E]), ALU.mult))
                link(nc.vector.tensor_reduce(rnk[:, t, E:E + NOV], pe3, AX.X, ALU.add))
                link(tt(rnk[:, t, E:E + NOV], rnk[:, t, E:E + NOV], off, ALU.add))
                link(tt(pe3, selo, rb(gat[:, t, 0:E]), ALU.mult))
                link(nc.vector.tensor_reduce(gat[:, t, E:E + NOV], pe3, AX.X, ALU.add))
            link(nc.vector.memset(ovf, 0.0))
            link(tt(pe3, selo, rb(C("eidx")), ALU.mult))
            link(nc.vector.tensor_reduce(ovf[:, 0:NOV], pe3, AX.X, ALU.add))
            link(nc.vector.tensor_copy(ovf[:, OVR:OVR + 1], ce[:, E - 1:E]))
            nc.vector.tensor_copy(ovi, ovf).then_inc(ov_ready, 1)

            with dve.Fori(0, E // 2) as i:
                link.enter(i, 1)
                expert_pair(first, i, bass.ds(i * 2 + 2, 2))
            link.leave(E // 2)
            dve.wait_ge(ov_ready, 1)
            nov = dve.value_load(ovi[0:1, OVR:OVR + 1], min_val=0, max_val=NOV)
            with dve.If(nov > 0):
                dve.sem_inc(later.tokT, 1)
                with dve.Fori(0, OVR // 2) as i:
                    link.enter(i, 1)
                    expert_pair(later, i, bass.ds(i * 2 + (E + 2), 2))
            dve.end_ifs()
            link = Chain(dve, chainD2)
            dve.wait_ge(g_ev, 2)
            for t in range(NT):
                link(tt(xn[:, t, :], y[:, t, :], gB[:, :], ALU.mult))
                tt(x[:, t, :], x[:, t, :], xn[:, t, :], ALU.add).then_inc(x_new, 1)

            def residual(b0, n, done_at):
                dve.wait_ge(g_ev, n)
                done_at()
                yy = ps[:, b0:b0 + 4, :].rearrange("p (t c) n -> p t (c n)", t=NT)
                for t in range(NT):
                    link(tt(xn[:, t, :], yy[:, t, :], gB[:, :], ALU.mult))
                    tt(x[:, t, :], x[:, t, :], xn[:, t, :], ALU.add).then_inc(x_new, 1)

            norm(2)
            (modulation(modcol[:, 1, :], V("nmix0")))
            norm_out(2, 4)
            dve.wait_ge(cx_sd, 1)
            link(nc.vector.reciprocal(cexc, cexc))
            for t in range(NT):
                last = ts(ctx_in[:, t, :], ctx_in[:, t, :], cexc[:, t:t + 1], None, ALU.mult)
            last.then_inc(cx_n, 1)
            dve.wait_ge(nrm_hT, 3)
            modulation(ctxcol[:, :], V("nmix0"))
            dve.wait_ge(cx_tr, 1)
            for k in range(KD):
                last = ts(ctxT[:, k, :], ps[:, k // 2, (k % 2) * T:(k % 2 + 1) * T], Acol[:, k:k + 1], Bcol[:, k:k + 1],
                          ALU.mult, ALU.add)
            last.then_inc(cx_T, 1)

            def rope(v, heads, sig):
                x1 = v.rearrange("p t (h f) -> p t h f", h=heads)[:, :, :, 0::2]
                x2 = v.rearrange("p t (h f) -> p t h f", h=heads)[:, :, :, 1::2]
                w = NT * heads * 32
                m = [xnf[:, n * 512:n * 512 + w].rearrange("p (t h f) -> p t h f", t=NT, h=heads) for n in range(4)]
                cs = [CB(n).rearrange("p (t f) -> p t f", t=NT).unsqueeze(2).to_broadcast([P, NT, heads, 32])
                      for n in ("rcos", "rsin")]
                for n, (a, b) in enumerate(((x1, 0), (x2, 1), (x1, 1), (x2, 0))):
                    for t in range(NT):
                        last = tt(m[n][:, t], a[:, t], cs[b][:, t], ALU.mult)
                link(last)
                for t in range(NT):
                    tt(x1[:, t], m[0][:, t], m[1][:, t], ALU.subtract)
                    last = tt(x2[:, t], m[2][:, t], m[3][:, t], ALU.add)
                last.then_inc(sig, 1)

            dve.wait_ge(m_ev, 3)
            dve.wait_ge(block2_in, 48)
            rope(kv2[:, :, 0:P], NKV, rope_k)
            dve.wait_ge(rope_k, 1)
            rope(q2, NH, rope_q)
            dve.wait_ge(kt2_tr, 1)
            nc.vector.tensor_copy(f1f[:, 0:512], ps[:, 2, :]).then_inc(kt2_ev, 1)
            dve.wait_ge(rope_q, 1)
            q52 = q2.rearrange("p t (h i d) -> p t h i d", h=2, d=HD)
            at5 = attn2.rearrange("p t (h i) d -> p t h i d", h=2)
            sk = sinkB.rearrange("p (h i) -> p h i", h=2)
            ih = lambda ap: ap.rearrange("p (i h) -> p i h", i=2)
            with dve.Fori(0, PAIRS) as i:
                link.enter(i, 9)
                one = bass.ds(i, 1)
                ts(qn2, q52[:, :, :, one, :].rearrange("p t h i d -> p t h (i d)"), SCALE, None, ALU.mult).then_inc(b_qn, 1)
                dve.wait_ge(b_qtr, i + 1)
                nc.vector.tensor_copy(qT2, ps[:, 7, 0:T]).then_inc(b_qT, 1)
                dve.wait_ge(b_s, i + 1)
                for t in range(NT):
                    last = tt(L2[:, 2 * t:2 * t + 2, 0:256], ps[:, 2 * t:2 * t + 2, 0:256],
                              CB("wmask").rearrange("p (t n) -> p t n", t=NT)[:, t:t + 1, :].to_broadcast([P, 2, 256]),
                              ALU.add)
                link(last)
                nc.vector.tensor_reduce(mc2, ps[:, 0:4, 256:512], AX.X, ALU.max)
                link(nc.vector.tensor_reduce(nM2, L2[:, :, 0:256], AX.X, ALU.max))
                link(tt(nM2, nM2, mc2, ALU.max))
                skb = sk[:, :, one].rearrange("p h i -> p (h i)").unsqueeze(1).to_broadcast([P, 2, 2])
                link(tt(ih(nM2), ih(nM2), skb, ALU.max))
                link(ts(nM2, nM2, -1.0, None, ALU.mult))
                tt(ih(se), ih(nM2), skb, ALU.add).then_inc(b_M, 1)
                dve.wait_ge(b_E, i + 1)
                link(tt(s1, s1, s2, ALU.add))
                link(tt(s1, s1, se, ALU.add))
                link(nc.vector.reciprocal(s1, s1))
                dve.wait_ge(b_T, i + 1)
                nc.vector.tensor_copy(PT2[:, 2:4, :], ps[:, 2:4, :]).then_inc(b_P, 1)
                dve.wait_ge(b_O, i + 1)
                for t in range(NT):
                    last = tt(at5[:, t, :, one, :].rearrange("p h i d -> p h (i d)"),
                              ps[:, 4, t * 128:(t + 1) * 128].rearrange("p (h d) -> p h d", h=2),
                              s1[:, 2 * t:2 * t + 2].unsqueeze(2).to_broadcast([P, 2, HD]), ALU.mult)
                link(last)
            link.leave(PAIRS)
            dve.sem_inc(b_done, 1)
            dve.wait_ge(at2_tr, 1)
            nc.vector.tensor_copy(mixT[:, 4:8, :].rearrange("p k t -> p (k t)"),
                                  ps[:, 5:7, :].rearrange("p b n -> p (b n)")).then_inc(at2_mix, 1)
            residual(4, 3, lambda: done(dve, RM + 4))

            def ffn_step(l, u, c, i=None):
                for f in range(2):
                    n = 2 * NF * l + 2 * c + f + 1
                    dve.wait_ge(f_s, n if i is None else i * 6 + n)
                    b = 2 * u + f
                    tt(gT[:, b, :], gs[:, b % 3, :], ps[:, b % 3, 256:512], ALU.mult).then_inc(f_g, 1)

            def ffn(l):
                for c in range(PEEL):
                    ffn_step(l, c + 1, c)
                with dve.Fori(0, (NF - PEEL) // 3) as i:
                    for u in range(3):
                        ffn_step(l, u, PEEL + u, i)

            norm(3)
            (modulation(modcol[:, 1, 16:32], V("nffn0")))
            norm_out(3, 4)
            ffn(0)
            residual(4, 4, lambda: None)
            norm(4)
            (modulation(modcol[:, 2, :], V("nmix1")))
            dve.wait_ge(p_tr, 1)
            for k in range(KD):
                last = ts(hT[:, k, :], ps[:, 4 + k // 2, (k % 2) * T:(k % 2 + 1) * T], Acol[:, k:k + 1], None, ALU.mult)
            last.then_inc(p_T, 1)
            dve.wait_ge(g_ev, 5)
            dve.wait_ge(row_in, 16)
            link(tt(gB[:, :], gB[:, :], rowB, ALU.mult))
            residual(0, 5, lambda: done(dve, RP))
            norm(5)
            (modulation(modcol[:, 2, 16:32], V("nffn1")))
            norm_out(4, 4)
            ffn(1)
            residual(4, 6, lambda: None)
            norm(6)
            dve.wait_ge(nrm_xn, 7)
            dve.wait_ge(row_in, 32)
            for t in range(NT):
                tt(xn[:, t, :], xn[:, t, :], rowB, ALU.mult).then_inc(x_new, 1)

        @block.tensor
        def _(pe):
            mm, tr = nc.tensor.matmul, nc.tensor.transpose

            def arrived(n, i=None):
                v = 16 * (n // NS + 1)
                pe.wait_ge(loaded[n % NS], v if i is None else i * 16 + v)

            def ada_chunk(n, s, cset, i=None):
                arrived(n, i)
                w = ring_view(n, KD)
                for k in range(KD):
                    for j in range(4):
                        last = mm(ps[32 * j:32 * j + 32, s // 4, (s % 4) * P:(s % 4 + 1) * P], cond[:, cset, k, :],
                                  w[:, k, j * P:(j + 1) * P], start=(k == 0), stop=(k == KD - 1))
                return last

            def columns(l):
                for n, c in enumerate((0, 1, 2, 3, 6, 7, 8, 9)):
                    last = tr(ps[:, 2 + n // 4, (n % 4) * P:(n % 4 + 1) * P],
                              modrow[:, l * 1536 + c * P:l * 1536 + (c + 1) * P], ident)
                last.then_inc(col_tr, 1)

            def gate_row(l, c0, b0):
                for c in range(2):
                    for j in range(4):
                        last = mm(ps[:, b0 + c, j * P:(j + 1) * P], sel[:, j, :],
                                  modrow[:, l * 1536 + (c0 + c) * P:l * 1536 + (c0 + c + 1) * P], start=True, stop=True)
                last.then_inc(g_mm, 1)

            def norm_tr(u, b0):
                pe.wait_ge(nrm_xn, u + 1)
                for k in range(KD):
                    for t in range(NT):
                        last = tr(ps[:, b0 + k // 2, (k % 2) * T + t * P:(k % 2) * T + (t + 1) * P],
                                  xn[:, t, k * P:(k + 1) * P], ident)
                last.then_inc(nrm_tr, 1)

            pe.sem_inc(ring_used, NS)
            pe.wait_ge(tab_in, 32)
            for h in range(NH):
                mm(ps[:, h, 0:384], relb[:, h:h + 1].to_broadcast([NB, P]), oh[:, :], start=True, stop=True
                   ).then_inc(tabr_mm, 1)
            pe.wait_ge(con_in, 32)
            pe.wait_ge(tabr_ev, NH)
            norm_tr(0, 4)
            pe.wait_ge(cond_ready, 1)
            with pe.Fori(0, 2) as i:
                pe.wait_ge(ada_ev, i + 1)
                for s in range(NS):
                    ada_chunk(RA + s, s, 0, i).then_inc(ring_used, 1)
            pe.wait_ge(ada_ev, 3)
            columns(0)

            def tokens(n, w, banks, at=0):
                arrived(n)
                v = chunk_slot(n)[:, 0:KD * w[1]].rearrange("p (k n) -> p k n", k=KD)
                for t in range(NT):
                    for k in range(KD):
                        last = mm(banks[t], hT[:, k, t * P:(t + 1) * P], v[:, k, w[0]:w[0] + banks[t].shape[1]],
                                  start=(k == 0), stop=(k == KD - 1))
                return last

            def features(n, w, tiles, b0):
                arrived(n)
                v = chunk_slot(n)[:, 0:KD * w].rearrange("p (k n) -> p k n", k=KD)
                for f in range(tiles):
                    for k in range(KD):
                        last = mm(ps[:, b0 + f // 2, (f % 2) * T:(f % 2 + 1) * T], v[:, k, f * P:(f + 1) * P], hT[:, k, :],
                                  start=(k == 0), stop=(k == KD - 1))
                return last

            pe.wait_ge(nrm_hT, 1)
            tokens(RW, (0, 512), [ps[:, t, :] for t in range(NT)]).then_inc(ring_used, 1)
            features(RW + 1, 512, 2, 2)
            tokens(RW + 1, (256, 512), [ps[:, 3, t * 256:(t + 1) * 256] for t in range(NT)]).then_inc(ring_used, 1)
            tokens(RW + 2, (0, 280), [ps[:, 4 + t, 0:280] for t in range(NT)]).then_inc(ring_used, 1)
            features(RW + 3, 512, 4, 6).then_inc(ring_used, 1)
            pe.wait_ge(win_act, 1)
            features(RW + 4, 512, 4, 0).then_inc(ring_used, 1)
            pe.wait_ge(win_act, 2)
            pe.wait_ge(win_dve, 1)
            features(RW + 5, 512, 4, 2).then_inc(ring_used, 1)
            pe.wait_ge(k_n, 1)
            pe.wait_ge(win_act, 4)
            for n, kk in enumerate((ksv, kwg)):
                for t in range(NT):
                    last = tr(ps[:, 7, n * T + t * P:n * T + (t + 1) * P], kk[:, t, 0:P], ident)
            last.then_inc(k_tr, 1)
            pe.wait_ge(cv_sq, 1)
            for f in range(4):
                last = mm(ps[:, f // 2, (f % 2) * T:(f % 2 + 1) * T], C("bd"), sq[:, f * T:(f + 1) * T], start=True,
                          stop=True)
            last.then_inc(cv_sum, 1)
            pe.wait_ge(blk_ready, 1)
            for v in range(2):
                arrived(RC + v)
                w = ring_view(RC + v, LPAIRS)
                for m in range(LPAIRS):
                    last = mm(ps[0:30, 4, v * CMP_HID:(v + 1) * CMP_HID], blk[:, v, m, :, :].rearrange("p g n -> p (g n)"),
                              w[:, m, :], start=(m == 0), stop=(m == LPAIRS - 1))
                last.then_inc(ring_used, 1)
            pe.wait_ge(hid_act, 1)
            for v in range(4):
                last = tr(ps[:, 5, v * 32:v * 32 + 30], hidS[0:30, v * P:(v + 1) * P], ident[0:30, 0:30])
            last.then_inc(hidT_tr, 1)
            pe.wait_ge(hidT_ev, 1)
            pe.wait_ge(misc_in, 64)
            for v in range(2):
                for p0 in ((0,) if v == 0 else (0, 32)):
                    for g in range(2):
                        for j in range(2):
                            last = mm(ps[p0:p0 + NC, 6, v * P + g * HD:v * P + (g + 1) * HD],
                                      hidT[:, 2 * v + j, g * NC:(g + 1) * NC], cw2[:, v, j, :], start=(j == 0),
                                      stop=(j == 1))
            last.then_inc(kc_mm, 1)
            pe.wait_ge(kc_n, 1)
            tr(ps[:, 6, 256:256 + NC], kcn[0:NC, :], ident[0:NC, 0:NC]).then_inc(kc_tr, 1)
            pe.wait_ge(kc_ready, 1)
            pe.wait_ge(k_ready, 1)

            with pe.Fori(0, PAIRS) as i:
                pe.wait_ge(a_qn, i + 1)
                for t in range(NT):
                    last = tr(ps[:, 7, t * P:(t + 1) * P], qn[:, t, :, :].rearrange("p h d -> p (h d)"), ident)
                last.then_inc(a_qtr, 1)
                pe.wait_ge(ada_ev, i + 3)
                ada = lambda s: ada_chunk(RL + s, s, 1, i).then_inc(ring_used, 1)
                ada(0)
                pe.wait_ge(a_qT, i + 1)
                for b, (kT, b0) in enumerate(((kTs, 2), (kTw, 4))):
                    for h in range(2):
                        r = slice(64 * h, 64 * h + 64)
                        mm(ps[:, b0 + h, 0:256], qT[r, P:T], kT[r, :], start=True, stop=True)
                        last = mm(ps[:, b0 + h, 256:384], qT[r, 0:P], kT[r, 0:P], start=True, stop=True)
                        if b == 0:
                            mm(ps[:, b0 + h, C1:C1 + NC], qT[r, P:T], kcT[r, 0:NC], start=True, stop=True)
                            last = mm(ps[:, b0 + h, C0:C0 + NC], qT[r, 0:P], kcT[r, 0:NC], start=True, stop=True)
                    last.then_inc((a_s, a_w)[b], 1)
                ada(1)
                ada(2)
                pe.wait_ge(a_E, i + 1)
                for b, b0 in enumerate((2, 4)):
                    for h in range(2):
                        for c in range(3):
                            last = tr(ps[:, b0 + h, c * P:(c + 1) * P], L[:, 2 * b + h, c * P:(c + 1) * P], ident)
                        if b == 0:
                            last = tr(ps[0:47, b0 + h, 384:512], L[:, h, C1:C1 + 47], ident)
                    last.then_inc(a_T, 1)
                ada(3)
                pe.wait_ge(a_P, i * 2 + 2)
                for h in range(2):
                    o = lambda b, ii: ps[:, 6 + h, (2 * b + ii) * HD:(2 * b + ii + 1) * HD]
                    for ii in range(2):
                        mm(o(0, ii), PTs[0:47, h, 384:512], vc[0:47, ii, h, :], start=True, stop=True)
                    for b, (PT, kv) in enumerate(((PTs, ksv), (PTw, kwg))):
                        vv = [kv[:, t, P + h * HD:P + (h + 1) * HD] for t in range(NT)]
                        mm(o(1 + b, 0), PT[:, h, 0:P], vv[0], start=True, stop=False)
                        mm(o(1 + b, 0), PT[:, h, P:2 * P], vv[1], start=False, stop=True)
                        last = mm(o(1 + b, 1), PT[:, h, 2 * P:3 * P], vv[0], start=True, stop=True)
                last.then_inc(a_O, 1)
                ada(4)
                ada(5)

            pe.wait_ge(ada_ev, 7)
            gate_row(0, 4, 0)
            pe.wait_ge(at_n, 1)
            a2 = attn.rearrange("p j h d -> p j (h d)")
            for j in range(4):
                for t in range(NT):
                    last = tr(ps[:, 2 + j // 2, (j % 2) * T + t * P:(j % 2) * T + (t + 1) * P],
                              a2[:, 1 - t, j * P:(j + 1) * P], ident)
            last.then_inc(at_tr, 1)
            pe.wait_ge(at_mix, 1)
            pe.wait_ge(cv_mix, 1)

            def project_out(n0, src, b0):
                for c in range(2):
                    arrived(n0 + c)
                    w = ring_view(n0 + c, KD)
                    for t in range(NT):
                        for k in range(KD):
                            last = mm(ps[:, b0 + 2 * t + c, :], src[:, k, t * P:(t + 1) * P], w[:, k, :], start=(k == 0),
                                      stop=(k == KD - 1))
                    last.then_inc(ring_used, 1)

            project_out(RO, mixT, 4)
            columns(1)
            pe.wait_ge(col_ev, 2)
            columns(2)
            norm_tr(1, 4)
            pe.wait_ge(nrm_hT, 2)
            pe.wait_ge(g_ev, 1)
            for t in range(NT):
                for k in range(KD):
                    last = mm(ps[:, 0, t * 72:(t + 1) * 72], hT[:, k, t * P:(t + 1) * P], wr[:, k, :], start=(k == 0),
                              stop=(k == KD - 1))
            last.then_inc(lg_mm, 1)
            for t in range(NT):
                for k in range(KD):
                    last = tr(ps[:, 4 + 2 * t + k // 4, (k % 4) * P:(k % 4 + 1) * P], hT[:, k, t * P:(t + 1) * P], ident)
            last.then_inc(h2_tr, 1)
            pe.wait_ge(lg_mask, 1)
            mm(ps[:, 1, 0:E], tri, msk[:, 0, :], start=True, stop=True)
            mm(ps[:, 1, E:2 * E], ones, msk[:, 0, :], start=True, stop=False)
            mm(ps[:, 1, E:2 * E], tri, msk[:, 1, :], start=False, stop=True)
            mm(ps[:, 1, 2 * E:3 * E], ones, msk[:, 0, :], start=True, stop=False)
            mm(ps[:, 1, 2 * E:3 * E], ones, msk[:, 1, :], start=False, stop=True).then_inc(lg_rank, 1)
            pe.wait_ge(h2_ev, 1)
            pe.wait_ge(acc_zero, 1)
            for b in range(4, 8):
                mm(ps[:, b, :], ident, Ye[:, 0:512], start=True, stop=True)

            def gather(S, v):
                pe.wait_ge(S.sel, v)
                for k in range(KD):
                    for t in range(NT):
                        last = mm(ps[:, 2 + k // 4, (k % 4) * P:(k % 4 + 1) * P], xn[:, t, k * P:(k + 1) * P],
                                  Ssel[:, t, :], start=(t == 0), stop=(t == NT - 1))
                last.then_inc(S.tok, 1)

            def expert_pair(S, i):
                half = (slice(0, SLOTS), slice(SLOTS, P))

                def weights(j, k):
                    for n in (RE + 2 * j, RE + 2 * j + 1):
                        pe.wait_ge(S.loaded[n % NS], i * 16 + (16 * (n // NS + 1) if S is first else 16))
                    return [chunk_slot(RE + 2 * j + u).rearrange("p (k n) -> p k n", k=k) for u in range(2)]

                pe.wait_ge(S.tokT, i + 1)
                for j in range(2):
                    w = weights(j, KD)
                    for k in range(KD):
                        for u in range(2):
                            last = mm(ps[half[u], j, :], XeT[:, k, half[u]], w[u][:, k, :], start=(k == 0),
                                      stop=(k == KD - 1))
                    last.then_inc((S.h1, S.h3)[j], 1)
                    if j == 0:
                        for t in range(NT):
                            tr(ps[:, 2, t * P:(t + 1) * P], SG[:, t, :], ident)
                pe.wait_ge(S.hid, i + 1)
                pe.sem_inc(S.used, 4)
                for f in range(FE // P):
                    last = tr(ps[:, 3, f * P:(f + 1) * P], hexp[:, f * P:(f + 1) * P], ident)
                last.then_inc(S.tr, 1)
                w = weights(2, FE // P)
                pe.wait_ge(S.trT, i + 1)
                for k in range(FE // P):
                    for m in range(2):
                        for u in range(2):
                            last = mm(ps[half[u], m, :], heT[:, k, half[u]], w[u][:, k, m * 512:(m + 1) * 512],
                                      start=(k == 0), stop=(k == FE // P - 1))
                last.then_inc(S.y, 1)
                gather(S, i + (1 + (S is first)))
                pe.wait_ge(S.yc, i + 1)
                pe.sem_inc(S.used, 2)
                for t in range(NT):
                    for m in range(2):
                        last = mm(ps[:, 4 + 2 * t + m, :], SGT[:, t * P:(t + 1) * P], Ye[:, m * 512:(m + 1) * 512],
                                  start=False, stop=True, skip_group_check=True)
                last.then_inc(S.out, 1)

            gather(first, 1)
            with pe.Fori(0, E // 2) as i:
                expert_pair(first, i)
            pe.wait_ge(ov_ready, 1)
            nov = pe.value_load(ovi[0:1, OVR:OVR + 1], min_val=0, max_val=NOV)
            with pe.If(nov > 0):
                pe.sem_inc(ov_used, NS)
                pe.wait_ge(first.tokT, E // 2 + 1)
                with pe.Fori(0, OVR // 2) as i:
                    expert_pair(later, i)
            pe.end_ifs()
            gate_row(0, 10, 0)
            norm_tr(2, 4)
            pe.wait_ge(cx_n, 1)
            pe.wait_ge(g_ev, 2)
            for k in range(KD):
                for t in range(NT):
                    last = tr(ps[:, k // 2, (k % 2) * T + t * P:(k % 2) * T + (t + 1) * P],
                              ctx_in[:, t, k * P:(k + 1) * P], ident)
            last.then_inc(cx_tr, 1)
            pe.wait_ge(nrm_hT, 3)
            tokens(RM, (0, 512), [ps[:, 4 + t, :] for t in range(NT)]).then_inc(ring_used, 1)
            tokens(RM + 1, (0, 512), [ps[:, 6 + t, :] for t in range(NT)]).then_inc(ring_used, 1)
            pe.wait_ge(cx_T, 1)
            tokens(RM + 2, (0, 256), [ps[:, 0, t * 256:(t + 1) * 256] for t in range(NT)])
            w = ring[:, (RM + 2) % NS, 0:2048].rearrange("p (k n) -> p k n", k=KD)
            for t in range(NT):
                for k in range(KD):
                    last = mm(ps[:, 1, t * 256:(t + 1) * 256], ctxT[:, k, t * P:(t + 1) * P], w[:, k, :], start=(k == 0),
                              stop=(k == KD - 1))
            last.then_inc(ring_used, 1)
            pe.wait_ge(m_ev, 2)
            for h in range(4):
                for c, n in enumerate(("cosn", "sinn")):
                    F = CB(n).rearrange("p (t n) -> p t n", t=NT)
                    for t in range(NT):
                        last = mm(ps[:, 4 + h, c * T:(c + 1) * T], u2[:, t, h * P:(h + 1) * P], F[:, t, :],
                                  start=(t == 0), stop=(t == NT - 1))
            last.then_inc(f_T1, 1)
            pe.wait_ge(f_T1ev, 1)
            pe.wait_ge(m_ev, 3)
            for h in range(4):
                for c, n in enumerate(("cosd", "nsind")):
                    last = mm(ps[:, h // 2, (h % 2) * T:(h % 2 + 1) * T], CB(n), T1[:, h, c, :], start=(c == 0),
                              stop=(c == 1))
            last.then_inc(f_y, 1)
            pe.wait_ge(rope_k, 1)
            for n, kk in enumerate((kv2, kvc)):
                for t in range(NT):
                    last = tr(ps[:, 2, n * T + t * P:n * T + (t + 1) * P], kk[:, t, 0:P], ident)
            last.then_inc(kt2_tr, 1)
            pe.wait_ge(kt2_ev, 1)
            pe.wait_ge(f_yev, 1)
            with pe.Fori(0, PAIRS) as i:
                pe.wait_ge(b_qn, i + 1)
                for t in range(NT):
                    last = tr(ps[:, 7, t * P:(t + 1) * P], qn2[:, t, :, :].rearrange("p h d -> p (h d)"), ident)
                last.then_inc(b_qtr, 1)
                pe.wait_ge(b_qT, i + 1)
                for t in range(NT):
                    for h in range(2):
                        r = slice(64 * h, 64 * h + 64)
                        mm(ps[:, 2 * t + h, 0:256], qT2[r, t * P:(t + 1) * P], kT2[r, :], start=True, stop=True)
                        last = mm(ps[:, 2 * t + h, 256:512], qT2[r, t * P:(t + 1) * P], kcT2[r, :], start=True, stop=True)
                last.then_inc(b_s, 1)
                pe.wait_ge(b_E, i + 1)
                for a in range(4):
                    for k in range(4):
                        last = tr(ps[:, a, k * P:(k + 1) * P], L2[:, a, k * P:(k + 1) * P], ident)
                last.then_inc(b_T, 1)
                pe.wait_ge(b_P, i * 2 + 2)
                for a in range(4):
                    for k in range(4):
                        vv = (kv2, kvc)[k // 2][:, k % 2, P + (a % 2) * HD:P + (a % 2 + 1) * HD]
                        last = mm(ps[:, 4, a * HD:(a + 1) * HD], PT2[:, a, k * P:(k + 1) * P], vv, start=(k == 0),
                                  stop=(k == 3))
                last.then_inc(b_O, 1)
            pe.wait_ge(b_done, 1)
            af = attn2.rearrange("p t h d -> p t (h d)")
            for j in range(4):
                for t in range(NT):
                    last = tr(ps[:, 5 + j // 2, (j % 2) * T + t * P:(j % 2) * T + (t + 1) * P],
                              af[:, t, j * P:(j + 1) * P], ident)
            last.then_inc(at2_tr, 1)
            gate_row(1, 4, 2)
            pe.wait_ge(at2_mix, 1)
            project_out(RM + 3, mixT, 4)

            def ffn_step(l, n, u, c, i=None):
                arrived(n, i)
                w = ring_view(n, KD)
                for f in range(2):
                    for j in range(2):
                        for k in range(KD):
                            last = mm(ps[:, (2 * u + f) % 3, j * T:(j + 1) * T],
                                      w[:, k, j * FCH + f * P:j * FCH + (f + 1) * P], hT[:, k, :], start=(k == 0),
                                      stop=(k == KD - 1))
                    last.then_inc(f_h, 1)
                arrived(n + 1, i)
                w = ring[:, (n + 1) % NS, 0:2 * D].rearrange("p (k n) -> p k n", k=2)
                for f in range(2):
                    g = 2 * NF * l + 2 * c + f + 1
                    pe.wait_ge(f_g, g if i is None else i * 6 + g)
                    for t in range(NT):
                        for m in range(2):
                            last = mm(ps[:, 4 + 2 * t + m, :], gT[:, 2 * u + f, t * P:(t + 1) * P],
                                      w[:, f, m * 512:(m + 1) * 512], start=(i is None and c == 0 and f == 0),
                                      stop=(c == NF - 1), skip_group_check=True)
                last.then_inc(ring_used, 2)

            def ffn(l, n0):
                for c in range(PEEL):
                    ffn_step(l, n0 + 2 * c, c + 1, c)
                with pe.Fori(0, (NF - PEEL) // 3) as i:
                    for u in range(3):
                        ffn_step(l, n0 + 2 * (PEEL + u), u, PEEL + u, i)

            norm_tr(3, 4)
            pe.wait_ge(nrm_hT, 4)
            pe.wait_ge(g_ev, 3)
            ffn(0, RF0)
            gate_row(1, 10, 0)
            pe.wait_ge(nrm_xn, 5)
            pw = CB("pool").rearrange("p (t g n) -> p t g n", t=NT, g=4)
            for k in range(KD):
                for t in range(NT):
                    last = mm(ps[:, 4 + k // 2, (k % 2) * T:(k % 2 + 1) * T], xn[:, t, k * P:(k + 1) * P],
                              pw[:, t, k // 2, :], start=(t == 0), stop=(t == NT - 1))
            last.then_inc(p_tr, 1)
            arrived(RP)
            w = ring[:, RP % NS, 0:2048].rearrange("p (k n) -> p k n", k=KD)
            pe.wait_ge(p_T, 1)
            gate_row(2, 4, 4)
            for g in range(4):
                for t in range(NT):
                    for k in range(2):
                        last = mm(ps[:, 2 * t + g // 2, (g % 2) * 256:(g % 2 + 1) * 256],
                                  hT[:, 2 * g + k, t * P:(t + 1) * P], w[:, 2 * g + k, :], start=(k == 0), stop=(k == 1))
            last.then_inc(ring_used, 1)
            pe.wait_ge(nrm_xn, 6)
            norm_tr(5, 4)
            pe.wait_ge(nrm_hT, 5)
            ffn(1, RF1)
            gate_row(2, 10, 0)


def t5_buckets(n):
    n = np.maximum(n, 0)
    f = np.float32
    large = 16 + (np.log(np.maximum(n, 1).astype(f) / f(16)) / f(math.log(128 / 16)) * f(16)).astype(np.int32)
    return np.where(n < 16, n, np.minimum(large, NB - 1))


def constants():
    f = np.float32
    p = np.arange(P)
    con = np.zeros((P, NCON), f)

    def put(into, where, n, v):
        a, b = where[n]
        into[:, a:b] = np.asarray(v, f).reshape(P, b - a)

    put(con, CON, "ident", np.eye(P))
    put(con, CON, "tri", np.triu(np.ones((P, P))))
    put(con, CON, "ones", np.ones((P, P)))
    put(con, CON, "bd", np.kron(np.eye(2), np.ones((64, 64))))
    put(con, CON, "sel", np.repeat((p[:, None] == 32 * np.arange(4))[:, :, None], P, 2))
    put(con, CON, "iota", np.tile(np.arange(1, SLOTS + 1), (P, 1)))
    put(con, CON, "rev", np.tile(np.arange(8, 0, -1), (P, 1)))
    put(con, CON, "eidx", np.tile(np.arange(E), (P, 1)))
    put(con, CON, "cmask", np.where(np.arange(256)[None] > 128 + p[:, None], NEG, 0.0))
    conb = np.zeros((P, NCONB), f)
    n = np.arange(T)
    ang = 2 * np.pi * np.outer(n, n) / T
    norm = 1 / math.sqrt(T * 128)
    tiled = lambda m: m.reshape(NT, P, -1).transpose(1, 0, 2)
    put(conb, CONB, "cosn", tiled(np.cos(ang) * norm))
    put(conb, CONB, "sinn", tiled(np.sin(ang) * norm))
    ang = 2 * np.pi * np.outer(p, p) / P
    put(conb, CONB, "cosd", np.cos(ang))
    put(conb, CONB, "nsind", -np.sin(ang))
    pool = np.zeros((T, 4, T))
    for g, w in enumerate((2, 4, 8, 16)):
        for t in range(T):
            lo, hi = max(t - w // 2, 0), min(t + w // 2, T)
            pool[lo:hi, g, t] = 1.0 / (hi - lo)
            pool[t, g, t] -= 1.0
    put(conb, CONB, "pool", tiled(pool.reshape(T, 4 * T)))
    row, col = (n // 64).astype(f), (n % 64).astype(f)
    inv = (f(10000.0) ** (-np.arange(16, dtype=f) / f(16))).astype(f)
    ang = np.concatenate([row[:, None] * inv, col[:, None] * inv], 1).astype(f)
    put(conb, CONB, "rcos", tiled(np.cos(ang)))
    put(conb, CONB, "rsin", tiled(np.sin(ang)))
    put(conb, CONB, "wmask", tiled(np.where(np.abs(n[:, None] - n[None]) > 128, NEG, 0.0)))
    oh = np.zeros((NB, 384), f)
    oh[t5_buckets(255 - np.arange(384)), np.arange(384)] = 1.0
    return con, conb, oh


def kernel(**inputs):
    import concourse.bacc as _bacc
    from concourse.bass_utils import run_bass_kernel_spmd as _run

    a = {k: np.asarray(v) for k, v in inputs.items()}
    col = lambda v: np.reshape(v, (-1, P)).T
    con, conb, oh = constants()
    kn = a["k_norm_w"][0]
    vec = np.concatenate([
        col(a["norm1_w"]), col(a["norm2_w"]), col(a["out_norm_w"]), col(a["norm_mix_g_2"]), col(a["norm_ffn_g_2"]),
        col(a["pool_scale_2"]), col(a["c"]), col(a["c_2"]), col(a["c_ctx_2"]),
        col(np.concatenate([a["q_norm_w"][0]] * 2)), col(np.concatenate([kn, kn], 1)), col(a["cmp_pos_k"]),
        col(a["cmp_pos_v"]), col(a["conv_w"])], 1)
    biases = np.stack([a["b_ada"][0], a["ada_b_2"][0], a["ada_b_2"][1]])
    arrays = {
        "con": con, "conb": conb, "oh": oh, "vec": vec, "x": a["x"][0], "ctx": a["ctx_2"][0],
        "adab": biases.reshape(3, 12, 4, P).transpose(0, 2, 1, 3).reshape(3, 4, 1536),
        "w_ada": a["w_ada"][0], "ada_w_2": a["ada_w_2"].transpose(1, 0, 2).reshape(D, -1),
        "w_in": a["w_in"][0], "cmp_k_w1": a["cmp_k_w1"][0], "cmp_v_w1": a["cmp_v_w1"][0],
        "cmp_k_w2": a["cmp_k_w2"][0], "cmp_v_w2": a["cmp_v_w2"][0], "w_out": a["w_out"][0],
        "rel_bias": a["rel_bias"], "wr": np.concatenate([a["w_group"][0], a["w_expert"][0]], 1),
        "br": np.concatenate([a["b_group"][0], a["b_expert"][0]]),
        "w1": a["w1"][0], "w3": a["w3"][0], "w2": a["w2"][0],
        "mix_in": a["mix_in_w_2"][0], "mix_out": a["mix_out_w_2"][0], "sink": a["attn_sink_2"][0],
        "pool_w": a["pool_w_2"][0].reshape(D, 256), "f13": np.stack([a["ffn_w1_2"].reshape(2, D, NF, FCH), a["ffn_w3_2"].reshape(2, D, NF, FCH)], 3
                        ).reshape(2, D, 2 * FFN), "f2": a["ffn_w2_2"],
        "final_g": a["final_g_2"], "pscale": a["pool_scale_2"][0],
    }
    arrays = {k: np.ascontiguousarray(v) for k, v in arrays.items()}
    nc = _bacc.Bacc("TRN2", target_bir_lowering=False, num_devices=1)
    A = {k: nc.dram_tensor(f"in_{k}", v.shape, F32, kind="ExternalInput").ap() for k, v in arrays.items()}
    out = nc.dram_tensor("out", (1, T, D), F32, kind="ExternalOutput").ap()
    build(nc, A, out)
    r = _run(nc, [{f"in_{k}": v for k, v in arrays.items()}], core_ids=[0])
    return r.results[0]["out"]
```

```python
import math
from contextlib import ExitStack

import numpy as np
import concourse.bass as bass
from concourse import mybir

F32 = mybir.dt.float32
F32R = mybir.dt.float32r
I32 = mybir.dt.int32
ACT = mybir.ActivationFunctionType
ALU = mybir.AluOpType
AX = mybir.AxisListType

P = 128
T = 256
NT = T // P
D = 1024
KD = D // P
HD = 64
NH = 8
NKV = 2
PAIRS = NH // NKV
EPS = 1e-6
NEG = -1.0e30
SCALE = HD ** -0.5
CMP_STRIDE, CMP_LEN = 16, 32
NC = (T - CMP_LEN) // CMP_STRIDE + 1
LPAIRS = CMP_LEN // 2
CMP_HID = 256
NB = 32
TABW = 448
C1, C0 = 384, 416
E = 64
FE = 512
SLOTS = 64
NOV = 7
OVR = NOV + 1
ECOL = E + OVR + 2
FFN = 2816
FCH = 256
NS = 6
CHUNK = 4096

VEC = {}
_at = 0
for _n, _w in [("norm1", 8), ("norm2", 8), ("outn", 8), ("nmix0", 8), ("nmix1", 8), ("nffn0", 8), ("nffn1", 8),
               ("pscale", 8), ("c", 8), ("c2", 8), ("cctx", 8), ("qn", 1), ("kn", 3), ("posk", 16), ("posv", 16),
               ("conv", 12)]:
    VEC[_n] = (_at, _at + _w)
    _at += _w
NVEC = _at

CON, CONB = {}, {}
_at = 0
for _n, _w in [("ident", 128), ("tri", 128), ("ones", 128), ("bd", 128), ("sel", 512), ("iota", 64), ("rev", 8),
               ("eidx", 64), ("cmask", 256)]:
    CON[_n] = (_at, _at + _w)
    _at += _w
NCON = _at
_at = 0
for _n, _w in [("cosn", 512), ("sinn", 512), ("cosd", 128), ("nsind", 128), ("pool", 2048), ("rcos", 64),
               ("rsin", 64), ("wmask", 512)]:
    CONB[_n] = (_at, _at + _w)
    _at += _w
NCONB = _at

RA = (0, 1, 2, 3, 8, 9, 10, 11, 14, 15, 18, 19)
RW = (4, 5, 6, 7, 12, 13)
RC = 16
RL0 = 20
RO = RL0 + 12
RK = RO + 2
RE = RK + 1
RM = RE + 3 * E
RL1 = RM + 3
RMO = RL1 + 12
NF = FFN // FCH
ADA_COLS = (0, 1, 2, 3, 6, 7, 8, 9)
PEEL = 2


class Chain:

    def __init__(self, eng, sem):
        self.eng, self.sem, self.n, self.i = eng, sem, 0, None

    def __call__(self, ins):
        ins.then_inc(self.sem, 1)
        self.n += 1
        at = self.n if self.i is None else self.i * self.per + (self.before + self.n)
        self.eng.wait_ge(self.sem, at)

    def enter(self, i, per):
        self.before, self.n, self.i, self.per = self.n, 0, i, per

    def leave(self, times):
        assert self.n == self.per, (self.n, self.per)
        self.n, self.i = self.before + times * self.per, None


def build(nc, A, out):
    with ExitStack() as ctx:
        base = {}

        def sb(n, s, d=F32):
            t = ctx.enter_context(nc.sbuf_tensor(n, s, d))
            base[n] = nc.sbuf_base - 4 * int(np.prod(s[1:]))
            assert base[n] % 32 == 0
            return t

        def parts(n, s):
            return nc.alloc_sbuf_tensor_at(n + "_parts", s, F32, offset=base[n])

        sem = lambda n: ctx.enter_context(nc.semaphore(n))

        ring = sb("ring", [P, NS, CHUNK])
        con = sb("con", [P, NCON])
        vec = sb("vec", [P, NVEC])
        x = sb("x", [P, NT, D])
        xn = sb("xn", [P, NT, D])
        hT = sb("hT", [P, KD, T])
        mixT = sb("mixT", [P, KD, T])
        modrow = sb("modrow", [P, 3 * 1536])
        modcol = sb("modcol", [P, 3, 32])
        ctxcol = sb("ctxcol", [P, 16])
        cond = sb("cond", [P, 2, KD, 32])
        gB = sb("gB", [P, D])
        small = sb("small", [P, 256])
        wr = sb("wr", [P, KD, 72])
        brB = sb("brB", [P, 72])
        oh, relb = gB[0:NB, 0:384], gB[0:NB, 384:384 + NH]
        cw2 = sb("cw2", [P, 2, 2, HD])
        arena = sb("arena", [P, 11400])
        ringR, hTR, mixTR, arenaR = (parts(*a) for a in (
            ("ring", [P, NS, CHUNK]), ("hT", [P, KD * T]), ("mixT", [P, KD * T]), ("arena", [P, 11400])))
        ps = ctx.enter_context(nc.psum_tensor("ps", [P, 8, 512], F32))

        epsc = small[:, 0:1]
        ss = small[:, 2:4]
        rstd = small[:, 4:6]
        Acol = small[:, 8:16]
        Bcol = small[:, 16:24]
        SS = small[:, 24:48]
        RS = small[:, 48:72]
        nM = small[:, 72:84].rearrange("p (h b i) -> p h b i", h=2, b=3)
        SM = small[:, 84:96].rearrange("p (h b i) -> p h b i", h=2, b=3)
        CO = small[:, 96:108].rearrange("p (h b i) -> p h b i", h=2, b=3)
        sd24 = small[:, 112:136]
        G3 = small[:, 136:184].rearrange("p (h b i) -> p h b i", h=8, b=3)
        sd2 = small[:, 184:186]

        def C(n):
            return con[:, CON[n][0]:CON[n][1]]

        def V(n):
            return vec[:, VEC[n][0]:VEC[n][1]]

        ident, ones, tri = C("ident"), C("ones"), C("tri")
        sel = C("sel").rearrange("p (j m) -> p j m", j=4)

        at = [0]

        def take(n):
            at[0] += n
            assert at[0] <= 11400, at[0]
            return arena[:, at[0] - n:at[0]]

        q = take(1024).rearrange("p (t n) -> p t n", t=NT)
        ksv = take(512).rearrange("p (t n) -> p t n", t=NT)
        kwg = take(560).rearrange("p (t n) -> p t n", t=NT)
        kTs, kTw = take(256), take(256)
        zone = take(3104)
        bT = zone[:, 0:1024].rearrange("p (f t) -> p f t", f=4)
        cT = zone[:, 1024:2048].rearrange("p (f t) -> p f t", f=4)
        vT = zone[:, 2048:2048 + 4 * 258].rearrange("p (f t) -> p f t", f=4)
        L = zone[:, 0:4 * TABW].rearrange("p (a n) -> p a n", a=4)
        PTs = zone[:, 1792:2816].rearrange("p (h n) -> p h n", h=2)
        hTf = hT[:, :, :].rearrange("p k t -> p (k t)")
        PTw = hTf[:, 0:768].rearrange("p (h n) -> p h n", h=2)
        qT = hTf[:, 768:1024]
        qn = hTf[:, 1024:1280].rearrange("p (t h d) -> p t h d", t=2, h=2)
        xnf = xn[:, :, :].rearrange("p t d -> p (t d)")
        sq = xnf[:, 0:1024]
        attn = xnf[:, 0:1024].rearrange("p (i h d) -> p i h d", i=2, h=NH)
        Ot = xnf[:, 1024:1792].rearrange("p (h b i d) -> p h b i d", h=2, b=3, i=2)
        kvT2 = xnf[:, 1024:2048].rearrange("p (v g t) -> p v g t", v=2, g=2)
        blk = take(2 * LPAIRS * 2 * NC).rearrange("p (v m g n) -> p v m g n", v=2, m=LPAIRS, g=2)
        hidS = xnf[:, 1024:1536]
        hidT = xnf[:, 1536:1664].rearrange("p (v n) -> p v n", v=4)
        kcn = xnf[:, 1664:1792]
        vc = take(256).rearrange("p (i g d) -> p i g d", i=2, g=2)
        kcT = take(16)
        tab = take(NH * TABW).rearrange("p (h n) -> p h n", h=NH)
        tabrow = tab.rearrange("p h n -> p (h n)")[:, 0:NH * 384].rearrange("p (h n) -> p h n", h=NH)
        btab = nc.dram_tensor("btab", (NH, P * 384), F32, kind="Internal").ap()

        at[0] = 0
        gat = take(2 * ECOL).rearrange("p (t e) -> p t e", t=NT)
        rnk = take(2 * ECOL).rearrange("p (t e) -> p t e", t=NT)
        msk = take(2 * E).rearrange("p (t e) -> p t e", t=NT)
        lg = take(144).rearrange("p (t e) -> p t e", t=NT)
        prod = take(2 * NOV * E)
        selo = take(NOV * E).rearrange("p (b e) -> p b e", b=NOV)
        cnt, nx, ce, cex = take(E), take(E), take(E), take(E)
        r8 = [take(16).rearrange("p (t e) -> p t e", t=NT) for _ in range(8)]
        r1 = [take(2) for _ in range(8)]
        ovf = take(10)
        ovi = take(10).bitcast(I32)
        Ssel, SG = (take(NT * P).rearrange("p (t s) -> p t s", t=NT) for _ in range(2))
        XeT = mixT[:, :, 0:P]
        gsil = take(FE)
        hexp = gsil
        SGT = take(T)
        heT = take(FE).rearrange("p (f s) -> p f s", f=FE // P)
        Ye = take(D)
        at[0] = max(at[0], 5120)
        conb = take(NCONB)
        ctx_in = take(NT * D).rearrange("p (t d) -> p t d", t=NT)
        at[0] = 0
        u2 = take(1024).rearrange("p (t n) -> p t n", t=NT)
        attn2 = u2.rearrange("p t (h d) -> p t h d", d=HD)
        T1 = take(2048).rearrange("p (h c n) -> p h c n", h=4, c=2)
        q2 = take(1024).rearrange("p (t n) -> p t n", t=NT)
        kv2 = take(512).rearrange("p (t n) -> p t n", t=NT)
        kvc = wr.rearrange("p k n -> p (k n)")[:, 0:512].rearrange("p (t n) -> p t n", t=NT)
        assert at[0] <= 5200
        f1f = T1.rearrange("p h c n -> p (h c n)")
        kT2, kcT2, qT2 = f1f[:, 0:256], f1f[:, 256:512], f1f[:, 512:768]
        qn2 = f1f[:, 768:1024].rearrange("p (t h d) -> p t h d", t=2, h=2)
        L2 = ctx_in.rearrange("p t d -> p (t d)").rearrange("p (a n) -> p a n", a=4)
        PT2 = xnf.rearrange("p (a n) -> p a n", a=4)
        ctxT = hT
        sinkB = small[:, 186:194]
        nM2, mc2, s1, s2, se = (small[:, 196 + 4 * n:200 + 4 * n] for n in range(5))
        cexc, cssc = small[:, 216:218], small[:, 218:220]
        AcolC, BcolC = small[:, 220:228], small[:, 228:236]
        warm = small[:, 236:237]
        rs1 = small[:, 240:244]
        gs = arena[:, 0:1024].rearrange("p (b n) -> p b n", b=4)
        hid = arena[:, 1024:2048].rearrange("p (b n) -> p b n", b=4)
        gL = arenaR[:, 1024:2048].rearrange("p (b n) -> p b n", b=4)
        gH = arenaR[:, 2048:3072].rearrange("p (b n) -> p b n", b=4)
        hH, hL = mixTR, hTR
        rowB = arena[:, 3072:3072 + D]
        poolw = arena[:, 4096:4096 + 2048].rearrange("p (k n) -> p k n", k=KD)
        slot = lambda n, r=ring: r[:, (RMO + n) % NS, :]
        w13, w13L = ((slot(2, r), slot(0, r)) for r in (ring, ringR))
        w13H = (slot(-2, ringR), slot(-1, ringR))
        w2, w2L = ((slot(3, r)[:, 0:2 * D], slot(1, r)[:, 0:2 * D]) for r in (ring, ringR))
        w2H = (slot(3, ringR)[:, 2 * D:4 * D], slot(1, ringR)[:, 2 * D:4 * D])

        def CB(n):
            return conb[:, CONB[n][0]:CONB[n][1]]

        loaded = [sem(f"ring_loaded{s}") for s in range(NS)]
        ring_used = sem("ring_used")
        con_in, x_in, bias_in, bias2_in, tab_in, misc_in, btab_out, out_done = map(
            sem, ["con_in", "x_in", "bias_in", "bias2_in", "tab_in", "misc_in", "btab_out", "out_done"])
        zeroed, cond_ready = sem("zeroed"), sem("cond_ready")
        chainD, chainD2, chainA = sem("chain_dve"), sem("chain_dve2"), sem("chain_act")
        ada_ev, col_tr, col_ev = map(sem, ["ada_ev", "col_tr", "col_ev"])
        nrm_sq, nrm_xn, nrm_tr, nrm_hT = map(sem, ["nrm_sq", "nrm_xn", "nrm_tr", "nrm_hT"])
        x_new, mod_ready = sem("x_new"), sem("mod_ready")
        win_act, win_dve = map(sem, ["win_act", "win_dve"])
        cv_sq, cv_sum, cv_sd, cv_y, cv_mix = map(sem, ["cv_sq", "cv_sum", "cv_sd", "cv_y", "cv_mix"])
        blk_ready, hid_act, hidT_tr, hidT_ev, kc_mm, kc_ss, kc_sd, kc_n, kc_tr, kc_ready = map(
            sem, ["blk_ready", "hid_act", "hidT_tr", "hidT_ev", "kc_mm", "kc_ss", "kc_sd", "kc_n", "kc_tr",
                  "kc_ready"])
        tabr_mm, tabr_ev = sem("tabr_mm"), sem("tabr_ev")
        qk_ss, qk_sd, k_n, k_tr, k_ready = map(sem, ["qk_ss", "qk_sd", "k_n", "k_tr", "k_ready"])
        q_normed = sem("q_normed")
        a_qn, a_qtr, a_qT, a_s, a_w, a_M, a_E, a_T, a_P, a_O, a_done = map(
            sem, ["a_qn", "a_qtr", "a_qT", "a_s", "a_w", "a_M", "a_E", "a_T", "a_P", "a_O", "a_done"])
        at_ss, at_sd, at_n, at_tr, at_mix = map(sem, ["at_ss", "at_sd", "at_n", "at_tr", "at_mix"])
        g_mm, g_ev = sem("g_mm"), sem("g_ev")

        lg_mm, lg_gx, lg_ex, lg_mask, lg_rank, h2_tr, h2_ev, ov_ready, acc_zero = map(
            sem, ["lg_mm", "lg_gx", "lg_ex", "lg_mask", "lg_rank", "h2_tr", "h2_ev", "ov_ready", "acc_zero"])

        block2_in, context_in, row_in = sem("block2_in"), sem("context_in"), sem("row_in")
        cx_mod, cx_sd, cx_n, cx_tr, cx_T, cx_kv = map(sem, ["cx_mod", "cx_sd", "cx_n", "cx_tr", "cx_T", "cx_kv"])
        m_ev, rope_q, rope_k, kt2_tr, kt2_ev, f_T1, f_T1ev, f_y, f_yev = map(
            sem, ["m_ev", "rope_q", "rope_k", "kt2_tr", "kt2_ev", "f_T1", "f_T1ev", "f_y", "f_yev"])
        b_qn, b_qtr, b_qT, b_s, b_M, b_E, b_T, b_P, b_O, b_done, at2_tr, at2_mix = map(
            sem, ["b_qn", "b_qtr", "b_qT", "b_s", "b_M", "b_E", "b_T", "b_P", "b_O", "b_done", "at2_tr", "at2_mix"])
        f_h, f_s, f_g, f_out, h_split, w13_split, w2_split = map(
            sem, ["f_h", "f_s", "f_g", "f_out", "h_split", "w13_split", "w2_split"])
        w13_in, w2_in = ([sem(f"{n}_in{s}") for s in range(2)] for n in ("w13", "w2"))
        pool_in = sem("pool_in")
        p_tr, p_T, p_y = sem("p_tr"), sem("p_T"), sem("p_y")

        class Signals:

            def __init__(self, name):
                (self.sel, self.tok, self.tokT, self.h1, self.h3, self.silu, self.hid, self.tr, self.trT, self.y, self.yc,
                 self.out) = (sem(f"{name}_{n}") for n in ("sel", "tok", "tokT", "h1", "h3", "silu", "hid", "tr", "trT",
                                                           "y", "yc", "out"))

        first, later = Signals("first"), Signals("later")
        ov_loaded = [sem(f"ov_loaded{s}") for s in range(NS)]
        ov_used = sem("ov_used")
        first.loaded, first.used = loaded, ring_used
        later.loaded, later.used = ov_loaded, ov_used

        def chunk_slot(n):
            return ring[:, n % NS, :]

        def done(eng, n, i=None):
            eng.wait_ge(ring_used, NS + n + 1 if i is None else i * NS + (NS + n + 1))

        def ring_view(n, k):
            return chunk_slot(n).rearrange("p (k n) -> p k n", k=k)

        block = ctx.enter_context(nc.Block())

        @block.sync
        def _(sp):
            def load(n, src, k, w, i=None, per=NS):
                sp.wait_ge(ring_used, n + 1 if i is None else i * per + (n + 1))
                dst = chunk_slot(n)[:, 0:k * w].rearrange("p (k n) -> p k n", k=k)
                sp.dma_start(dst, src).then_inc(loaded[n % NS], 16)

            rows = lambda w: w.rearrange("(k p) n -> p k n", p=P)
            sp.dma_start(con[:, :], A["con"]).then_inc(con_in, 16)
            sp.dma_start(vec[:, :], A["vec"]).then_inc(con_in, 16)
            sp.dma_start(x[:, :, :], A["x"].rearrange("(t p) d -> p t d", p=P)).then_inc(x_in, 16)
            wa = rows(A["w_ada"])
            wi = rows(A["w_in"])
            cuts = (0, 512, 1024, 1304, 1816, 2328, 2840)
            front = {n: (wa[:, :, c * 512:(c + 1) * 512], KD, 512) for c, n in enumerate(RA)}
            front.update({n: (wi[:, :, cuts[c]:cuts[c + 1]], KD, cuts[c + 1] - cuts[c]) for c, n in enumerate(RW)})
            front.update({RC: (rows(A["cmp_k_w1"]), LPAIRS, CMP_HID), RC + 1: (rows(A["cmp_v_w1"]), LPAIRS, CMP_HID)})
            for n in range(RL0):
                load(n, *front[n])
            wa2 = rows(A["ada_w_2"])

            def ada_loads(l, n):
                with sp.Fori(0, 2) as i:
                    for s in range(NS):
                        load(n + s, wa2[:, :, bass.ds(i * (NS * 512) + (l * 12 + s) * 512, 512)], KD, 512, i)

            ada_loads(0, RL0)
            wo = rows(A["w_out"])
            for c in range(2):
                load(RO + c, wo[:, :, c * 512:(c + 1) * 512], KD, 512)
            mi = rows(A["mix_in"])
            load(RK, mi[:, :, 1024:1280], KD, 256)

            def expert_loads(S, pair, i):
                for j, (w, k) in enumerate((("w1", KD), ("w3", KD), ("w2", FE // P))):
                    for u in range(2):
                        n = 2 * j + u
                        sp.wait_ge(S.used, i * NS + (n + 1 + (RE if S is first else 0)))
                        src = A[w][bass.ds(pair[u], 1)].rearrange("e (k p) n -> p (e k) n", p=P)
                        dst = chunk_slot(RE + n).rearrange("p (k n) -> p k n", k=k)
                        sp.dma_start(dst, src).then_inc(S.loaded[(RE + n) % NS], 16)

            with sp.Fori(0, E // 2) as i:
                expert_loads(first, (i * 2, i * 2 + 1), i)
            sp.wait_ge(ov_ready, 1)
            nov = sp.value_load(ovi[0:1, OVR:OVR + 1], min_val=0, max_val=NOV)
            with sp.If(nov > 0):
                sp.wait_ge(ring_used, NS + RE + 3 * E)
                with sp.Fori(0, OVR // 2) as i:
                    pair = [sp.value_load(ovi[0:1, bass.ds(i * 2 + u, 1)], min_val=0, max_val=E - 1) for u in range(2)]
                    expert_loads(later, pair, i)
                sp.wait_ge(ov_used, NS + 3 * OVR)
            sp.end_ifs()
            for c in range(3):
                w = min(512, 1280 - c * 512)
                load(RM + c, mi[:, :, c * 512:c * 512 + w], KD, w)
            ada_loads(1, RL1)
            mo = rows(A["mix_out"])
            for c in range(2):
                load(RMO + c, mo[:, :, c * 512:(c + 1) * 512], KD, 512)

            def ffn_step(l, c, i=None):
                g = NF * l + c
                s, v = g % 2, 16 * (g // 2 + 1)
                if g < 2:
                    sp.wait_ge(ring_used, NS + (RMO - 3, RMO + 1)[g])
                else:
                    sp.wait_ge(f_h, 2 * g - 2 if i is None else i * 4 + (2 * g - 2))
                f13 = rows(A["f13"][l])
                f2 = A["f2"][l].rearrange("(k p) n -> p k n", p=P)
                sp.dma_start(w13[s].rearrange("p (k n) -> p k n", k=KD),
                             f13[:, :, c * 512:(c + 1) * 512] if i is None else
                             f13[:, :, bass.ds(i * 1024 + c * 512, 512)]).then_inc(w13_in[s], 16)
                if g < 2:
                    sp.wait_ge(ring_used, NS + (RMO - 2, RMO + 2)[g])
                else:
                    sp.wait_ge(f_out, g - 1 if i is None else i * 2 + (g - 1))
                sp.dma_start(w2[s].rearrange("p (k n) -> p k n", k=2),
                             f2[:, 2 * c:2 * c + 2, :] if i is None else
                             f2[:, bass.ds(i * 4 + 2 * c, 2), :]).then_inc(w2_in[s], 16)

            for l in range(2):
                for c in range(3):
                    ffn_step(l, c)
                if l == 0:
                    sp.dma_start(poolw, rows(A["pool_w"])).then_inc(pool_in, 16)
                with sp.Fori(0, (NF - 3) // 2) as i:
                    for c in (3, 4):
                        ffn_step(l, c, i)
            for t in range(NT):
                sp.wait_ge(x_new, 6 * NT + t + 1)
                sp.dma_start(out[0, t * P:(t + 1) * P, :], xn[:, t, :]).then_inc(out_done, 16)
            sp.wait_ge(out_done, 16 * NT)
        @block.gpsimd
        def _(pool):
            nc.gpsimd.memset(modrow[:, 0:1536], 0.0).then_inc(zeroed, 1)
            nc.gpsimd.memset(cond[:, :, :, :], 0.0).then_inc(zeroed, 1)
            nc.gpsimd.memset(vT[:, :, 0:2], 0.0).then_inc(zeroed, 1)
            nc.gpsimd.memset(epsc, EPS).then_inc(zeroed, 1)
            nc.gpsimd.memset(vc, 0.0).then_inc(zeroed, 1)
            nc.gpsimd.memset(modrow[:, 1536:4608], 0.0).then_inc(zeroed, 1)

        @block.scalar
        def _(act):
            link = Chain(act, chainA)
            act.dma_start(relb[:, :], A["rel_bias"]).then_inc(tab_in, 16)
            act.dma_start(oh[:, :], A["oh"]).then_inc(tab_in, 16)
            act.wait_ge(zeroed, 1)
            act.dma_start(modrow[0:P:32, 0:1536], A["adab"][0]).then_inc(bias_in, 16)
            act.wait_ge(con_in, 32)
            act.wait_ge(zeroed, 2)
            nc.scalar.activation(cond[:, 0, :, 0], V("c"), ACT.Silu)
            nc.scalar.activation(cond[:, 1, :, 0], V("c2"), ACT.Silu)
            nc.scalar.activation(cond[:, 1, :, 1], V("cctx"), ACT.Silu).then_inc(cond_ready, 1)

            def norm(u, ready):
                if u == 0:
                    act.wait_ge(zeroed, 4)
                nc.scalar.activation(warm, epsc, ACT.Sqrt)
                for t in range(NT):
                    act.wait_ge(*ready(t))
                    link(nc.scalar.activation(xn[:, t, :], x[:, t, :], ACT.Square, accum_out=ss[:, t:t + 1]))
                    nc.scalar.activation(sd2[:, t:t + 1], ss[:, t:t + 1], ACT.Sqrt, scale=1.0 / D, bias=epsc
                                         ).then_inc(nrm_sq, 1)

            def after(n):
                return lambda t: (x_new, NT * (n - 1) + t + 1)

            def norm_out(u, b0):
                act.wait_ge(nrm_tr, u + 1)
                act.wait_ge(mod_ready, u + 1 + (u > 3))
                for k in range(KD // 2, KD):
                    last = nc.scalar.activation(hT[:, k, :], ps[:, b0 + k // 2, (k % 2) * T:(k % 2 + 1) * T], ACT.Identity,
                                                scale=Acol[:, k:k + 1], bias=Bcol[:, k:k + 1])
                last.then_inc(nrm_hT, 1)

            norm(0, lambda t: (x_in, 16))
            for h in range(NH):
                act.wait_ge(tabr_mm, h + 1)
                nc.scalar.activation(tabrow[:, h, :], ps[:, h, 0:384], ACT.Copy).then_inc(tabr_ev, 1)
            act.wait_ge(tabr_ev, NH)
            act.dma_start(btab.rearrange("h (p n) -> p h n", p=P), tabrow).then_inc(btab_out, 16)
            norm_out(0, 4)
            act.wait_ge(btab_out, 16)
            for h in range(NH):
                src = btab[h, 127:127 + P * 383].rearrange("(p w) -> p w", w=383)[:, 0:256]
                act.dma_start(tab[:, h, 0:256], src).then_inc(tab_in, 16)

            act.dma_start(cw2[:, 0, :, :], A["cmp_k_w2"].rearrange("(j p) n -> p j n", p=P)).then_inc(misc_in, 16)
            act.dma_start(cw2[:, 1, :, :], A["cmp_v_w2"].rearrange("(j p) n -> p j n", p=P)).then_inc(misc_in, 16)
            act.dma_start(wr[:, :, :], A["wr"].rearrange("(k p) n -> p k n", p=P)).then_inc(misc_in, 16)
            act.dma_start(brB[:, :], A["br"].partition_broadcast(P)).then_inc(misc_in, 16)
            act.wait_ge(zeroed, 6)
            for l in range(1, 3):
                act.dma_start(modrow[0:P:32, l * 1536:(l + 1) * 1536], A["adab"][l]).then_inc(bias2_in, 16)
            act.dma_start(modrow[1:P:32, 1536:3072], A["adab"][1]).then_inc(bias2_in, 16)
            done(act, RW[0])
            for t in range(NT):
                last = nc.scalar.activation(q[:, t, :], ps[:, t, :], ACT.Copy)
            last.then_inc(win_act, 1)
            done(act, RW[1])
            nc.scalar.activation(ksv, ps[:, 3, :].rearrange("p (t n) -> p t n", t=NT), ACT.Copy).then_inc(win_act, 1)
            done(act, RW[2])
            for t in range(NT):
                last = nc.scalar.activation(kwg[:, t, :], ps[:, 4 + t, 0:280], ACT.Copy)
            link(last)
            for t in range(NT):
                last = nc.scalar.activation(
                    G3[:, :, :, 1 - t], kwg[:, t, 256:280].rearrange("p (h b) -> p h b", b=3), ACT.Sigmoid)
            last.then_inc(win_act, 1)
            done(act, RW[3])
            nc.scalar.activation(bT, ps[:, 6:8, :].rearrange("p b (f t) -> p (b f) t", f=2), ACT.Copy).then_inc(win_act, 1)
            done(act, RW[4])
            nc.scalar.activation(cT, ps[:, 0:2, :].rearrange("p b (f t) -> p (b f) t", f=2), ACT.Copy).then_inc(win_act, 1)
            act.wait_ge(qk_ss, 1)
            nc.scalar.activation(sd24, SS, ACT.Sqrt, scale=1.0 / HD, bias=epsc).then_inc(qk_sd, 1)
            act.wait_ge(cv_y, 1)
            nc.scalar.activation(sq.rearrange("p (f t) -> p f t", f=4), cT, ACT.Square).then_inc(cv_sq, 1)
            act.wait_ge(cv_sum, 1)
            nc.scalar.activation(sq, ps[:, 0:2, :].rearrange("p b n -> p (b n)"), ACT.Sqrt, scale=1.0 / HD,
                                 bias=epsc).then_inc(cv_sd, 1)
            done(act, RC + 1)
            nc.scalar.activation(hidS[0:30, :], ps[0:30, 4, :], ACT.Silu).then_inc(hid_act, 1)
            act.wait_ge(kc_ss, 1)
            nc.scalar.activation(sd24[0:NC, 0:2], SS[0:NC, 0:2], ACT.Sqrt, scale=1.0 / HD,
                                 bias=epsc[0:NC]).then_inc(kc_sd, 1)

            q5 = q.rearrange("p t (h i d) -> p t h i d", h=2, d=HD)

            def queries(i, u):
                if u:
                    act.wait_ge(a_qtr, i * 2 + 1)
                one = bass.ds(i * 2 + u, 1)
                nc.scalar.activation(qn, q5[:, :, :, one, :].rearrange("p t h i d -> p t h (i d)"), ACT.Copy
                                     ).then_inc(a_qn, 1)

            act.wait_ge(q_normed, 1)
            with act.Fori(0, PAIRS // 2) as i:
                queries(i, 0)
                queries(i, 1)
                for u in range(2):
                    act.wait_ge(a_M, i * 2 + (u + 1))
                    for a in range(4):
                        h, b = a % 2, 1 + a // 2
                        for ii, (lo, hi) in enumerate([(0, 256), (256, 384)]):
                            nc.scalar.activation(L[:, a, lo:hi], L[:, a, lo:hi], ACT.Exp, bias=nM[:, h, b, ii:ii + 1],
                                                 accum_out=SM[:, h, b, ii:ii + 1])
                    for h in range(2):
                        for ii, lo in enumerate([C1, C0]):
                            last = nc.scalar.activation(L[:, h, lo:lo + NC], L[:, h, lo:lo + NC], ACT.Exp,
                                                        bias=nM[:, h, 0, ii:ii + 1], accum_out=SM[:, h, 0, ii:ii + 1])
                    last.then_inc(a_E, 1)
                    act.wait_ge(a_T, i * 4 + (2 * u + 2))
                    nc.scalar.activation(PTw, ps[:, 4:6, 0:384], ACT.Copy).then_inc(a_P, 1)
            act.wait_ge(a_done, PAIRS)
            act.dma_start(ctx_in, A["ctx"].rearrange("(t p) d -> p t d", p=P)).then_inc(context_in, 16)
            act.wait_ge(at_ss, 1)
            nc.scalar.activation(sd24[:, 0:16], SS[:, 0:16], ACT.Sqrt, scale=1.0 / HD, bias=epsc).then_inc(at_sd, 1)
            act.wait_ge(g_mm, 1)
            nc.scalar.activation(gB[:, :], ps[:, 0:2, :].rearrange("p b n -> p (b n)"), ACT.Copy).then_inc(g_ev, 1)

            act.wait_ge(at_mix, 1)
            act.dma_start(conb, A["conb"]).then_inc(block2_in, 16)
            act.dma_start(sinkB, A["sink"].partition_broadcast(P)).then_inc(block2_in, 16)
            act.wait_ge(context_in, 16)
            for t in range(NT):
                last = nc.scalar.activation(xnf[:, 1024:2048], ctx_in[:, t, :], ACT.Square, accum_out=cssc[:, t:t + 1])
                link(last)
            nc.scalar.activation(cexc, cssc, ACT.Sqrt, scale=1.0 / D, bias=epsc).then_inc(cx_sd, 1)
            act.wait_ge(cx_tr, 1)
            act.wait_ge(cx_mod, 1)
            for k in range(KD):
                last = nc.scalar.activation(ctxT[:, k, :], ps[:, k // 2, (k % 2) * T:(k % 2 + 1) * T], ACT.Identity,
                                            scale=AcolC[:, k:k + 1], bias=BcolC[:, k:k + 1])
            last.then_inc(cx_T, 1)
            norm(1, after(1))
            act.wait_ge(g_mm, 2)
            nc.scalar.activation(gB[:, :], ps[:, 2:4, :].rearrange("p b n -> p (b n)"), ACT.Copy).then_inc(g_ev, 1)
            norm_out(1, 4)
            act.wait_ge(lg_mm, 1)
            nc.scalar.activation(kvc.rearrange("p t n -> p (t n)"), ps[:, 1, :], ACT.Copy).then_inc(cx_kv, 1)
            act.wait_ge(lg_gx, 1)
            nc.scalar.activation(r8[1], r8[0], ACT.Exp).then_inc(lg_ex, 1)
            act.wait_ge(h2_tr, 1)
            for t in range(NT):
                last = nc.scalar.activation(xn[:, t, :], ps[:, 4 + 2 * t:6 + 2 * t, :].rearrange("p b n -> p (b n)"),
                                            ACT.Copy)
            last.then_inc(h2_ev, 1)
            act.wait_ge(lg_gx, 2)
            nc.scalar.activation(r1[4], r1[3], ACT.Exp).then_inc(lg_ex, 1)

            def expert_pair(S, i):
                act.wait_ge(S.h1, i + 1)
                nc.scalar.activation(gsil, ps[:, 0, :], ACT.Silu).then_inc(S.silu, 1)
                act.wait_ge(S.y, i + 1)
                nc.scalar.activation(Ye, ps[:, 0:2, :].rearrange("p b n -> p (b n)"), ACT.Copy).then_inc(S.yc, 1)

            with act.Fori(0, E // 2) as i:
                expert_pair(first, i)
            act.wait_ge(ov_ready, 1)
            nov = act.value_load(ovi[0:1, OVR:OVR + 1], min_val=0, max_val=NOV)
            with act.If(nov > 0):
                with act.Fori(0, OVR // 2) as i:
                    expert_pair(later, i)
            act.end_ifs()
            flat = lambda a, b: ps[:, a:b, :].rearrange("p b n -> p (b n)")
            norm(2, after(2))
            norm_out(2, 4)
            done(act, RM)
            nc.scalar.activation(u2.rearrange("p t n -> p (t n)"), flat(4, 6), ACT.Copy).then_inc(m_ev, 1)
            done(act, RM + 1)
            nc.scalar.activation(q2.rearrange("p t n -> p (t n)"), flat(6, 8), ACT.Copy).then_inc(m_ev, 1)
            done(act, RM + 2)
            nc.scalar.activation(kv2.rearrange("p t n -> p (t n)"), ps[:, 0, :], ACT.Copy).then_inc(m_ev, 1)
            act.wait_ge(f_T1, 1)
            nc.scalar.activation(f1f, flat(4, 8), ACT.Copy).then_inc(f_T1ev, 1)
            act.wait_ge(f_y, 1)
            nc.scalar.activation(mixT[:, 0:4, :].rearrange("p k t -> p (k t)"), flat(0, 2), ACT.Copy).then_inc(f_yev, 1)
            q52 = q2.rearrange("p t (h i d) -> p t h i d", h=2, d=HD)

            def queries2(i, u):
                if u:
                    act.wait_ge(b_qtr, i * 2 + 1)
                one = bass.ds(i * 2 + u, 1)
                nc.scalar.activation(qn2, q52[:, :, :, one, :].rearrange("p t h i d -> p t h (i d)"), ACT.Copy,
                                     scale=SCALE).then_inc(b_qn, 1)

            act.wait_ge(rope_q, 1)
            act.wait_ge(f_y, 1)
            with act.Fori(0, PAIRS // 2) as i:
                queries2(i, 0)
                queries2(i, 1)
                for u in range(2):
                    act.wait_ge(b_M, i * 2 + (u + 1))
                    nc.scalar.activation(se, se, ACT.Exp)
                    for a in range(4):
                        nc.scalar.activation(L2[:, a, 0:256], L2[:, a, 0:256], ACT.Exp, bias=nM2[:, a:a + 1],
                                             accum_out=s1[:, a:a + 1])
                        last = nc.scalar.activation(L2[:, a, 256:512], ps[:, a, 256:512], ACT.Exp, bias=nM2[:, a:a + 1],
                                                    accum_out=s2[:, a:a + 1])
                    last.then_inc(b_E, 1)
                    act.wait_ge(b_T, i * 2 + (u + 1))
                    nc.scalar.activation(PT2[:, 0:2, :], ps[:, 0:2, :], ACT.Copy).then_inc(b_P, 1)

            def gate(n, b0):
                act.wait_ge(g_mm, n)
                nc.scalar.activation(gB[:, :], flat(b0, b0 + 2), ACT.Copy).then_inc(g_ev, 1)

            def ffn_step(l, c, i=None):
                for f in range(2):
                    n = 2 * (NF * l + c) + f + 1
                    b = (n - 1) % 4
                    act.wait_ge(f_h, n if i is None else i * 4 + n)
                    nc.scalar.activation(gs[:, b, :], ps[:, b, 0:256], ACT.Silu).then_inc(f_s, 1)

            def ffn(l):
                ffn_step(l, 0)
                with act.Fori(0, (NF - 1) // 2) as i:
                    for c in (1, 2):
                        ffn_step(l, c, i)

            gate(3, 2)
            norm(3, after(3))
            gate(4, 2)
            norm_out(3, 4)
            act.dma_start(rowB, A["pscale"].partition_broadcast(P)).then_inc(row_in, 16)
            ffn(0)
            norm(4, after(4))
            gate(5, 2)
            act.wait_ge(p_tr, 1)
            act.wait_ge(mod_ready, 5)
            for k in range(KD // 2, KD):
                last = nc.scalar.activation(hT[:, k, :], ps[:, 4 + k // 2, (k % 2) * T:(k % 2 + 1) * T], ACT.Copy,
                                            scale=Acol[:, k:k + 1])
            last.then_inc(p_T, 1)
            norm(5, after(5))
            act.dma_start(rowB, A["final_g"].partition_broadcast(P)).then_inc(row_in, 16)
            gate(6, 2)
            norm_out(4, 4)
            ffn(1)
            norm(6, after(6))

        @block.vector
        def _(dve):
            link = Chain(dve, chainD)
            tt, ts, stt = nc.vector.tensor_tensor, nc.vector.tensor_scalar, nc.vector.scalar_tensor_tensor

            def modulation(src, w):
                stt(Acol, src[:, 8:16], 1.0, w, ALU.add, ALU.mult)
                nc.vector.tensor_copy(Bcol, src[:, 0:8]).then_inc(mod_ready, 1)

            def norm(u):
                for t in range(NT):
                    dve.wait_ge(nrm_sq, NT * u + t + 1)
                    link(nc.vector.reciprocal(rstd[:, t:t + 1], sd2[:, t:t + 1]))
                    ts(xn[:, t, :], x[:, t, :], rstd[:, t:t + 1], None, ALU.mult).then_inc(nrm_xn, 1)

            def norm_out(u, b0):
                dve.wait_ge(nrm_tr, u + 1)
                dve.wait_ge(mod_ready, u + 1 + (u > 3))
                for k in range(KD // 2):
                    last = ts(hT[:, k, :], ps[:, b0 + k // 2, (k % 2) * T:(k % 2 + 1) * T], Acol[:, k:k + 1],
                              Bcol[:, k:k + 1], ALU.mult, ALU.add)
                last.then_inc(nrm_hT, 1)

            def columns(l, a, b, bank, n):
                dve.wait_ge(col_tr, n)
                v = ps[:, bank:bank + (b - a) // 4, :].rearrange("p b (c n) -> p (b c) n", n=P)
                last = nc.vector.tensor_copy(modcol[:, l, 4 * a:4 * b].rearrange("p (c j) -> p c j", j=4), v[:, :, 0:P:32])
                if l == 1:
                    last = nc.vector.tensor_copy(ctxcol[:, :].rearrange("p (c j) -> p c j", j=4), v[:, 0:4, 1:P:32])
                last.then_inc(col_ev, 1)

            def ada_round(r, bank):
                done(dve, RA[4 * r + 3])
                m = modrow[:, r * 512:(r + 1) * 512]
                tt(m, ps[:, bank, :], m, ALU.add).then_inc(ada_ev, 1)

            norm(0)
            dve.wait_ge(bias_in, 16)
            ada_round(0, 0)
            columns(0, 0, 4, 2, 1)
            dve.wait_ge(col_ev, 1)
            modulation(modcol[:, 0, :], V("norm1"))
            norm_out(0, 4)

            done(dve, RW[1])
            for v in range(2):
                for g in range(2):
                    src = ps[64 * g:64 * g + 64, 2, v * T:(v + 1) * T]
                    nc.vector.tensor_copy(kvT2[0:64, v, g, :], src)
                    last = nc.vector.tensor_copy(kvT2[64:128, v, g, 0:T - 1], src[:, 1:T])
            last.then_inc(win_dve, 1)
            dve.wait_ge(win_dve, 1)
            for v in range(2):
                pos = V("posk" if v == 0 else "posv")
                for g in range(2):
                    for half in range(2):
                        src = kvT2[:, v, g, 16 * half:16 * half + 240].rearrange("p (n m) -> p m n", m=16)[:, 0:16:2, :]
                        last = tt(blk[:, v, 8 * half:8 * half + 8, g, :], src,
                                  pos[:, 8 * half:8 * half + 8].unsqueeze(2).to_broadcast([P, 8, NC]), ALU.add)
            last.then_inc(blk_ready, 1)

            dve.wait_ge(win_act, 3)
            qh = q.rearrange("p t (h d) -> p (t h) d", d=HD)
            sq3 = sq.rearrange("p (h d) -> p h d", d=HD)
            link(tt(sq3, qh, qh, ALU.mult))
            link(nc.vector.tensor_reduce(SS[:, 0:16], sq3, AX.X, ALU.add))
            for n, kk in enumerate((ksv, kwg)):
                k4 = kk[:, :, 0:P]
                s4 = sq[:, 0:256].rearrange("p (t n) -> p t n", t=2)
                link(tt(s4, k4, k4, ALU.mult))
                link(nc.vector.tensor_reduce(SS[:, 16 + 4 * n:20 + 4 * n], sq3[:, 0:4, :], AX.X, ALU.add))
            dve.sem_inc(qk_ss, 1)
            dve.wait_ge(qk_sd, 1)
            link(nc.vector.reciprocal(RS, sd24))
            for n, kk in enumerate((ksv, kwg)):
                for t in range(NT):
                    k3 = kk[:, t, 0:P].rearrange("p (g d) -> p g d", g=2)
                    r = RS[:, 16 + 4 * n + 2 * t:18 + 4 * n + 2 * t].unsqueeze(2).to_broadcast([P, 2, HD])
                    last = tt(k3, k3, r, ALU.mult)
            last.then_inc(k_n, 1)
            tt(qh, qh, RS[:, 0:16].unsqueeze(2).to_broadcast([P, 16, HD]), ALU.mult).then_inc(q_normed, 1)
            ada_round(1, 4)

            done(dve, RW[5])
            dve.wait_ge(win_act, 5)
            dve.wait_ge(zeroed, 3)
            link(tt(vT[:, :, 2:258], ps[:, 2:4, :].rearrange("p b (f t) -> p (b f) t", f=2), cT, ALU.mult))
            cw = V("conv").rearrange("p (j f) -> p j f", j=3)
            for f in range(4):
                last = ts(cT[:, f, :], vT[:, f, 2:258], cw[:, 2, f:f + 1], None, ALU.mult)
            link(last)
            for j in (1, 0):
                for f in range(4):
                    last = stt(cT[:, f, :], vT[:, f, j:j + T], cw[:, j, f:f + 1], cT[:, f, :], ALU.mult, ALU.add)
                link(last)
            tt(cT, cT, bT, ALU.mult).then_inc(cv_y, 1)
            dve.wait_ge(k_tr, 1)
            kn = V("kn")
            ts(kTs, ps[:, 7, 0:256], kn[:, 1:2], None, ALU.mult)
            ts(kTw, ps[:, 7, 256:512], kn[:, 2:3], None, ALU.mult).then_inc(k_ready, 1)
            dve.wait_ge(cv_sd, 1)
            link(nc.vector.reciprocal(sq, sq))
            for f in range(4):
                last = stt(mixT[:, 4 + f, :], cT[:, f, :], V("outn")[:, 4 + f:5 + f], sq[:, f * T:(f + 1) * T], ALU.mult,
                           ALU.mult)
            last.then_inc(cv_mix, 1)
            dve.wait_ge(hidT_tr, 1)
            nc.vector.tensor_copy(hidT[:, :, 0:30], ps[:, 6, 384:512].rearrange("p (v n) -> p v n", v=4)[:, :, 0:30]
                                  ).then_inc(hidT_ev, 1)
            dve.wait_ge(kc_mm, 1)
            kc = ps[0:NC, 6, 0:128]
            dve.wait_ge(zeroed, 5)
            nc.vector.tensor_copy(vc[0:NC, 0, :, :], ps[0:NC, 6, 128:256].rearrange("p (g d) -> p g d", g=2))
            nc.vector.tensor_copy(vc[32:32 + NC, 1, :, :], ps[32:32 + NC, 6, 128:256].rearrange("p (g d) -> p g d", g=2))
            link(nc.vector.tensor_copy(kcn[0:NC, :], kc))
            link(tt(hidS[0:NC, 0:128], kcn[0:NC, :], kcn[0:NC, :], ALU.mult))
            nc.vector.tensor_reduce(SS[0:NC, 0:2], hidS[0:NC, 0:128].rearrange("p (g d) -> p g d", g=2), AX.X,
                                    ALU.add).then_inc(kc_ss, 1)
            dve.wait_ge(kc_sd, 1)
            link(nc.vector.reciprocal(sd24[0:NC, 2:4], sd24[0:NC, 0:2]))
            tt(kcn[0:NC, :].rearrange("p (g d) -> p g d", g=2), kcn[0:NC, :].rearrange("p (g d) -> p g d", g=2),
               sd24[0:NC, 2:4].unsqueeze(2).to_broadcast([NC, 2, HD]), ALU.mult).then_inc(kc_n, 1)
            ada_round(2, 5)
            dve.wait_ge(kc_tr, 1)
            ts(kcT[:, 0:NC], ps[:, 6, 256:256 + NC], kn[:, 0:1], None, ALU.mult).then_inc(kc_ready, 1)
            dve.wait_ge(tab_in, 32 + 16 * NH)
            link(tt(tab[:, :, 0:256], tab[:, :, 0:256], C("cmask").unsqueeze(1).to_broadcast([P, NH, 256]), ALU.add))
            nc.vector.tensor_copy(tab[:, :, 256:384], tab[:, :, 128:256])
            nc.vector.memset(tab[:, :, C0 + 7:C0 + NC], NEG)
            nc.vector.tensor_copy(tab[:, :, C0:C0 + 7], tab[:, :, 159:256:16])
            nc.vector.memset(L[:, 0:2, C1 + NC:C0], 0.0)
            link(nc.vector.tensor_copy(tab[:, :, C1:C1 + NC], tab[:, :, 31:256:16]))

            tab4 = tab.rearrange("p (h i) n -> p h i n", h=2)
            G4 = G3.rearrange("p (h i) b j -> p h i (b j)", h=2)
            attn5 = attn.rearrange("p j (h i) d -> p h j i d", h=2)
            COf = CO.rearrange("p h b j -> p h (b j)")
            split = lambda ap: ap.rearrange("p h (j n) -> p h j n", j=2)[:, :, :, 0:NC]

            def logits(i, u):
                dve.wait_ge(a_qtr, i * 2 + (u + 1))
                ts(qT, ps[:, 1, 256:512], V("qn"), SCALE, ALU.mult, ALU.mult).then_inc(a_qT, 1)
                tb = tab4[:, :, bass.ds(i * 2 + u, 1), :].rearrange("p h i n -> p h (i n)")
                dve.wait_ge(a_s, i * 2 + (u + 1))
                tt(L[:, 0:2, 0:384], ps[:, 2:4, 0:384], tb[:, :, 0:384], ALU.add)
                tt(split(L[:, 0:2, C1:TABW]), split(ps[:, 2:4, C1:TABW]), split(tb[:, :, C1:TABW]), ALU.add)
                dve.wait_ge(a_w, i * 2 + (u + 1))
                link(tt(L[:, 2:4, 0:384], ps[:, 4:6, 0:384], tb[:, :, 0:384], ALU.add))
                Lb = L.rearrange("p (b h) n -> p h b n", b=2)
                nc.vector.tensor_reduce(nM[:, :, 1:3, 0], Lb[:, :, :, 0:256], AX.X, ALU.max, negate=True)
                nc.vector.tensor_reduce(nM[:, :, 1:3, 1], Lb[:, :, :, 256:384], AX.X, ALU.max, negate=True)
                link(nc.vector.tensor_reduce(nM[:, :, 0, :], split(L[:, 0:2, C1:TABW]), AX.X, ALU.max, negate=True))
                ts(nM[:, :, 0, :], nM[:, :, 0, :], -0.01 * NEG, None, ALU.min).then_inc(a_M, 1)

            def probabilities(i, u):
                dve.wait_ge(a_E, i * 2 + (u + 1))
                link(ts(CO, SM, 1e-30, None, ALU.max))
                link(nc.vector.reciprocal(CO, CO))
                g = G4[:, :, bass.ds(i * 2 + u, 1), :].rearrange("p h i n -> p h (i n)")
                link(tt(COf, COf, g, ALU.mult))
                dve.wait_ge(a_T, i * 4 + (2 * u + 1))
                nc.vector.tensor_copy(PTs[:, :, 0:384], ps[:, 2:4, 0:384])
                nc.vector.tensor_copy(PTs[0:47, :, 384:512], ps[0:47, 2:4, 384:512]).then_inc(a_P, 1)

            def combined(i, u):
                dve.wait_ge(a_O, i * 2 + (u + 1))
                link(tt(Ot.rearrange("p h b j d -> p h (b j) d"), ps[:, 6:8, 0:384].rearrange("p h (c d) -> p h c d", d=HD),
                        COf.unsqueeze(3).to_broadcast([P, 2, 6, HD]), ALU.mult))
                link(tt(Ot[:, :, 0], Ot[:, :, 0], Ot[:, :, 1], ALU.add))
                one = bass.ds(i * 2 + u, 1)
                tt(attn5[:, :, :, one, :].rearrange("p h j i d -> p h j (i d)"), Ot[:, :, 0], Ot[:, :, 2], ALU.add
                   ).then_inc(a_done, 1)

            def ada_sums(l, n, i, bank):
                done(dve, n + NS - 1, i)
                m = modrow[:, bass.ds(i * 768 + l * 1536, 768)]
                tt(m, ps[:, bank:bank + 2, :].rearrange("p b n -> p (b n)")[:, 0:768], m, ALU.add).then_inc(ada_ev, 1)

            dve.wait_ge(bias2_in, 48)
            with dve.Fori(0, PAIRS // 2) as i:
                link.enter(i, 14)
                logits(i, 0)
                probabilities(i, 0)
                logits(i, 1)
                combined(i, 0)
                probabilities(i, 1)
                ada_sums(1, RL0, i, 0)
                combined(i, 1)
            link.leave(PAIRS // 2)
            columns(0, 4, 8, 0, 2)
            columns(1, 0, 8, 2, 3)
            dve.wait_ge(a_done, PAIRS)
            at3 = attn.rearrange("p j h d -> p (j h) d")
            sqa = zone[:, 0:1024].rearrange("p (h d) -> p h d", d=HD)
            link(tt(sqa, at3, at3, ALU.mult))
            nc.vector.tensor_reduce(SS[:, 0:16], sqa, AX.X, ALU.add).then_inc(at_ss, 1)
            dve.wait_ge(at_sd, 1)
            link(nc.vector.reciprocal(RS[:, 0:16], sd24[:, 0:16]))
            tt(at3, at3, RS[:, 0:16].unsqueeze(2).to_broadcast([P, 16, HD]), ALU.mult).then_inc(at_n, 1)
            dve.wait_ge(at_tr, 1)
            for j in range(4):
                last = ts(mixT[:, j, :], ps[:, 2 + j // 2, (j % 2) * T:(j % 2 + 1) * T], V("outn")[:, j:j + 1], None, ALU.mult)
            last.then_inc(at_mix, 1)
            nc.vector.memset(Ye, 0.0).then_inc(acc_zero, 1)
            stt(AcolC, ctxcol[:, 8:16], 1.0, V("nmix0"), ALU.add, ALU.mult)
            nc.vector.tensor_copy(BcolC, ctxcol[:, 0:8]).then_inc(cx_mod, 1)
            dve.wait_ge(cx_sd, 1)
            link(nc.vector.reciprocal(cexc, cexc))
            for t in range(NT):
                last = ts(ctx_in[:, t, :], ctx_in[:, t, :], cexc[:, t:t + 1], None, ALU.mult)
            last.then_inc(cx_n, 1)
            dve.wait_ge(g_ev, 1)
            done(dve, RO + 1)
            y = ps[:, 4:8, :].rearrange("p (t c) n -> p t (c n)", t=NT)
            for t in range(NT):
                link(tt(xn[:, t, :], y[:, t, :], gB[:, :], ALU.mult))
                tt(x[:, t, :], x[:, t, :], xn[:, t, :], ALU.add).then_inc(x_new, 1)

            dve.wait_ge(col_ev, 3)
            modulation(modcol[:, 0, 16:32], V("norm2"))
            norm(1)
            norm_out(1, 4)
            dve.wait_ge(misc_in, 64)
            dve.wait_ge(lg_mm, 1)
            b2 = lambda ap: ap.unsqueeze(2).to_broadcast([P, NT, 8])
            lgg = lg[:, :, 0:8]
            link(tt(lg, ps[:, 0, 0:144].rearrange("p (t e) -> p t e", t=NT),
                    brB[:, :].unsqueeze(1).to_broadcast([P, NT, 72]), ALU.add))
            gmax, gsum, gp, d21, rr, w1c, w2c, mx = r1
            gx, gex, onehot_g, ein, o1, o2, e2, tmp8 = r8
            rev = C("rev").unsqueeze(1).to_broadcast([P, NT, 8])

            def first_max(onehot, v, m):
                link(nc.vector.tensor_reduce(m, v, AX.X, ALU.max))
                link(tt(tmp8, v, b2(m), ALU.is_equal))
                link(tt(tmp8, tmp8, rev, ALU.mult))
                link(nc.vector.tensor_reduce(mx, tmp8, AX.X, ALU.max))
                link(tt(onehot, tmp8, b2(mx), ALU.is_equal))

            link(nc.vector.tensor_reduce(gmax, lgg, AX.X, ALU.max))
            tt(gx, lgg, b2(gmax), ALU.subtract).then_inc(lg_gx, 1)
            first_max(onehot_g, lgg, w2c)
            pv = prod[:, 0:128].rearrange("p (t e g) -> p t e g", t=NT, e=8)
            link(tt(pv, lg[:, :, 8:72].rearrange("p t (g e) -> p t e g", g=8),
                    onehot_g.unsqueeze(2).to_broadcast([P, NT, 8, 8]), ALU.mult))
            link(nc.vector.tensor_reduce(ein, pv, AX.X, ALU.add))
            first_max(o1, ein, w1c)
            link(stt(e2, o1, 2 * NEG, ein, ALU.mult, ALU.add))
            first_max(o2, e2, w2c)
            tt(d21, w2c, w1c, ALU.subtract).then_inc(lg_gx, 1)
            link(tt(tmp8, o1, o2, ALU.add))
            mt = msk.rearrange("p t (g e) -> p t g e", g=8)
            tt(mt, onehot_g.unsqueeze(3).to_broadcast([P, NT, 8, 8]), tmp8.unsqueeze(2).to_broadcast([P, NT, 8, 8]),
               ALU.mult).then_inc(lg_mask, 1)
            dve.wait_ge(lg_ex, 1)
            link(nc.vector.tensor_reduce(gsum, gex, AX.X, ALU.add))
            link(nc.vector.reciprocal(gp, gsum))
            dve.wait_ge(lg_ex, 2)
            link(ts(w1c, rr, 1.0, None, ALU.add))
            link(nc.vector.reciprocal(w1c, w1c))
            link(tt(w1c, w1c, gp, ALU.mult))
            link(tt(w2c, w1c, rr, ALU.mult))
            link(tt(o1, o1, b2(w1c), ALU.mult))
            link(tt(o2, o2, b2(w2c), ALU.mult))
            link(tt(o1, o1, o2, ALU.add))
            nc.vector.memset(gat[:, :, E:ECOL], 0.0)
            nc.vector.memset(rnk[:, :, E:ECOL], 0.0)
            link(tt(gat[:, :, 0:E].rearrange("p t (g e) -> p t g e", g=8),
                    onehot_g.unsqueeze(3).to_broadcast([P, NT, 8, 8]), o1.unsqueeze(2).to_broadcast([P, NT, 8, 8]),
                    ALU.mult))
            dve.wait_ge(lg_rank, 1)
            rk = ps[:, 1, 0:128].rearrange("p (t e) -> p t e", t=NT)
            link(tt(rnk[:, :, 0:E], rk, msk, ALU.mult))

            def select(S, cols):
                four = lambda ap: ap.rearrange("p t (e s) -> p t e s", e=2)
                iota = C("iota").unsqueeze(1).to_broadcast([P, 2, SLOTS])
                bc = lambda ap: ap[:, :, cols].unsqueeze(3).to_broadcast([P, NT, 2, SLOTS])
                for t in range(NT):
                    last = tt(four(Ssel)[:, t], bc(rnk)[:, t], iota, ALU.is_equal)
                link(last)
                for t in range(NT):
                    last = tt(four(SG)[:, t], four(Ssel)[:, t], bc(gat)[:, t], ALU.mult)
                last.then_inc(S.sel, 1)

            def gathered(S, v):
                dve.wait_ge(S.tok, v)
                nc.vector.tensor_copy(XeT, ps[:, 2:4, :].rearrange("p b (k s) -> p (b k) s", s=P)).then_inc(S.tokT, 1)

            def expert_pair(S, i, cols):
                dve.wait_ge(S.silu, i + 1)
                dve.wait_ge(S.h3, i + 1)
                tt(hexp, gsil, ps[:, 1, :], ALU.mult).then_inc(S.hid, 1)
                dve.wait_ge(S.tr, i + 1)
                nc.vector.tensor_copy(SGT, ps[:, 2, 0:T])
                nc.vector.tensor_copy(heT.rearrange("p f s -> p (f s)"), ps[:, 3, :]).then_inc(S.trT, 1)
                select(S, cols)
                gathered(S, i + (1 + (S is first)))

            link(nc.vector.tensor_copy(cnt, ps[:, 1, 128:192]))
            select(first, slice(0, 2))
            link(ts(nx, cnt, float(SLOTS), None, ALU.is_gt))
            link(stt(nx, cnt, 2.0 * SLOTS, nx, ALU.is_gt, ALU.add))
            link(stt(nx, cnt, 3.0 * SLOTS, nx, ALU.is_gt, ALU.add))
            gathered(first, 1)
            link(nc.vector.tensor_tensor_scan(ce, C("ones")[:, 0:E], nx, 0.0, ALU.mult, ALU.add))
            link(tt(cex, ce, nx, ALU.subtract))
            for b in range(NOV):
                last = ts(selo[:, b, :], ce, float(b), None, ALU.is_gt)
            link(last)
            for b in range(NOV):
                last = stt(selo[:, b, :], cex, float(b), selo[:, b, :], ALU.is_le, ALU.mult)
            link(last)
            pe3 = prod[:, 0:NOV * E].rearrange("p (b e) -> p b e", b=NOV)
            rb = lambda ap: ap.unsqueeze(1).to_broadcast([P, NOV, E])
            link(tt(pe3, selo, rb(cex), ALU.mult))
            off = r8[6].rearrange("p t e -> p (t e)")[:, 0:NOV]
            link(nc.vector.tensor_reduce(off, pe3, AX.X, ALU.add))
            link(tt(off, off, C("iota")[:, 0:NOV], ALU.subtract))
            link(ts(off, off, float(SLOTS), None, ALU.mult))
            for t in range(NT):
                link(tt(pe3, selo, rb(rnk[:, t, 0:E]), ALU.mult))
                link(nc.vector.tensor_reduce(rnk[:, t, E:E + NOV], pe3, AX.X, ALU.add))
                link(tt(rnk[:, t, E:E + NOV], rnk[:, t, E:E + NOV], off, ALU.add))
                link(tt(pe3, selo, rb(gat[:, t, 0:E]), ALU.mult))
                link(nc.vector.tensor_reduce(gat[:, t, E:E + NOV], pe3, AX.X, ALU.add))
            link(nc.vector.memset(ovf, 0.0))
            link(tt(pe3, selo, rb(C("eidx")), ALU.mult))
            link(nc.vector.tensor_reduce(ovf[:, 0:NOV], pe3, AX.X, ALU.add))
            link(nc.vector.tensor_copy(ovf[:, OVR:OVR + 1], ce[:, E - 1:E]))
            nc.vector.tensor_copy(ovi, ovf).then_inc(ov_ready, 1)

            with dve.Fori(0, E // 2) as i:
                link.enter(i, 1)
                expert_pair(first, i, bass.ds(i * 2 + 2, 2))
            link.leave(E // 2)
            dve.wait_ge(ov_ready, 1)
            nov = dve.value_load(ovi[0:1, OVR:OVR + 1], min_val=0, max_val=NOV)
            with dve.If(nov > 0):
                dve.sem_inc(later.tokT, 1)
                with dve.Fori(0, OVR // 2) as i:
                    link.enter(i, 1)
                    expert_pair(later, i, bass.ds(i * 2 + (E + 2), 2))
                dve.wait_ge(later.out, OVR // 2)
            dve.end_ifs()
            link = Chain(dve, chainD2)
            modulation(modcol[:, 1, :], V("nmix0"))
            dve.wait_ge(g_ev, 2)
            dve.wait_ge(first.out, E // 2)
            for t in range(NT):
                link(tt(xn[:, t, :], y[:, t, :], gB[:, :], ALU.mult))
                tt(x[:, t, :], x[:, t, :], xn[:, t, :], ALU.add).then_inc(x_new, 1)

            def residual(b0, n, done_at):
                dve.wait_ge(g_ev, n)
                done_at()
                yy = ps[:, b0:b0 + 4, :].rearrange("p (t c) n -> p t (c n)", t=NT)
                for t in range(NT):
                    link(tt(xn[:, t, :], yy[:, t, :], gB[:, :], ALU.mult))
                    tt(x[:, t, :], x[:, t, :], xn[:, t, :], ALU.add).then_inc(x_new, 1)

            norm(2)
            norm_out(2, 4)

            def rope(v, heads, sig):
                x1 = v.rearrange("p t (h f) -> p t h f", h=heads)[:, :, :, 0::2]
                x2 = v.rearrange("p t (h f) -> p t h f", h=heads)[:, :, :, 1::2]
                w = NT * heads * 32
                m = [xnf[:, n * 512:n * 512 + w].rearrange("p (t h f) -> p t h f", t=NT, h=heads) for n in range(4)]
                cs = [CB(n).rearrange("p (t f) -> p t f", t=NT).unsqueeze(2).to_broadcast([P, NT, heads, 32])
                      for n in ("rcos", "rsin")]
                for n, (a, b) in enumerate(((x1, 0), (x2, 1), (x1, 1), (x2, 0))):
                    for t in range(NT):
                        last = tt(m[n][:, t], a[:, t], cs[b][:, t], ALU.mult)
                link(last)
                for t in range(NT):
                    tt(x1[:, t], m[0][:, t], m[1][:, t], ALU.subtract)
                    last = tt(x2[:, t], m[2][:, t], m[3][:, t], ALU.add)
                last.then_inc(sig, 1)

            dve.wait_ge(m_ev, 3)
            dve.wait_ge(block2_in, 32)
            rope(kv2[:, :, 0:P], NKV, rope_k)
            dve.wait_ge(rope_k, 1)
            rope(q2, NH, rope_q)
            dve.wait_ge(kt2_tr, 1)
            nc.vector.tensor_copy(f1f[:, 0:512], ps[:, 2, :]).then_inc(kt2_ev, 1)
            dve.wait_ge(rope_q, 1)
            at5 = attn2.rearrange("p t (h i) d -> p t h i d", h=2)
            sk = sinkB.rearrange("p (h i) -> p h i", h=2)
            ih = lambda ap: ap.rearrange("p (i h) -> p i h", i=2)

            def logits2(i, u):
                dve.wait_ge(b_qtr, i * 2 + (u + 1))
                nc.vector.tensor_copy(qT2, ps[:, 7, 0:T]).then_inc(b_qT, 1)
                dve.wait_ge(b_s, i * 2 + (u + 1))
                for t in range(NT):
                    last = tt(L2[:, 2 * t:2 * t + 2, 0:256], ps[:, 2 * t:2 * t + 2, 0:256],
                              CB("wmask").rearrange("p (t n) -> p t n", t=NT)[:, t:t + 1, :].to_broadcast([P, 2, 256]),
                              ALU.add)
                link(last)
                nc.vector.tensor_reduce(mc2, ps[:, 0:4, 256:512], AX.X, ALU.max)
                link(nc.vector.tensor_reduce(nM2, L2[:, :, 0:256], AX.X, ALU.max))
                link(tt(nM2, nM2, mc2, ALU.max))
                skb = sk[:, :, bass.ds(i * 2 + u, 1)].rearrange("p h i -> p (h i)").unsqueeze(1).to_broadcast([P, 2, 2])
                link(tt(ih(nM2), ih(nM2), skb, ALU.max))
                link(ts(nM2, nM2, -1.0, None, ALU.mult))
                tt(ih(se), ih(nM2), skb, ALU.add).then_inc(b_M, 1)

            def probabilities2(i, u):
                dve.wait_ge(b_E, i * 2 + (u + 1))
                link(tt(s1, s1, s2, ALU.add))
                link(tt(s1, s1, se, ALU.add))
                link(nc.vector.reciprocal(rs1, s1))
                dve.wait_ge(b_T, i * 2 + (u + 1))
                nc.vector.tensor_copy(PT2[:, 2:4, :], ps[:, 2:4, :]).then_inc(b_P, 1)

            def combined2(i, u):
                dve.wait_ge(b_O, i * 2 + (u + 1))
                one = bass.ds(i * 2 + u, 1)
                for t in range(NT):
                    last = tt(at5[:, t, :, one, :].rearrange("p h i d -> p h (i d)"),
                              ps[:, 4, t * 128:(t + 1) * 128].rearrange("p (h d) -> p h d", h=2),
                              rs1[:, 2 * t:2 * t + 2].unsqueeze(2).to_broadcast([P, 2, HD]), ALU.mult)
                last.then_inc(b_done, 1)

            with dve.Fori(0, PAIRS // 2) as i:
                link.enter(i, 16)
                logits2(i, 0)
                probabilities2(i, 0)
                logits2(i, 1)
                combined2(i, 0)
                probabilities2(i, 1)
                ada_sums(2, RL1, i, 5)
                combined2(i, 1)
            link.leave(PAIRS // 2)
            columns(2, 0, 8, 2, 4)
            dve.wait_ge(at2_tr, 1)
            nc.vector.tensor_copy(mixT[:, 4:8, :].rearrange("p k t -> p (k t)"),
                                  ps[:, 0:2, :].rearrange("p b n -> p (b n)")).then_inc(at2_mix, 1)
            modulation(modcol[:, 1, 16:32], V("nffn0"))

            def high(out, v):
                return nc.vector.tensor_copy(out.bitcast(F32R), v)

            def low(out, v, hi):
                return tt(out.bitcast(F32R), v, hi, ALU.subtract)

            def split13(g, i, quarters):
                s, at = g % 2, 16 * (g // 2 + 1)
                q = lambda v, n: v[:, n * 1024:(n + 1) * 1024]
                if 0 in quarters:
                    dve.wait_ge(w13_in[s], at if i is None else i * 16 + at)
                    for n in range(4):
                        last = high(q(w13H[s], n), q(w13[s], n))
                    link(last)
                for n in quarters:
                    last = low(q(w13L[s], n), q(w13[s], n), q(w13H[s], n))
                if 3 in quarters:
                    last.then_inc(w13_split, 1)

            def split2_high(g, i):
                s, at = g % 2, 16 * (g // 2 + 1)
                dve.wait_ge(w2_in[s], at if i is None else i * 16 + at)
                link(high(w2H[s], w2[s]))

            def split2_low(g):
                low(w2L[g % 2], w2[g % 2], w2H[g % 2]).then_inc(w2_split, 1)

            done(dve, RMO - 2)
            split13(0, None, range(4))
            split2_high(0, None)
            split2_low(0)
            residual(4, 3, lambda: done(dve, RMO + 1))

            def hidden(g, f, i):
                n = 2 * g + f + 1
                b = (n - 1) % 4
                dve.wait_ge(f_s, n if i is None else i * 4 + n)
                link(tt(hid[:, b, :], gs[:, b, :], ps[:, b, 256:512], ALU.mult))
                link(high(gH[:, b, :], hid[:, b, :]))
                low(gL[:, b, :], hid[:, b, :], gH[:, b, :]).then_inc(f_g, 1)

            def ffn_step(l, c, i=None, more=True):
                g = NF * l + c
                if more:
                    split13(g + 1, i, (0, 1))
                hidden(g, 0, i)
                if more:
                    split13(g + 1, i, (2, 3))
                    split2_high(g + 1, i)
                hidden(g, 1, i)
                if more:
                    split2_low(g + 1)

            def ffn(l):
                dve.wait_ge(nrm_hT, 8 + 2 * l)
                high(hH[:, :], hTf).then_inc(h_split, 1)
                dve.wait_ge(h_split, 2 * l + 1)
                low(hL[:, :], hTf, hH[:, :]).then_inc(h_split, 1)
                ffn_step(l, 0)
                rounds = (NF - 1) // 2 - l
                with dve.Fori(0, rounds) as i:
                    link.enter(i, 12)
                    for c in (1, 2):
                        ffn_step(l, c, i)
                link.leave(rounds)
                for c in range(2 * rounds + 1, NF):
                    ffn_step(l, c, None, c < NF - 1)

            norm(3)
            norm_out(3, 4)
            ffn(0)
            modulation(modcol[:, 2, :], V("nmix1"))
            residual(4, 4, lambda: dve.wait_ge(f_out, NF))
            norm(4)
            dve.wait_ge(p_tr, 1)
            for k in range(KD // 2):
                last = ts(hT[:, k, :], ps[:, 4 + k // 2, (k % 2) * T:(k % 2 + 1) * T], Acol[:, k:k + 1], None, ALU.mult)
            last.then_inc(p_T, 1)
            dve.wait_ge(g_ev, 5)
            dve.wait_ge(row_in, 16)
            link(tt(gB[:, :], gB[:, :], rowB, ALU.mult))
            dve.wait_ge(p_T, 2)
            modulation(modcol[:, 2, 16:32], V("nffn1"))
            residual(0, 5, lambda: dve.wait_ge(p_y, 1))
            norm(5)
            norm_out(4, 4)
            ffn(1)
            residual(4, 6, lambda: dve.wait_ge(f_out, 2 * NF))
            norm(6)
            dve.wait_ge(nrm_xn, 14)
            dve.wait_ge(row_in, 32)
            for t in range(NT):
                tt(xn[:, t, :], xn[:, t, :], rowB, ALU.mult).then_inc(x_new, 1)

        @block.tensor
        def _(pe):
            mm, tr = nc.tensor.matmul, nc.tensor.transpose

            def arrived(n, i=None):
                v = 16 * (n // NS + 1)
                pe.wait_ge(loaded[n % NS], v if i is None else i * 16 + v)

            def ada_chunk(n, bank, s, cset, i=None):
                arrived(n, i)
                w = ring_view(n, KD)
                for k in range(KD):
                    for j in range(4):
                        last = mm(ps[32 * j:32 * j + 32, bank + s // 4, (s % 4) * P:(s % 4 + 1) * P], cond[:, cset, k, :],
                                  w[:, k, j * P:(j + 1) * P], start=(k == 0), stop=(k == KD - 1))
                last.then_inc(ring_used, 1)

            def columns(l, a, b, bank):
                for n, c in enumerate(ADA_COLS[a:b]):
                    last = tr(ps[:, bank + n // 4, (n % 4) * P:(n % 4 + 1) * P],
                              modrow[:, l * 1536 + c * P:l * 1536 + (c + 1) * P], ident)
                last.then_inc(col_tr, 1)

            def gate_row(l, c0, b0):
                for c in range(2):
                    for j in range(4):
                        last = mm(ps[:, b0 + c, j * P:(j + 1) * P], sel[:, j, :],
                                  modrow[:, l * 1536 + (c0 + c) * P:l * 1536 + (c0 + c + 1) * P], start=True, stop=True)
                last.then_inc(g_mm, 1)

            def norm_tr(u, b0):
                for t in range(NT):
                    pe.wait_ge(nrm_xn, NT * u + t + 1)
                    for k in range(KD):
                        last = tr(ps[:, b0 + k // 2, (k % 2) * T + t * P:(k % 2) * T + (t + 1) * P],
                                  xn[:, t, k * P:(k + 1) * P], ident)
                last.then_inc(nrm_tr, 1)

            pe.sem_inc(ring_used, NS)
            pe.wait_ge(tab_in, 32)
            for h in range(NH):
                mm(ps[:, h, 0:384], relb[:, h:h + 1].to_broadcast([NB, P]), oh[:, :], start=True, stop=True
                   ).then_inc(tabr_mm, 1)
            pe.wait_ge(con_in, 32)
            pe.wait_ge(tabr_ev, NH)
            norm_tr(0, 4)
            pe.wait_ge(cond_ready, 1)
            for c in range(4):
                ada_chunk(RA[c], 0, c, 0)
            pe.wait_ge(ada_ev, 1)
            columns(0, 0, 4, 2)

            def tokens(n, w, banks, at=0):
                arrived(n)
                v = chunk_slot(n)[:, 0:KD * w[1]].rearrange("p (k n) -> p k n", k=KD)
                for t in range(NT):
                    for k in range(KD):
                        last = mm(banks[t], hT[:, k, t * P:(t + 1) * P], v[:, k, w[0]:w[0] + banks[t].shape[1]],
                                  start=(k == 0), stop=(k == KD - 1))
                return last

            def features(n, w, tiles, b0):
                arrived(n)
                v = chunk_slot(n)[:, 0:KD * w].rearrange("p (k n) -> p k n", k=KD)
                for f in range(tiles):
                    for k in range(KD):
                        last = mm(ps[:, b0 + f // 2, (f % 2) * T:(f % 2 + 1) * T], v[:, k, f * P:(f + 1) * P], hT[:, k, :],
                                  start=(k == 0), stop=(k == KD - 1))
                return last

            pe.wait_ge(nrm_hT, 2)
            tokens(RW[0], (0, 512), [ps[:, t, :] for t in range(NT)]).then_inc(ring_used, 1)
            features(RW[1], 512, 2, 2)
            tokens(RW[1], (256, 512), [ps[:, 3, t * 256:(t + 1) * 256] for t in range(NT)]).then_inc(ring_used, 1)
            tokens(RW[2], (0, 280), [ps[:, 4 + t, 0:280] for t in range(NT)]).then_inc(ring_used, 1)
            features(RW[3], 512, 4, 6).then_inc(ring_used, 1)
            pe.wait_ge(win_act, 3)
            for c in range(4):
                ada_chunk(RA[4 + c], 4, c, 0)
            features(RW[4], 512, 4, 0).then_inc(ring_used, 1)
            pe.wait_ge(win_dve, 1)
            features(RW[5], 512, 4, 2).then_inc(ring_used, 1)
            ada_chunk(RA[8], 5, 0, 0)
            pe.wait_ge(k_n, 1)
            pe.wait_ge(win_act, 4)
            for n, kk in enumerate((ksv, kwg)):
                for t in range(NT):
                    last = tr(ps[:, 7, n * T + t * P:n * T + (t + 1) * P], kk[:, t, 0:P], ident)
            last.then_inc(k_tr, 1)
            ada_chunk(RA[9], 5, 1, 0)
            pe.wait_ge(cv_sq, 1)
            for f in range(4):
                last = mm(ps[:, f // 2, (f % 2) * T:(f % 2 + 1) * T], C("bd"), sq[:, f * T:(f + 1) * T], start=True,
                          stop=True)
            last.then_inc(cv_sum, 1)
            pe.wait_ge(blk_ready, 1)
            pe.wait_ge(ada_ev, 2)
            for v in range(2):
                arrived(RC + v)
                w = ring_view(RC + v, LPAIRS)
                for m in range(LPAIRS):
                    last = mm(ps[0:30, 4, v * CMP_HID:(v + 1) * CMP_HID], blk[:, v, m, :, :].rearrange("p g n -> p (g n)"),
                              w[:, m, :], start=(m == 0), stop=(m == LPAIRS - 1))
                last.then_inc(ring_used, 1)
            ada_chunk(RA[10], 5, 2, 0)
            pe.wait_ge(hid_act, 1)
            for v in range(4):
                last = tr(ps[:, 6, 384 + v * 32:384 + v * 32 + 30], hidS[0:30, v * P:(v + 1) * P], ident[0:30, 0:30])
            last.then_inc(hidT_tr, 1)
            pe.wait_ge(hidT_ev, 1)
            pe.wait_ge(misc_in, 64)
            for v in range(2):
                for p0 in ((0,) if v == 0 else (0, 32)):
                    for g in range(2):
                        for j in range(2):
                            last = mm(ps[p0:p0 + NC, 6, v * P + g * HD:v * P + (g + 1) * HD],
                                      hidT[:, 2 * v + j, g * NC:(g + 1) * NC], cw2[:, v, j, :], start=(j == 0),
                                      stop=(j == 1))
            last.then_inc(kc_mm, 1)
            ada_chunk(RA[11], 5, 3, 0)
            pe.wait_ge(kc_n, 1)
            tr(ps[:, 6, 256:256 + NC], kcn[0:NC, :], ident[0:NC, 0:NC]).then_inc(kc_tr, 1)
            pe.wait_ge(kc_ready, 1)
            pe.wait_ge(k_ready, 1)

            def queries(i, u):
                pe.wait_ge(a_qn, i * 2 + (u + 1))
                for t in range(NT):
                    last = tr(ps[:, 1, 256 + t * P:256 + (t + 1) * P], qn[:, t, :, :].rearrange("p h d -> p (h d)"), ident)
                last.then_inc(a_qtr, 1)

            def scores(i, u):
                pe.wait_ge(a_qT, i * 2 + (u + 1))
                for b, (kT, b0) in enumerate(((kTs, 2), (kTw, 4))):
                    for h in range(2):
                        r = slice(64 * h, 64 * h + 64)
                        mm(ps[:, b0 + h, 0:256], qT[r, P:T], kT[r, :], start=True, stop=True)
                        last = mm(ps[:, b0 + h, 256:384], qT[r, 0:P], kT[r, 0:P], start=True, stop=True)
                        if b == 0:
                            mm(ps[:, b0 + h, C1:C1 + NC], qT[r, P:T], kcT[r, 0:NC], start=True, stop=True)
                            last = mm(ps[:, b0 + h, C0:C0 + NC], qT[r, 0:P], kcT[r, 0:NC], start=True, stop=True)
                    last.then_inc((a_s, a_w)[b], 1)

            def transposes(i, u):
                pe.wait_ge(a_E, i * 2 + (u + 1))
                for b, b0 in enumerate((2, 4)):
                    for h in range(2):
                        for c in range(3):
                            last = tr(ps[:, b0 + h, c * P:(c + 1) * P], L[:, 2 * b + h, c * P:(c + 1) * P], ident)
                        if b == 0:
                            last = tr(ps[0:47, b0 + h, 384:512], L[:, h, C1:C1 + 47], ident)
                    last.then_inc(a_T, 1)

            def values(i, u):
                if u:
                    pe.wait_ge(a_done, i * 2 + 1)
                for h in range(2):
                    o = lambda b, ii: ps[:, 6 + h, (2 * b + ii) * HD:(2 * b + ii + 1) * HD]
                    for ii in range(2):
                        mm(o(0, ii), PTs[0:47, h, 384:512], vc[0:47, ii, h, :], start=True, stop=True)
                    for b, (PT, kv) in enumerate(((PTs, ksv), (PTw, kwg))):
                        vv = [kv[:, t, P + h * HD:P + (h + 1) * HD] for t in range(NT)]
                        mm(o(1 + b, 0), PT[:, h, 0:P], vv[0], start=True, stop=False)
                        mm(o(1 + b, 0), PT[:, h, P:2 * P], vv[1], start=False, stop=True)
                        last = mm(o(1 + b, 1), PT[:, h, 2 * P:3 * P], vv[0], start=True, stop=True)
                last.then_inc(a_O, 1)

            pe.wait_ge(cv_sd, 1)
            with pe.Fori(0, PAIRS // 2) as i:
                ada = lambda s: ada_chunk(RL0 + s, 0, s, 1, i)
                pe.wait_ge(ada_ev, i + 3)
                queries(i, 0)
                ada(0)
                scores(i, 0)
                ada(1)
                ada(2)
                transposes(i, 0)
                queries(i, 1)
                ada(3)
                pe.wait_ge(a_P, i * 4 + 2)
                scores(i, 1)
                values(i, 0)
                ada(4)
                transposes(i, 1)
                ada(5)
                pe.wait_ge(a_P, i * 4 + 4)
                values(i, 1)

            pe.wait_ge(ada_ev, 5)
            columns(0, 4, 8, 0)
            columns(1, 0, 8, 2)

            def project_out(n0, src, b0, ks, first, tiles=(0, 1), parts=(0, 1)):
                for c in parts:
                    arrived(n0 + c)
                    w = ring_view(n0 + c, KD)
                    for t in tiles:
                        for n, k in enumerate(ks):
                            last = mm(ps[:, b0 + 2 * t + c, :], src[:, k, t * P:(t + 1) * P], w[:, k, :],
                                      start=(first and n == 0), stop=(not first and n == len(ks) - 1))
                    if not first:
                        last.then_inc(ring_used, 1)

            pe.wait_ge(cv_mix, 1)
            project_out(RO, mixT, 4, range(4, KD), True, (0,))
            pe.wait_ge(a_done, PAIRS)
            project_out(RO, mixT, 4, range(4, KD), True, (1,))
            pe.wait_ge(col_ev, 3)
            gate_row(0, 4, 0)
            pe.wait_ge(at_n, 1)
            a2 = attn.rearrange("p j h d -> p j (h d)")
            for j in range(4):
                for t in range(NT):
                    last = tr(ps[:, 2 + j // 2, (j % 2) * T + t * P:(j % 2) * T + (t + 1) * P],
                              a2[:, 1 - t, j * P:(j + 1) * P], ident)
            last.then_inc(at_tr, 1)
            pe.wait_ge(at_mix, 1)
            project_out(RO, mixT, 4, range(4), False, parts=(0,))
            pe.wait_ge(g_ev, 1)
            pe.wait_ge(cx_n, 1)
            for k in range(KD):
                for t in range(NT):
                    last = tr(ps[:, k // 2, (k % 2) * T + t * P:(k % 2) * T + (t + 1) * P],
                              ctx_in[:, t, k * P:(k + 1) * P], ident)
            last.then_inc(cx_tr, 1)
            project_out(RO, mixT, 4, range(4), False, parts=(1,))
            arrived(RK)
            w = ring[:, RK % NS, 0:2048].rearrange("p (k n) -> p k n", k=KD)
            pe.wait_ge(cx_T, 1)
            for t in range(NT):
                for k in range(KD):
                    last = mm(ps[:, 1, t * 256:(t + 1) * 256], ctxT[:, k, t * P:(t + 1) * P], w[:, k, :], start=(k == 0),
                              stop=(k == KD - 1))
            last.then_inc(ring_used, 1)
            pe.wait_ge(x_new, NT)
            gate_row(0, 10, 2)
            norm_tr(1, 4)
            pe.wait_ge(nrm_hT, 4)
            for t in range(NT):
                for k in range(KD):
                    last = mm(ps[:, 0, t * 72:(t + 1) * 72], hT[:, k, t * P:(t + 1) * P], wr[:, k, :], start=(k == 0),
                              stop=(k == KD - 1))
            last.then_inc(lg_mm, 1)
            for t in range(NT):
                for k in range(KD):
                    last = tr(ps[:, 4 + 2 * t + k // 4, (k % 4) * P:(k % 4 + 1) * P], hT[:, k, t * P:(t + 1) * P], ident)
            last.then_inc(h2_tr, 1)
            pe.wait_ge(acc_zero, 1)
            pe.wait_ge(h2_ev, 1)
            for b in range(4, 8):
                mm(ps[:, b, :], ident, Ye[:, 0:512], start=True, stop=True)
            pe.wait_ge(lg_mask, 1)
            pe.wait_ge(cx_kv, 1)
            mm(ps[:, 1, 0:E], tri, msk[:, 0, :], start=True, stop=True)
            mm(ps[:, 1, E:2 * E], ones, msk[:, 0, :], start=True, stop=False)
            mm(ps[:, 1, E:2 * E], tri, msk[:, 1, :], start=False, stop=True)
            mm(ps[:, 1, 2 * E:3 * E], ones, msk[:, 0, :], start=True, stop=False)
            mm(ps[:, 1, 2 * E:3 * E], ones, msk[:, 1, :], start=False, stop=True).then_inc(lg_rank, 1)

            def gather(S, v):
                pe.wait_ge(S.sel, v)
                for k in range(KD):
                    for t in range(NT):
                        last = mm(ps[:, 2 + k // 4, (k % 4) * P:(k % 4 + 1) * P], xn[:, t, k * P:(k + 1) * P],
                                  Ssel[:, t, :], start=(t == 0), stop=(t == NT - 1))
                last.then_inc(S.tok, 1)

            def expert_pair(S, i):
                half = (slice(0, SLOTS), slice(SLOTS, P))

                def weights(j, k):
                    for n in (RE + 2 * j, RE + 2 * j + 1):
                        pe.wait_ge(S.loaded[n % NS], i * 16 + (16 * (n // NS + 1) if S is first else 16))
                    return [chunk_slot(RE + 2 * j + u).rearrange("p (k n) -> p k n", k=k) for u in range(2)]

                pe.wait_ge(S.tokT, i + 1)
                for j in range(2):
                    w = weights(j, KD)
                    for k in range(KD):
                        for u in range(2):
                            last = mm(ps[half[u], j, :], XeT[:, k, half[u]], w[u][:, k, :], start=(k == 0),
                                      stop=(k == KD - 1))
                    last.then_inc((S.h1, S.h3)[j], 1)
                    if j == 0:
                        for t in range(NT):
                            tr(ps[:, 2, t * P:(t + 1) * P], SG[:, t, :], ident)
                pe.wait_ge(S.hid, i + 1)
                pe.sem_inc(S.used, 4)
                for f in range(FE // P):
                    last = tr(ps[:, 3, f * P:(f + 1) * P], hexp[:, f * P:(f + 1) * P], ident)
                last.then_inc(S.tr, 1)
                w = weights(2, FE // P)
                pe.wait_ge(S.trT, i + 1)
                for k in range(FE // P):
                    for m in range(2):
                        for u in range(2):
                            last = mm(ps[half[u], m, :], heT[:, k, half[u]], w[u][:, k, m * 512:(m + 1) * 512],
                                      start=(k == 0), stop=(k == FE // P - 1))
                last.then_inc(S.y, 1)
                gather(S, i + (1 + (S is first)))
                pe.wait_ge(S.yc, i + 1)
                pe.sem_inc(S.used, 2)
                for t in range(NT):
                    for m in range(2):
                        last = mm(ps[:, 4 + 2 * t + m, :], SGT[:, t * P:(t + 1) * P], Ye[:, m * 512:(m + 1) * 512],
                                  start=False, stop=True, skip_group_check=True)
                last.then_inc(S.out, 1)

            pe.wait_ge(g_ev, 2)
            gather(first, 1)
            with pe.Fori(0, E // 2) as i:
                expert_pair(first, i)
            pe.wait_ge(ov_ready, 1)
            nov = pe.value_load(ovi[0:1, OVR:OVR + 1], min_val=0, max_val=NOV)
            with pe.If(nov > 0):
                pe.sem_inc(ov_used, NS)
                pe.wait_ge(first.tokT, E // 2 + 1)
                with pe.Fori(0, OVR // 2) as i:
                    expert_pair(later, i)
            pe.end_ifs()
            norm_tr(2, 4)
            pe.wait_ge(nrm_hT, 6)
            tokens(RM, (0, 512), [ps[:, 4 + t, :] for t in range(NT)]).then_inc(ring_used, 1)
            tokens(RM + 1, (0, 512), [ps[:, 6 + t, :] for t in range(NT)]).then_inc(ring_used, 1)
            tokens(RM + 2, (0, 256), [ps[:, 0, t * 256:(t + 1) * 256] for t in range(NT)]).then_inc(ring_used, 1)
            pe.wait_ge(block2_in, 32)
            pe.wait_ge(m_ev, 2)
            for h in range(4):
                for c, n in enumerate(("cosn", "sinn")):
                    F = CB(n).rearrange("p (t n) -> p t n", t=NT)
                    for t in range(NT):
                        last = mm(ps[:, 4 + h, c * T:(c + 1) * T], u2[:, t, h * P:(h + 1) * P], F[:, t, :],
                                  start=(t == 0), stop=(t == NT - 1))
            last.then_inc(f_T1, 1)
            pe.wait_ge(f_T1ev, 1)
            pe.wait_ge(m_ev, 3)
            for h in range(4):
                for c, n in enumerate(("cosd", "nsind")):
                    last = mm(ps[:, h // 2, (h % 2) * T:(h % 2 + 1) * T], CB(n), T1[:, h, c, :], start=(c == 0),
                              stop=(c == 1))
            last.then_inc(f_y, 1)
            pe.wait_ge(rope_k, 1)
            for n, kk in enumerate((kv2, kvc)):
                for t in range(NT):
                    last = tr(ps[:, 2, n * T + t * P:n * T + (t + 1) * P], kk[:, t, 0:P], ident)
            last.then_inc(kt2_tr, 1)
            pe.wait_ge(kt2_ev, 1)
            pe.wait_ge(f_yev, 1)
            def queries2(i, u):
                pe.wait_ge(b_qn, i * 2 + (u + 1))
                for t in range(NT):
                    last = tr(ps[:, 7, t * P:(t + 1) * P], qn2[:, t, :, :].rearrange("p h d -> p (h d)"), ident)
                last.then_inc(b_qtr, 1)

            def scores2(i, u):
                pe.wait_ge(b_qT, i * 2 + (u + 1))
                for t in range(NT):
                    for h in range(2):
                        r = slice(64 * h, 64 * h + 64)
                        mm(ps[:, 2 * t + h, 0:256], qT2[r, t * P:(t + 1) * P], kT2[r, :], start=True, stop=True)
                        last = mm(ps[:, 2 * t + h, 256:512], qT2[r, t * P:(t + 1) * P], kcT2[r, :], start=True, stop=True)
                last.then_inc(b_s, 1)

            def transposes2(i, u):
                pe.wait_ge(b_E, i * 2 + (u + 1))
                for a in range(4):
                    for k in range(4):
                        last = tr(ps[:, a, k * P:(k + 1) * P], L2[:, a, k * P:(k + 1) * P], ident)
                last.then_inc(b_T, 1)

            def values2(i, u):
                if u:
                    pe.wait_ge(b_done, i * 2 + 1)
                for a in range(4):
                    for k in range(4):
                        vv = (kv2, kvc)[k // 2][:, k % 2, P + (a % 2) * HD:P + (a % 2 + 1) * HD]
                        last = mm(ps[:, 4, a * HD:(a + 1) * HD], PT2[:, a, k * P:(k + 1) * P], vv, start=(k == 0),
                                  stop=(k == 3))
                last.then_inc(b_O, 1)

            with pe.Fori(0, PAIRS // 2) as i:
                ada = lambda s: ada_chunk(RL1 + s, 5, s, 1, i)
                queries2(i, 0)
                pe.wait_ge(ada_ev, i + 5)
                ada(0)
                scores2(i, 0)
                ada(1)
                ada(2)
                transposes2(i, 0)
                queries2(i, 1)
                ada(3)
                pe.wait_ge(b_P, i * 4 + 2)
                scores2(i, 1)
                values2(i, 0)
                ada(4)
                transposes2(i, 1)
                ada(5)
                pe.wait_ge(b_P, i * 4 + 4)
                values2(i, 1)
            pe.wait_ge(ada_ev, 7)
            columns(2, 0, 8, 2)
            project_out(RMO, mixT, 4, range(4), True, (1,))
            pe.wait_ge(b_done, PAIRS)
            project_out(RMO, mixT, 4, range(4), True, (0,))
            af = attn2.rearrange("p t h d -> p t (h d)")
            for j in range(4):
                for t in range(NT):
                    last = tr(ps[:, j // 2, (j % 2) * T + t * P:(j % 2) * T + (t + 1) * P],
                              af[:, t, j * P:(j + 1) * P], ident)
            last.then_inc(at2_tr, 1)
            pe.wait_ge(col_ev, 4)
            gate_row(1, 4, 2)
            pe.wait_ge(at2_mix, 1)
            project_out(RMO, mixT, 4, range(4, KD), False)

            def ffn_step(l, c, i=None):
                g = NF * l + c
                s = g % 2
                at = lambda per, v: v if i is None else i * per + v
                r = lambda v: v.bitcast(F32R)
                wH, wL = (r(v[s]).rearrange("p (k n) -> p k n", k=KD) for v in (w13H, w13L))
                hh, hl = (r(v[:, :]).rearrange("p (k t) -> p k t", k=KD) for v in (hH, hL))
                pe.wait_ge(w13_split, at(2, g + 1))
                for f in range(2):
                    b = 2 * s + f
                    for j in range(2):
                        col = slice(j * FCH + f * P, j * FCH + (f + 1) * P)
                        o = ps[:, b, j * T:(j + 1) * T]
                        for k in range(KD):
                            mm(o, wH[:, k, col], hh[:, k, :], start=(k == 0), stop=False)
                            mm(o, wL[:, k, col], hh[:, k, :], start=False, stop=False)
                        if i is None and c == 0 and f == 0 and j == 0:
                            pe.wait_ge(h_split, 2 * l + 2)
                        for k in range(KD):
                            last = mm(o, wH[:, k, col], hl[:, k, :], start=False, stop=(k == KD - 1))
                    last.then_inc(f_h, 1)
                vH, vL = (r(v[s]).rearrange("p (k n) -> p k n", k=2) for v in (w2H, w2L))
                pe.wait_ge(w2_split, at(2, g + 1))
                for f in range(2):
                    b = 2 * s + f
                    pe.wait_ge(f_g, at(4, 2 * g + f + 1))
                    for t in range(NT):
                        for m in range(2):
                            o = ps[:, 4 + 2 * t + m, :]
                            tk, col = slice(t * P, (t + 1) * P), slice(m * 512, (m + 1) * 512)
                            mm(o, r(gH[:, b, tk]), vH[:, f, col], start=(i is None and c == 0 and f == 0), stop=False,
                               skip_group_check=True)
                            mm(o, r(gH[:, b, tk]), vL[:, f, col], start=False, stop=False, skip_group_check=True)
                            last = mm(o, r(gL[:, b, tk]), vH[:, f, col], start=False, stop=(c == NF - 1),
                                      skip_group_check=True)
                last.then_inc(f_out, 1)

            def ffn(l):
                pe.wait_ge(h_split, 2 * l + 1)
                ffn_step(l, 0)
                with pe.Fori(0, (NF - 1) // 2) as i:
                    for c in (1, 2):
                        ffn_step(l, c, i)

            pe.wait_ge(g_ev, 3)
            gate_row(1, 10, 2)
            norm_tr(3, 4)
            pe.wait_ge(g_ev, 4)
            ffn(0)
            gate_row(2, 4, 2)
            pe.wait_ge(nrm_xn, 10)
            pw = CB("pool").rearrange("p (t g n) -> p t g n", t=NT, g=4)
            for k in range(KD):
                for t in range(NT):
                    last = mm(ps[:, 4 + k // 2, (k % 2) * T:(k % 2 + 1) * T], xn[:, t, k * P:(k + 1) * P],
                              pw[:, t, k // 2, :], start=(t == 0), stop=(t == NT - 1))
            last.then_inc(p_tr, 1)
            pe.wait_ge(pool_in, 16)
            pe.wait_ge(p_T, 2)
            pe.wait_ge(g_ev, 5)
            for g in range(4):
                for t in range(NT):
                    for k in range(2):
                        last = mm(ps[:, 2 * t + g // 2, (g % 2) * 256:(g % 2 + 1) * 256],
                                  hT[:, 2 * g + k, t * P:(t + 1) * P], poolw[:, 2 * g + k, :], start=(k == 0),
                                  stop=(k == 1))
            last.then_inc(p_y, 1)
            pe.wait_ge(x_new, 5 * NT)
            gate_row(2, 10, 2)
            norm_tr(5, 4)
            pe.wait_ge(g_ev, 6)
            ffn(1)


def t5_buckets(n):
    n = np.maximum(n, 0)
    f = np.float32
    large = 16 + (np.log(np.maximum(n, 1).astype(f) / f(16)) / f(math.log(128 / 16)) * f(16)).astype(np.int32)
    return np.where(n < 16, n, np.minimum(large, NB - 1))


def constants():
    f = np.float32
    p = np.arange(P)
    con = np.zeros((P, NCON), f)

    def put(into, where, n, v):
        a, b = where[n]
        into[:, a:b] = np.asarray(v, f).reshape(P, b - a)

    put(con, CON, "ident", np.eye(P))
    put(con, CON, "tri", np.triu(np.ones((P, P))))
    put(con, CON, "ones", np.ones((P, P)))
    put(con, CON, "bd", np.kron(np.eye(2), np.ones((64, 64))))
    put(con, CON, "sel", np.repeat((p[:, None] == 32 * np.arange(4))[:, :, None], P, 2))
    put(con, CON, "iota", np.tile(np.arange(1, SLOTS + 1), (P, 1)))
    put(con, CON, "rev", np.tile(np.arange(8, 0, -1), (P, 1)))
    put(con, CON, "eidx", np.tile(np.arange(E), (P, 1)))
    put(con, CON, "cmask", np.where(np.arange(256)[None] > 128 + p[:, None], NEG, 0.0))
    conb = np.zeros((P, NCONB), f)
    n = np.arange(T)
    ang = 2 * np.pi * np.outer(n, n) / T
    norm = 1 / math.sqrt(T * 128)
    tiled = lambda m: m.reshape(NT, P, -1).transpose(1, 0, 2)
    put(conb, CONB, "cosn", tiled(np.cos(ang) * norm))
    put(conb, CONB, "sinn", tiled(np.sin(ang) * norm))
    ang = 2 * np.pi * np.outer(p, p) / P
    put(conb, CONB, "cosd", np.cos(ang))
    put(conb, CONB, "nsind", -np.sin(ang))
    pool = np.zeros((T, 4, T))
    for g, w in enumerate((2, 4, 8, 16)):
        for t in range(T):
            lo, hi = max(t - w // 2, 0), min(t + w // 2, T)
            pool[lo:hi, g, t] = 1.0 / (hi - lo)
            pool[t, g, t] -= 1.0
    put(conb, CONB, "pool", tiled(pool.reshape(T, 4 * T)))
    row, col = (n // 64).astype(f), (n % 64).astype(f)
    inv = (f(10000.0) ** (-np.arange(16, dtype=f) / f(16))).astype(f)
    ang = np.concatenate([row[:, None] * inv, col[:, None] * inv], 1).astype(f)
    put(conb, CONB, "rcos", tiled(np.cos(ang)))
    put(conb, CONB, "rsin", tiled(np.sin(ang)))
    put(conb, CONB, "wmask", tiled(np.where(np.abs(n[:, None] - n[None]) > 128, NEG, 0.0)))
    oh = np.zeros((NB, 384), f)
    oh[t5_buckets(255 - np.arange(384)), np.arange(384)] = 1.0
    return con, conb, oh


def kernel(**inputs):
    import concourse.bacc as _bacc
    from concourse.bass_utils import run_bass_kernel_spmd as _run

    a = {k: np.asarray(v) for k, v in inputs.items()}
    col = lambda v: np.reshape(v, (-1, P)).T
    con, conb, oh = constants()
    kn = a["k_norm_w"][0]
    vec = np.concatenate([
        col(a["norm1_w"]), col(a["norm2_w"]), col(a["out_norm_w"]), col(a["norm_mix_g_2"]), col(a["norm_ffn_g_2"]),
        col(a["pool_scale_2"]), col(a["c"]), col(a["c_2"]), col(a["c_ctx_2"]),
        col(np.concatenate([a["q_norm_w"][0]] * 2)), col(np.concatenate([kn, kn], 1)), col(a["cmp_pos_k"]),
        col(a["cmp_pos_v"]), col(a["conv_w"])], 1)
    biases = np.stack([a["b_ada"][0], a["ada_b_2"][0], a["ada_b_2"][1]])
    arrays = {
        "con": con, "conb": conb, "oh": oh, "vec": vec, "x": a["x"][0], "ctx": a["ctx_2"][0],
        "adab": biases.reshape(3, 12, 4, P).transpose(0, 2, 1, 3).reshape(3, 4, 1536),
        "w_ada": a["w_ada"][0], "ada_w_2": a["ada_w_2"].transpose(1, 0, 2).reshape(D, -1),
        "w_in": a["w_in"][0], "cmp_k_w1": a["cmp_k_w1"][0], "cmp_v_w1": a["cmp_v_w1"][0],
        "cmp_k_w2": a["cmp_k_w2"][0], "cmp_v_w2": a["cmp_v_w2"][0], "w_out": a["w_out"][0],
        "rel_bias": a["rel_bias"], "wr": np.concatenate([a["w_group"][0], a["w_expert"][0]], 1),
        "br": np.concatenate([a["b_group"][0], a["b_expert"][0]]),
        "w1": a["w1"][0], "w3": a["w3"][0], "w2": a["w2"][0],
        "mix_in": a["mix_in_w_2"][0], "mix_out": a["mix_out_w_2"][0], "sink": a["attn_sink_2"][0],
        "pool_w": a["pool_w_2"][0].reshape(D, 256), "f13": np.stack([a["ffn_w1_2"].reshape(2, D, NF, FCH), a["ffn_w3_2"].reshape(2, D, NF, FCH)], 3
                        ).reshape(2, D, 2 * FFN), "f2": a["ffn_w2_2"],
        "final_g": a["final_g_2"], "pscale": a["pool_scale_2"][0],
    }
    arrays = {k: np.ascontiguousarray(v) for k, v in arrays.items()}
    nc = _bacc.Bacc("TRN2", target_bir_lowering=False, num_devices=1)
    A = {k: nc.dram_tensor(f"in_{k}", v.shape, F32, kind="ExternalInput").ap() for k, v in arrays.items()}
    out = nc.dram_tensor("out", (1, T, D), F32, kind="ExternalOutput").ap()
    build(nc, A, out)
    r = _run(nc, [{f"in_{k}": v for k, v in arrays.items()}], core_ids=[0])
    return r.results[0]["out"]
```
